# Optimizing a Trainium2 kernel written in Bass

```python
import jax
import jax.numpy as jnp
from jax import lax
import numpy as np

D_MODEL = 1024
BATCH = 1
SEQ = 512
DEPTH = 1

GRID_W = 64
CTX_LEN = 256
HEAD_DIM = 64
BRANCH_W = 256
N_BRANCH = 4
A_HQ = 4
A_HKV = 2
C_HQ = 4
C_HKV = 2
WINDOW = 128
Q_BLOCK = 128
F_GROUPS = 4
F_GROUP_W = 64
G_HEADS = 4
G_DK = 64
G_DV = 64
G_CHUNK = 32
N_EXPERTS = 16
N_GROUPS = 4
EXPERTS_PER_GROUP = N_EXPERTS // N_GROUPS
TOP_K = 2
D_EXPERT = 256
ROPE_THETA = 10000.0
EPS = 1e-6
MOD_CHUNKS = 6

IN_WIDTHS = (
    A_HQ * HEAD_DIM, A_HKV * HEAD_DIM, A_HKV * HEAD_DIM,
    F_GROUPS * F_GROUP_W,
    C_HQ * HEAD_DIM, C_HKV * HEAD_DIM, C_HKV * HEAD_DIM,
    G_HEADS * G_DK, G_HEADS * G_DK, G_HEADS * G_DK,
    G_HEADS * G_DV, G_HEADS * G_DV,
    N_BRANCH * D_MODEL,
)
IN_SPLITS = tuple(int(v) for v in np.cumsum(IN_WIDTHS)[:-1])
IN_COLS = int(sum(IN_WIDTHS))

kernel_name = 'hybrid_gated_branch_dit_trunk'

def rms_norm(x, g):
    xf = x.astype(jnp.float32)
    y = xf * lax.rsqrt(jnp.mean(xf * xf, axis=-1, keepdims=True) + EPS)
    return (y * g.astype(jnp.float32)).astype(x.dtype)

def modulate(h, shift, scale):
    return h * (1 + scale) + shift

def split_heads(t, n):
    return t.reshape(t.shape[0], t.shape[1], n, -1)

def axial_rope_tables(rows):
    t = jnp.arange(rows * GRID_W)
    row = (t // GRID_W).astype(jnp.float32)
    col = (t % GRID_W).astype(jnp.float32)
    n_freq = HEAD_DIM // 4
    inv_freq = ROPE_THETA ** (-jnp.arange(n_freq, dtype=jnp.float32) / n_freq)
    ang = jnp.concatenate([row[:, None] * inv_freq, col[:, None] * inv_freq], axis=-1)
    return jnp.cos(ang), jnp.sin(ang)

def apply_rope(x, cos, sin):
    x1, x2 = jnp.split(x.astype(jnp.float32), 2, axis=-1)
    c = cos[None, :, None, :]
    s = sin[None, :, None, :]
    return jnp.concatenate([x1 * c - x2 * s, x1 * s + x2 * c], axis=-1).astype(x.dtype)

def global_attention(q, k, v, k_ctx, v_ctx):
    b_, s_, hq, hd = q.shape
    hkv = k.shape[2]
    grp = hq // hkv
    kk = jnp.concatenate([k, k_ctx], axis=1)
    vv = jnp.concatenate([v, v_ctx], axis=1)
    nb = s_ // Q_BLOCK
    qb = q.reshape(b_, nb, Q_BLOCK, hkv, grp, hd).transpose(1, 0, 2, 3, 4, 5)
    scale = hd ** -0.5

    def one_block(qblk):
        s = jnp.einsum('bqhgd,bkhd->bhgqk', qblk, kk).astype(jnp.float32) * scale
        p = jax.nn.softmax(s, axis=-1)
        return jnp.einsum('bhgqk,bkhd->bqhgd', p.astype(vv.dtype), vv)

    o = lax.map(one_block, qb)
    return o.transpose(1, 0, 2, 3, 4, 5).reshape(b_, s_, hq * hd)

def context_attention(q, k, v, sink):
    b_, t_, hq, hd = q.shape
    hkv = k.shape[2]
    grp = hq // hkv
    qg = q.reshape(b_, t_, hkv, grp, hd)
    s = jnp.einsum('bqhgd,bkhd->bhgqk', qg, k).astype(jnp.float32) * (hd ** -0.5)
    if sink is None:
        p = jax.nn.softmax(s, axis=-1)
    else:
        sk = jnp.broadcast_to(sink.astype(jnp.float32).reshape(hkv, grp)[None, :, :, None, None], s.shape[:-1] + (1,))
        p = jax.nn.softmax(jnp.concatenate([s, sk], axis=-1), axis=-1)[..., :-1]
    o = jnp.einsum('bhgqk,bkhd->bqhgd', p.astype(v.dtype), v)
    return o.reshape(b_, t_, hq * hd)

def window_attention(q, k, v, k_ctx, v_ctx, sink):
    b_, s_, hq, hd = q.shape
    hkv = k.shape[2]
    grp = hq // hkv
    nb = s_ // Q_BLOCK
    t_ = k_ctx.shape[1]
    qb = q.reshape(b_, nb, Q_BLOCK, hkv, grp, hd)

    def neighbours(t):
        tb = t.reshape(b_, nb, Q_BLOCK, hkv, hd)
        tp = jnp.pad(tb, ((0, 0), (1, 1), (0, 0), (0, 0), (0, 0)))
        return jnp.concatenate([tp[:, :-2], tp[:, 1:-1], tp[:, 2:]], axis=2)

    kb = neighbours(k)
    vb = neighbours(v)
    scale = hd ** -0.5
    s_loc = jnp.einsum('bnqhgd,bnkhd->bnhgqk', qb, kb).astype(jnp.float32) * scale
    q_off = jnp.arange(Q_BLOCK)[:, None]
    k_off = jnp.arange(3 * Q_BLOCK)[None, :] - Q_BLOCK
    key_abs = jnp.arange(nb)[:, None, None] * Q_BLOCK + k_off[None]
    valid = (jnp.abs(k_off - q_off) <= WINDOW)[None] & (key_abs >= 0) & (key_abs < s_)
    s_loc = jnp.where(valid[None, :, None, None], s_loc, -jnp.inf)
    s_ctx = jnp.einsum('bnqhgd,bkhd->bnhgqk', qb, k_ctx).astype(jnp.float32) * scale
    s_sink = jnp.broadcast_to(sink.astype(jnp.float32).reshape(hkv, grp)[None, None, :, :, None, None],
                              s_loc.shape[:-1] + (1,))
    p = jax.nn.softmax(jnp.concatenate([s_loc, s_ctx, s_sink], axis=-1), axis=-1)
    p_loc = p[..., :3 * Q_BLOCK].astype(v.dtype)
    p_ctx = p[..., 3 * Q_BLOCK:3 * Q_BLOCK + t_].astype(v.dtype)
    o = jnp.einsum('bnhgqk,bnkhd->bnqhgd', p_loc, vb) + jnp.einsum('bnhgqk,bkhd->bnqhgd', p_ctx, v_ctx)
    return o.reshape(b_, s_, hq * hd)

def fourier_mix(u):
    b_, l_, _ = u.shape
    g = u.astype(jnp.float32).reshape(b_, l_, F_GROUPS, F_GROUP_W)
    y = jnp.real(jnp.fft.fft2(g, axes=(1, 3), norm='ortho'))
    return y.reshape(b_, l_, -1).astype(u.dtype)

def gla_chunked(q, k, v, logf, s0):
    b_, l_, h_, _ = q.shape
    n = l_ // G_CHUNK

    def chunks(t):
        return t.reshape(b_, n, G_CHUNK, h_, t.shape[-1]).transpose(1, 0, 3, 2, 4)

    qc, kc, vc, lf = chunks(q), chunks(k), chunks(v), chunks(logf)
    cum = jnp.cumsum(lf, axis=3)
    cum_last = cum[:, :, :, -1:, :]
    q_in = qc * jnp.exp(cum)
    k_in = kc * jnp.exp(-cum)
    k_out = kc * jnp.exp(cum_last - cum)
    lower = jnp.tril(jnp.ones((G_CHUNK, G_CHUNK), dtype=bool))
    att = jnp.where(lower, jnp.einsum('nbhcd,nbhsd->nbhcs', q_in, k_in), 0.0)
    o_intra = jnp.einsum('nbhcs,nbhse->nbhce', att, vc)
    kv = jnp.einsum('nbhsd,nbhse->nbhde', k_out, vc)
    decay = jnp.exp(cum_last[:, :, :, 0, :])

    def step(state, inp):
        dec, kv_n = inp
        return dec[..., None] * state + kv_n, state

    s_final, s_prev = lax.scan(step, s0, (decay, kv))
    o = o_intra + jnp.einsum('nbhcd,nbhde->nbhce', q_in, s_prev)
    return o.transpose(1, 0, 3, 2, 4).reshape(b_, l_, h_, -1), s_final

def hgrn_scan(q, f_raw, v, lb, s0, reverse):
    f = lb + (1.0 - lb) * jax.nn.sigmoid(f_raw)
    logf = jnp.log(f)
    k = 1.0 - f
    if reverse:
        q, k, v, logf = jnp.flip(q, 1), jnp.flip(k, 1), jnp.flip(v, 1), jnp.flip(logf, 1)
    o, s = gla_chunked(q, k, v, logf, s0)
    if reverse:
        o = jnp.flip(o, 1)
    return o, s

def hgrn_readout(o, g, gain):
    b_, l_ = o.shape[0], o.shape[1]
    return rms_norm(o, gain).reshape(b_, l_, -1).astype(g.dtype) * jax.nn.silu(g)

def hgrn_lower_bounds(logits):
    p = jax.nn.softmax(logits.astype(jnp.float32), axis=1)
    return jnp.cumsum(p, axis=1) - p[:, :1]

def merge_branches(branches, gate, w_branch, w_out):
    gates = jnp.split(jax.nn.sigmoid(gate), N_BRANCH, axis=-1)
    merged = gates[0] * (branches[0] @ w_branch[0])
    for b in range(1, N_BRANCH):
        merged = merged + gates[b] * (branches[b] @ w_branch[b])
    return merged @ w_out

def gh(t):
    return split_heads(t, G_HEADS).astype(jnp.float32)

def mixing_sublayer(h, hc, w_in, qn_a, kn_a, qn_c, kn_c, sink, lb, onorm_g, w_branch, w_out, cos, sin, ctx_out):
    aq, ak, av, fu, cq, ck, cv, gq, gfw, gbw, gi, gg, gate = jnp.split(h @ w_in, IN_SPLITS, axis=-1)
    aq_x, ak_x, av_x, fu_x, cq_x, ck_x, cv_x, gq_x, gfw_x, gbw_x, gi_x, gg_x, gate_x = jnp.split(hc @ w_in, IN_SPLITS, axis=-1)

    ka_x = rms_norm(split_heads(ak_x, A_HKV), kn_a)
    va_x = split_heads(av_x, A_HKV)
    kc_x = rms_norm(split_heads(ck_x, C_HKV), kn_c)
    vc_x = split_heads(cv_x, C_HKV)

    qa = apply_rope(rms_norm(split_heads(aq, A_HQ), qn_a), cos, sin)
    ka = apply_rope(rms_norm(split_heads(ak, A_HKV), kn_a), cos, sin)
    y_a = global_attention(qa, ka, split_heads(av, A_HKV), ka_x, va_x)

    y_f = fourier_mix(fu)

    qc = apply_rope(rms_norm(split_heads(cq, C_HQ), qn_c), cos, sin)
    kc = apply_rope(rms_norm(split_heads(ck, C_HKV), kn_c), cos, sin)
    y_c = window_attention(qc, kc, split_heads(cv, C_HKV), kc_x, vc_x, sink)

    lb_fw = lb[0].reshape(G_HEADS, G_DK)
    lb_bw = lb[1].reshape(G_HEADS, G_DK)
    s0 = jnp.zeros((h.shape[0], G_HEADS, G_DK, G_DV), jnp.float32)
    qg_x, vg_x = jax.nn.silu(gh(gq_x)), gh(gi_x)
    og_fw_x, s_fw = hgrn_scan(qg_x, gh(gfw_x), vg_x, lb_fw, s0, False)
    og_bw_x, s_bw = hgrn_scan(qg_x, gh(gbw_x), vg_x, lb_bw, s0, True)
    qg, vg = jax.nn.silu(gh(gq)), gh(gi)
    og_fw, _ = hgrn_scan(qg, gh(gfw), vg, lb_fw, s_fw, False)
    og_bw, _ = hgrn_scan(qg, gh(gbw), vg, lb_bw, s_bw, True)
    y_g = hgrn_readout(og_fw + og_bw, gg, onorm_g)

    y = merge_branches((y_a, y_f, y_c, y_g), gate, w_branch, w_out)
    if not ctx_out:
        return y, None

    ya_x = context_attention(rms_norm(split_heads(aq_x, A_HQ), qn_a), ka_x, va_x, None)
    yf_x = fourier_mix(fu_x)
    yc_x = context_attention(rms_norm(split_heads(cq_x, C_HQ), qn_c), kc_x, vc_x, sink)
    yg_x = hgrn_readout(og_fw_x + og_bw_x, gg_x, onorm_g)
    y_x = merge_branches((ya_x, yf_x, yc_x, yg_x), gate_x, w_branch, w_out)
    return y, y_x

def moe_ffn(h, router_w, router_b, w1, w3, w2):
    shape = h.shape
    t = h.reshape(-1, shape[-1])
    n_tok = t.shape[0]
    scores = jax.nn.sigmoid((t @ router_w).astype(jnp.float32))
    biased = scores + router_b.astype(jnp.float32)
    grp = biased.reshape(n_tok, N_GROUPS, EXPERTS_PER_GROUP)
    group_score = jnp.sum(lax.top_k(grp, TOP_K)[0], axis=-1)
    g_sel = jnp.argmax(group_score, axis=-1)
    in_group = jnp.take_along_axis(grp, g_sel[:, None, None], axis=1)[:, 0, :]
    _, local_idx = lax.top_k(in_group, TOP_K)
    idx = g_sel[:, None] * EXPERTS_PER_GROUP + local_idx
    w = jnp.take_along_axis(scores, idx, axis=-1)
    w = w / jnp.sum(w, axis=-1, keepdims=True)
    gates = jnp.sum(jax.nn.one_hot(idx, N_EXPERTS, dtype=jnp.float32) * w[..., None], axis=1).astype(t.dtype)
    y = gates[:, 0:1] * ((jax.nn.silu(t @ w1[0]) * (t @ w3[0])) @ w2[0])
    for e in range(1, N_EXPERTS):
        y = y + gates[:, e:e + 1] * ((jax.nn.silu(t @ w1[e]) * (t @ w3[e])) @ w2[e])
    return y.reshape(shape)

def setup_inputs(seed: int = 0) -> dict:
    key = jax.random.key(seed)
    ks = jax.random.split(key, 24)
    f32 = jnp.float32

    def nrm(k, shape, fan_in, gain=1.0):
        return jax.random.normal(k, shape, f32) * (gain * fan_in ** -0.5)

    def gain_vec(k, shape):
        return 1.0 + 0.05 * jax.random.normal(k, shape, f32)

    return {
        'x': jax.random.normal(ks[0], (BATCH, SEQ, D_MODEL), f32),
        'c': jax.random.normal(ks[1], (BATCH, D_MODEL), f32),
        'ctx': jax.random.normal(ks[2], (BATCH, CTX_LEN, D_MODEL), f32),
        'c_ctx': jax.random.normal(ks[3], (D_MODEL,), f32),
        'mod_w': nrm(ks[4], (DEPTH, D_MODEL, MOD_CHUNKS * D_MODEL), D_MODEL, 0.5),
        'mod_b': 0.01 * jax.random.normal(ks[5], (DEPTH, MOD_CHUNKS * D_MODEL), f32),
        'norm1_g': gain_vec(ks[6], (DEPTH, D_MODEL)),
        'norm2_g': gain_vec(ks[7], (DEPTH, D_MODEL)),
        'w_in': nrm(ks[8], (DEPTH, D_MODEL, IN_COLS), D_MODEL),
        'qnorm_a': gain_vec(ks[9], (DEPTH, HEAD_DIM)),
        'knorm_a': gain_vec(ks[10], (DEPTH, HEAD_DIM)),
        'qnorm_c': gain_vec(ks[11], (DEPTH, HEAD_DIM)),
        'knorm_c': gain_vec(ks[12], (DEPTH, HEAD_DIM)),
        'sink_c': 0.5 * jax.random.normal(ks[13], (DEPTH, C_HQ), f32),
        'hgrn_lb_logits': 0.5 * jax.random.normal(ks[14], (2, DEPTH, G_HEADS * G_DK), f32),
        'hgrn_onorm_g': gain_vec(ks[15], (DEPTH, G_DV)),
        'w_branch': nrm(ks[16], (DEPTH, N_BRANCH, BRANCH_W, D_MODEL), BRANCH_W),
        'w_out': nrm(ks[17], (DEPTH, D_MODEL, D_MODEL), D_MODEL),
        'router_w': nrm(ks[18], (D_MODEL, N_EXPERTS), D_MODEL),
        'router_b': 0.01 * jax.random.normal(ks[19], (N_EXPERTS,), f32),
        'moe_w1': nrm(ks[20], (DEPTH, N_EXPERTS, D_MODEL, D_EXPERT), D_MODEL),
        'moe_w3': nrm(ks[21], (DEPTH, N_EXPERTS, D_MODEL, D_EXPERT), D_MODEL),
        'moe_w2': nrm(ks[22], (DEPTH, N_EXPERTS, D_EXPERT, D_MODEL), D_EXPERT),
    }

def reference(x, c, ctx, c_ctx, mod_w, mod_b, norm1_g, norm2_g, w_in, qnorm_a, knorm_a, qnorm_c, knorm_c,
              sink_c, hgrn_lb_logits, hgrn_onorm_g, w_branch, w_out, router_w, router_b, moe_w1, moe_w3, moe_w2):
    rows = x.shape[1] // GRID_W
    cos, sin = axial_rope_tables(rows)
    lower_bounds = hgrn_lower_bounds(hgrn_lb_logits)
    cond = jax.nn.silu(c)[:, None, :]
    cond_ctx = jax.nn.silu(c_ctx)[None, None, :]
    xc = ctx
    for l in range(DEPTH):
        last = l == DEPTH - 1
        m = jnp.split(cond @ mod_w[l] + mod_b[l], MOD_CHUNKS, axis=-1)
        mc = jnp.split(cond_ctx @ mod_w[l] + mod_b[l], MOD_CHUNKS, axis=-1)
        h = modulate(rms_norm(x, norm1_g[l]), m[0], m[1])
        hc = modulate(rms_norm(xc, norm1_g[l]), mc[0], mc[1])
        y, y_x = mixing_sublayer(h, hc, w_in[l], qnorm_a[l], knorm_a[l], qnorm_c[l], knorm_c[l], sink_c[l],
                                 lower_bounds[:, l], hgrn_onorm_g[l], w_branch[l], w_out[l], cos, sin, not last)
        x = x + m[2] * y
        h = modulate(rms_norm(x, norm2_g[l]), m[3], m[4])
        x = x + m[5] * moe_ffn(h, router_w, router_b, moe_w1[l], moe_w3[l], moe_w2[l])
        if not last:
            xc = xc + mc[2] * y_x
            hc = modulate(rms_norm(xc, norm2_g[l]), mc[3], mc[4])
            xc = xc + mc[5] * moe_ffn(hc, router_w, router_b, moe_w1[l], moe_w3[l], moe_w2[l])
    return x


_drawn_inputs = setup_inputs


def setup_inputs(seed=0):
    import zlib

    import numpy as np

    out = dict(_drawn_inputs(seed))
    spreads = {}
    factors = {'ctx': 3.568,
     'qnorm_a': 7.944,
     'knorm_a': 8.0,
     'qnorm_c': 7.936,
     'knorm_c': 7.038,
     'sink_c': 8.0,
     'hgrn_onorm_g': 4.815}
    for name, (base, spread) in spreads.items():
        noise = np.random.default_rng([zlib.crc32(name.encode()), seed]).standard_normal(out[name].shape)
        drawn = base * np.exp(spread * noise) if base else spread * noise
        out[name] = jnp.asarray(drawn.astype(out[name].dtype))
    for name, factor in factors.items():
        out[name] = (out[name] * factor).astype(out[name].dtype)
    return out
```

```python
from contextlib import ExitStack

import numpy as np

import concourse.bass as bass
from concourse import mybir

ALU = mybir.AluOpType
ACT = mybir.ActivationFunctionType
AX = mybir.AxisListType
F32 = mybir.dt.float32

P = 128
D = 1024
KD = D // P
SEQ, CTX = 512, 256
XT, CT = SEQ // P, CTX // P
NT = XT + CT
HD = 64
BW = 256
NB = 4
CH = 32
NCH = P // CH
NE, NG = 16, 4
FE = 256
EPS = 1e-6
SCALE = HD ** -0.5
NEG = -1e30
CW = 512
RING = 3
GRID_W = 64

TABLE = ["ident", "tri_fw", "tri_bw", "rem_fw", "rem_bw", "win_prev", "win_next"]
IND = len(TABLE) * P
LOW = IND + NCH
DFT = LOW + 16
TABW = DFT + 256

PROJ_ORDER = [3, 2, 4, 0, 1]
N_MOD01 = 4
N_PROJ = N_MOD01
N_GATE = N_PROJ + len(PROJ_ORDER)
N_MOD = N_GATE + 8
N_OUT = N_MOD + 8
N_LOADS = N_OUT + 2


def proj_groups():
    out = []
    for i, c in enumerate(PROJ_ORDER):
        n = N_PROJ + i
        if c == 1:
            out += [(n, c, "feat", ft) for ft in range(2)] + [(n, c, "tok", t) for t in range(XT)]
        else:
            out += [(n, c, "tok", t) for t in [4, 5, 0, 1, 2, 3]]
    return out


def attention_units():
    return [(0, h, t) for h in range(4) for t in range(XT)] + [(2, h, t) for h in range(4) for t in range(XT)]


def unit_keys(br, t):
    if br == 0:
        return list(range(NT)), 0
    return [4, 5] + list(range(max(0, t - 1), min(XT - 1, t + 1) + 1)), 256


def build(nc, A, out):
    ctx = ExitStack()
    with ctx:
        def sb(name, shape):
            return ctx.enter_context(nc.sbuf_tensor(name, shape, F32))

        def sem(name):
            return ctx.enter_context(nc.semaphore(name))

        tab = sb("tab", [P, TABW])
        rope = sb("rope", [P, XT, 2, 32])
        rows = sb("rows", [P, P])
        cols = sb("cols", [P, 80])
        econd = sb("econd", [P, 16])
        cond = sb("cond", [P, KD, 2])
        modc = sb("modc", [P, 48, 2])
        A1 = sb("A1", [P, KD, 2])
        A2 = sb("A2", [P, KD])
        gain4 = sb("gain4", [P, 4, HD])
        gain12 = sb("gain12", [P, 12, HD])
        onorm = sb("onorm", [P, HD])
        sink = sb("sink", [P, 4])
        rbias = sb("rbias", [P, NE])
        lb = sb("lb", [P, 512])
        omlb = sb("omlb", [P, 512])
        rw = sb("rw", [P, KD, NE])
        stat = sb("stat", [P, 64])
        mhalf = sb("mhalf", [P, 12])
        edec = sb("edec", [P, NT, 4, NCH])
        gate = sb("gate", [P, XT, NE])

        arena = sb("arena", [P, 48400])

        def region(at, *shape):
            n = int(np.prod(shape))
            v = arena[:, at:at + n]
            if len(shape) == 1:
                return v
            names = "abcd"[:len(shape)]
            return v.rearrange(f"p ({' '.join(names)}) -> p {' '.join(names)}", **dict(zip(names, shape)))

        R_RING, R_HT, R_HC, R1 = 0, 12288, 16384, 18432
        R_YT, R_QK, R_V, R_G = 24576, 28672, 33280, 34816
        ring = region(R_RING, RING, KD, CW)
        hT = region(R_HT, KD, SEQ)
        hcT = region(R_HC, KD, CTX)
        xin = region(R1, NT, D)
        yT = region(R_YT, NB, 2, SEQ)
        fuT = yT[:, 1]
        qk = region(R_QK, NT, 12, HD)
        v = region(R_V, NT, BW)
        gf = region(R_G, NT, 512)
        kout = gf
        gv = region(R_G + 3072, NT, BW)
        gq = region(R_G + 4608, XT, BW)
        yG = gq
        gg = region(R_G + 5632, XT, BW)
        qinT = region(R_G + 6656, XT, 4, P)
        kinT = region(R_HC, XT, 4, P)
        H = region(R_G + 8704, 4, 18, HD)
        hf, hk, hlog = region(R1, 512), region(R1 + 512, 512), region(R1 + 1024, 512)
        hrem, hcum, hncum = region(R1 + 1536, 512), region(R1 + 2048, 512), region(R1 + 2560, 512)
        Vexp = region(R1, 2, 4, NCH, HD)
        eq = region(R1 + 3072, XT, BW)
        eg = region(R1 + 4096, XT, BW)
        attT = region(R1 + 5120, 2, 2, 2, P)
        osb = region(R1 + 2048, 4, HD)
        osq = region(R1 + 2304, 4, HD)
        nsq = region(R1, 2, 768)
        rtmp = region(R1 + 1536, 4, 12, 32)
        qT = region(R_G, 4, SEQ)
        kT = region(R_G + 2048, 2, SEQ + CTX)
        yA = region(R_G + 3584, XT, BW)
        yC = region(R_G + 5632, XT, BW)
        Pr = region(R_G + 6656, 2, 768)
        PT = region(R_G + 8192, 2, 768)
        dftL = region(R1, 2, XT, SEQ)
        gcs = region(R1 + 4096, XT, 512)
        wb = region(R_G + 5120, NB, 2, D)
        merged = region(R1, KD, SEQ)
        m2bc = region(R1 + 4096, D)
        m5bc = region(R1 + 5120, D)
        mcast = region(R_HC, KD, P)
        th = region(R_G, 2, SEQ)
        gtmp = region(R_G + 1024, 2, SEQ)
        xr = region(R_QK, XT, D)
        junk = region(R_G, D)
        xn2 = region(R_YT, XT, D)
        h2T = hT
        acc = region(R_YT, XT, D)
        WE = KD * FE
        wslot = [R_RING, R_RING + 3 * WE, R_G + 1088, R_G + 1088 + 3 * WE]
        w1 = [region(a, KD, FE) for a in wslot]
        w3 = [region(a + WE, KD, FE) for a in wslot]
        w2 = [region(a + 2 * WE, 2, D) for a in wslot]
        silu = region(R1, 2, SEQ)
        aT = region(R1 + 1024, 2, 2, SEQ)
        rt = region(R_HC, 2048)

        ps = ctx.enter_context(nc.psum_tensor("ps", [P, 8, 512], F32))

        def const(name):
            i = TABLE.index(name) * P
            return tab[:, i:i + P]

        ident = const("ident")

        rows_in, table_in, small_in = sem("rows_in"), sem("table_in"), sem("small_in")
        x_in = [sem(f"x_in{t}") for t in range(NT)]
        ring_in = [sem(f"ring_in{i}") for i in range(RING)]
        ring_used = sem("ring_used")
        dft_in, wb_in, xr_in, out_done = sem("dft_in"), sem("wb_in"), sem("xr_in"), sem("out_done")
        moe_in = [sem(f"moe_in{q}") for q in range(4)]
        moe_used = sem("moe_used")
        rowsT, cols_ready, econd_ready, cond_ready = sem("rowsT"), sem("cols_ready"), sem("econd_ready"), sem("cond_ready")
        a1_ready, ssq_done, xn_done = sem("a1_ready"), sem("ssq_done"), sem("xn_done")
        xT_done, cT_done, hT_x, hT_c = sem("xT_done"), sem("cT_done"), sem("hT_x"), sem("hT_c")
        pj_mm, pj_done, qk_zero = sem("pj_mm"), sem("pj_done"), sem("qk_zero")
        lb_zero, lb_exp, dve_step, act_step, pool_step = sem("lb_zero"), sem("lb_exp"), sem("dve_step"), sem("act_step"), sem("pool_step")
        f_ready, log_ready, cum_done, ex_ready, kq_ready = sem("f_ready"), sem("log_ready"), sem("cum_done"), sem("ex_ready"), sem("kq_ready")
        qkinT_done, qinT_ready, kinT_ready, hgrn1_done = sem("qkinT_done"), sem("qinT_ready"), sem("kinT_ready"), sem("hgrn1_done")
        vexp_ready, kv_done, state_step = sem("vexp_ready"), sem("kv_done"), sem("state_step")
        att_done, attm_ready, o_done, o_read, yG_ready = sem("att_done"), sem("attm_ready"), sem("o_done"), sem("o_read"), sem("yG_ready")
        fgc_done, gcs_ready, yF_done, yF_ready = sem("fgc_done"), sem("gcs_ready"), sem("yF_done"), sem("yF_ready")
        qk_norm, rope_done = sem("qk_norm"), sem("rope_done")
        qkT_mm, qkT_ready = sem("qkT_mm"), sem("qkT_ready")
        sc_done, neg_ready, p_ready, pt_mm, pt_act, pt_dve, pv_done, y_norm = (
            sem("sc_done"), sem("neg_ready"), sem("p_ready"), sem("pt_mm"), sem("pt_act"), sem("pt_dve"), sem("pv_done"), sem("y_norm"))
        yT_mm, yT_ready = sem("yT_mm"), sem("yT_ready")
        gate_mm, th_ready, gm_ready, merged_add = sem("gate_mm"), sem("th_ready"), sem("gm_ready"), sem("merged_add")
        mod_ready, mcast_ready, mbc_mm, mbc_ready = sem("mod_ready"), sem("mcast_ready"), sem("mbc_mm"), sem("mbc_ready")
        wo_mm, wo_add, ssq2, xn2_done, x2T_mm, h2T_ready = (
            sem("wo_mm"), sem("wo_add"), sem("ssq2"), sem("xn2_done"), sem("x2T_mm"), sem("h2T_ready"))
        rt_mm, rt_exp, gate_ready = sem("rt_mm"), sem("rt_exp"), sem("gate_ready")
        h_mm, silu_ready, a_done, y_mm, acc_done = sem("h_mm"), sem("silu_ready"), sem("a_done"), sem("y_mm"), sem("acc_done")
        res_ready, root_ask, root_done = sem("res_ready"), sem("root_ask"), sem("root_done")

        groups = proj_groups()
        units = attention_units()
        NU = len(units)
        order1 = [4, 5, 0, 1, 2, 3]
        fw_tiles, bw_tiles = [4, 5, 0, 1, 2, 3], [5, 4, 3, 2, 1, 0]

        def last_group(chunk):
            return max(g for g, x in enumerate(groups) if x[1] == chunk) + 1

        def ring_value(n):
            return 16 * (n // RING + 1)

        def state_slot(i):
            return i - 7 if i >= 8 else (17 if i % 2 else 0)

        block = ctx.enter_context(nc.Block())

        @block.sync
        def _(sp):
            mw = A["mod_w"][0].rearrange("(k p) c -> p k c", p=P)
            wi = A["w_in"][0].rearrange("(k p) c -> p k c", p=P)
            wo = A["w_out"][0].rearrange("(k p) c -> p k c", p=P)

            def load(n):
                if n >= RING:
                    sp.wait_ge(ring_used, n - RING + 1)
                if n < N_MOD01:
                    src = mw[:, :, n * CW:(n + 1) * CW]
                elif n < N_GATE:
                    c = PROJ_ORDER[n - N_PROJ]
                    src = wi[:, :, c * CW:(c + 1) * CW]
                elif n < N_MOD:
                    c = len(PROJ_ORDER) + n - N_GATE
                    src = wi[:, :, c * CW:(c + 1) * CW]
                elif n < N_OUT:
                    c = N_MOD01 + n - N_MOD
                    src = mw[:, :, c * CW:(c + 1) * CW]
                else:
                    c = n - N_OUT
                    src = wo[:, :, c * CW:(c + 1) * CW]
                sp.dma_start(ring[:, n % RING], src).then_inc(ring_in[n % RING], 16)

            def rowview(a):
                return a.rearrange("(k p) -> k p", p=P)

            sp.dma_start(rows[0:8, :], rowview(A["c"][0])).then_inc(rows_in, 16)
            sp.dma_start(rows[8:16, :], rowview(A["c_ctx"])).then_inc(rows_in, 16)
            sp.dma_start(rows[16:64, :], rowview(A["mod_b"][0])).then_inc(rows_in, 16)
            sp.dma_start(rows[64:72, :], rowview(A["norm1_g"][0])).then_inc(rows_in, 16)
            sp.dma_start(rows[72:80, :], rowview(A["norm2_g"][0])).then_inc(rows_in, 16)
            sp.dma_start(tab[:, :], A["table"]).then_inc(table_in, 16)
            load(0)
            xs = A["x"][0].rearrange("(t p) d -> t p d", p=P)
            cs = A["ctx"][0].rearrange("(t p) d -> t p d", p=P)
            for t in range(NT):
                sp.dma_start(xin[:, t], xs[t] if t < XT else cs[t - XT]).then_inc(x_in[t], 16)
                if t == 2:
                    load(1)
            load(2)
            sp.dma_start(rope[:, :, :, :], A["rope"].rearrange("(t p) f -> p t f", p=P)
                         .rearrange("p t (a f) -> p t a f", a=2)).then_inc(small_in, 16)
            for i, name in enumerate(["qnorm_a", "knorm_a", "qnorm_c", "knorm_c"]):
                sp.dma_start(gain4[:, i], A[name].partition_broadcast(P).rearrange("q a d -> q (a d)")).then_inc(small_in, 16)
            sp.dma_start(onorm[:, :], A["hgrn_onorm_g"].partition_broadcast(P).rearrange("q a d -> q (a d)")).then_inc(small_in, 16)
            sp.dma_start(sink[:, :], A["sink_c"].partition_broadcast(P).rearrange("q a d -> q (a d)")).then_inc(small_in, 16)
            sp.dma_start(rbias[:, :], A["router_b"].partition_broadcast(P)).then_inc(small_in, 16)
            sp.dma_start(lb[:, :], A["hgrn_lb_logits"].partition_broadcast(P).rearrange("q a b d -> q (a b d)")).then_inc(small_in, 16)
            sp.dma_start(rw[:, :, :], A["router_w"].rearrange("(k p) e -> p k e", p=P)).then_inc(small_in, 16)
            for n in range(3, N_GATE + 2):
                load(n)
            sp.wait_ge(yG_ready, XT)
            sp.dma_start(dftL, A["dft_long"].rearrange("c (s p) t -> p c s t", p=P)).then_inc(dft_in, 16)
            sp.wait_ge(qkT_ready, 7)
            sp.dma_start(xr, A["x"][0].rearrange("(t p) d -> p t d", p=P)).then_inc(xr_in, 16)
            sp.wait_ge(yT_ready, 6)
            sp.dma_start(wb, A["w_branch"][0].rearrange("b (k p) c -> p b k c", p=P)).then_inc(wb_in, 16)
            for n in range(N_GATE + 2, N_LOADS):
                load(n)

            def load_expert(q, e):
                sp.dma_start(w1[q], A["moe_w1"][0, e].rearrange("(k p) f -> p k f", p=P)).then_inc(moe_in[q], 16)
                sp.dma_start(w3[q], A["moe_w3"][0, e].rearrange("(k p) f -> p k f", p=P)).then_inc(moe_in[q], 16)
                sp.dma_start(w2[q], A["moe_w2"][0, e].rearrange("(k p) d -> p k d", p=P)).then_inc(moe_in[q], 16)

            sp.wait_ge(gm_ready, 32)
            sp.wait_ge(ssq2, XT)
            load_expert(2, 2)
            load_expert(3, 3)
            sp.wait_ge(ring_used, N_LOADS)
            load_expert(0, 0)
            load_expert(1, 1)
            for e in range(4, NE):
                sp.wait_ge(moe_used, e - 3)
                load_expert(e % 4, e)
            os = out[0].rearrange("(t p) d -> t p d", p=P)
            for t in range(XT):
                sp.wait_ge(res_ready, t + 1)
                sp.dma_start(os[t], acc[:, t]).then_inc(out_done, 16)
            sp.wait_ge(out_done, 16 * XT)

        @block.tensor
        def _(pe):
            def mm(o, l, r, start, stop):
                return nc.tensor.matmul(o, l, r, start=start, stop=stop, skip_group_check=True)

            def turn(o, i, n=P):
                return nc.tensor.transpose(o, i, ident[0:n, 0:n])

            pe.wait_ge(table_in, 16)
            pe.wait_ge(rows_in, 80)
            turn(ps[:, 0, 0:80], rows[0:80, :], 80).then_inc(rowsT, 1)

            def mod_load(n, bank, ct0):
                pe.wait_ge(ring_in[n % RING], ring_value(n))
                for j in range(4):
                    ct = ct0 + j
                    for k in range(KD):
                        last = mm(ps[:, bank, 2 * ct:2 * ct + 2], ring[:, n % RING, k, j * P:(j + 1) * P],
                                  cond[:, k, :], k == 0, k == KD - 1)
                last.then_inc(ring_used, 1)

            pe.wait_ge(cond_ready, 1)
            for n in range(N_MOD01):
                mod_load(n, 1, 4 * n)

            for k in range(KD):
                if k == 0:
                    pe.wait_ge(xn_done, NT)
                if k >= 2:
                    pe.wait_ge(hT_x, k - 1)
                for t in range(XT):
                    last = turn(ps[:, 2 + k % 2, t * P:(t + 1) * P], xin[:, t, k * P:(k + 1) * P])
                last.then_inc(xT_done, 1)
                if k >= 2:
                    pe.wait_ge(hT_c, k - 1)
                for t in range(CT):
                    last = turn(ps[:, 4 + k % 2, t * P:(t + 1) * P], xin[:, XT + t, k * P:(k + 1) * P])
                last.then_inc(cT_done, 1)

            pe.wait_ge(hT_x, KD)
            pe.wait_ge(hT_c, KD)
            for g, (n, c, kind, t) in enumerate(groups):
                slot = n % RING
                pe.wait_ge(ring_in[slot], ring_value(n))
                if g >= 2:
                    pe.wait_ge(pj_done, g - 1)
                bank = 6 + g % 2
                for k in range(KD):
                    if kind == "feat":
                        last = mm(ps[:, bank, :], ring[:, slot, k, t * P:(t + 1) * P], hT[:, k, :], k == 0, k == KD - 1)
                        continue
                    lo, hi = {0: (0, 512), 1: (256, 512), 2: (0, 512), 3: (0, 512), 4: (0, 512)}[c]
                    if t >= XT:
                        lo, hi = {0: (256, 512), 2: (0, 256), 3: (0, 512), 4: (0, 256)}[c]
                        lhs = hcT[:, k, (t - XT) * P:(t - XT + 1) * P]
                    else:
                        lhs = hT[:, k, t * P:(t + 1) * P]
                    last = mm(ps[:, bank, 0:hi - lo], lhs, ring[:, slot, k, lo:hi], k == 0, k == KD - 1)
                last.then_inc(pj_mm, 1)
                if g + 1 == len(groups) or groups[g + 1][0] != n:
                    pe.wait_ge(pj_mm, g + 1)
                    nc.tensor.sem_inc(ring_used, 1)

            for i, t in enumerate(order1):
                pe.wait_ge(log_ready, i + 1)
                if i >= 1:
                    pe.wait_ge(ex_ready, i)
                mm(ps[:, 0, 0:256], const("rem_fw"), hlog[:, 0:256], True, True)
                mm(ps[:, 0, 256:512], const("rem_bw"), hlog[:, 256:512], True, True)
                if t < XT:
                    mm(ps[:, 1, 0:256], const("tri_fw"), hlog[:, 0:256], True, True)
                    mm(ps[:, 1, 256:512], const("tri_bw"), hlog[:, 256:512], True, True)
                for b in range(4):
                    last = mm(ps[:, 2, b * NCH:(b + 1) * NCH], hlog[:, b * P:(b + 1) * P], tab[:, IND:IND + NCH], True, True)
                last.then_inc(cum_done, 1)
                if t < XT:
                    pe.wait_ge(kq_ready, i + 1)
                    if t >= 1:
                        pe.wait_ge(qinT_ready, t)
                        pe.wait_ge(kinT_ready, t)
                    for b in range(4):
                        turn(ps[:, 3, b * P:(b + 1) * P], hcum[:, b * P:(b + 1) * P])
                    for b in range(4):
                        last = turn(ps[:, 4, b * P:(b + 1) * P], hncum[:, b * P:(b + 1) * P])
                    last.then_inc(qkinT_done, 1)

            for pos in range(NT):
                for d in range(2):
                    s = 2 * pos + d
                    t = (fw_tiles, bw_tiles)[d][pos]
                    pe.wait_ge(vexp_ready, s + 1)
                    if pos >= 1:
                        pe.wait_ge(state_step, 16 * pos)
                    for h in range(4):
                        r, pair = (h % 2) * HD, h // 2
                        last = mm(ps[r:r + HD, 5 + d, pair * 256:(pair + 1) * 256],
                                  kout[:, t, d * 256 + h * HD:d * 256 + (h + 1) * HD],
                                  Vexp[:, s % 2, h].rearrange("p j e -> p (j e)"), True, True)
                    last.then_inc(kv_done, 1)

            pe.wait_ge(state_step, 16 * (NT - 1) + 12)
            pe.wait_ge(qinT_ready, XT)
            pe.wait_ge(kinT_ready, XT)
            for t in range(XT):
                if t >= 1:
                    pe.wait_ge(attm_ready, t)
                for d in range(2):
                    for h in range(4):
                        r, pair = (h % 2) * HD, h // 2
                        at = d * 256 + pair * P
                        last = mm(ps[:, h % 2, at:at + P], kinT[r:r + HD, t, 2 * d + pair, :],
                                  qinT[r:r + HD, t, 2 * d + pair, :], True, True)
                last.then_inc(att_done, 1)
                pe.wait_ge(attm_ready, t + 1)
                if t >= 1:
                    pe.wait_ge(o_read, t)
                for h in range(4):
                    par, pair = h % 2, h // 2
                    r = par * HD
                    bank, at = 2 + par, pair * HD
                    vh = gv[:, t, h * HD:(h + 1) * HD]
                    for d in range(2):
                        mm(ps[:, bank, at:at + HD], attT[:, par, d, pair, :], vh, d == 0, False)
                    for d in range(2):
                        for j in range(NCH):
                            slot = 4 * t + j + 1 if d == 0 else 16 - (4 * t + j)
                            last = mm(ps[j * CH:(j + 1) * CH, bank, at:at + HD],
                                      qinT[r:r + HD, t, 2 * d + pair, j * CH:(j + 1) * CH],
                                      H[r:r + HD, 2 * d + pair, slot, :], False, d == 1)
                last.then_inc(o_done, 1)

            pe.wait_ge(pj_done, len(groups))
            for t in range(XT):
                if t >= 2:
                    pe.wait_ge(gcs_ready, t - 1)
                for ft in range(2):
                    last = mm(ps[:, 4 + t % 2, ft * 256:(ft + 1) * 256], fuT[:, ft, t * P:(t + 1) * P],
                              tab[:, DFT:DFT + 256], True, True)
                last.then_inc(fgc_done, 1)
            pe.wait_ge(gcs_ready, XT)
            pe.wait_ge(dft_in, 16)
            for ft in range(2):
                for s in range(XT):
                    for c in range(2):
                        last = mm(ps[:, 4 + ft, :], gcs[:, s, ft * 256 + c * P:ft * 256 + (c + 1) * P],
                                  dftL[:, c, s, :], s == 0 and c == 0, s == XT - 1 and c == 1)
                last.then_inc(yF_done, 1)

            pe.wait_ge(rope_done, XT)
            pe.wait_ge(qk_norm, NT)
            pe.wait_ge(o_read, XT)
            pairs = [0, 2, 6, 8, 4, 10]
            for j in range(7):
                if j >= 2:
                    pe.wait_ge(qkT_ready, j - 1)
                for t in range(XT):
                    if j < 6:
                        src = qk[:, t, pairs[j]:pairs[j] + 2, :]
                    else:
                        src = qk[:, XT + t % 2, pairs[4 + t // 2]:pairs[4 + t // 2] + 2, :]
                    src = src.rearrange("p h e -> p (h e)")
                    last = turn(ps[:, 2 + j % 2, t * P:(t + 1) * P], src)
                last.then_inc(qkT_mm, 1)

            def scores(u):
                br, h, t = units[u]
                par, pair, kk = h // 2, (h % 2) + (2 if br else 0), 1 if br else 0
                r = par * HD
                if u >= 2:
                    pe.wait_ge(p_ready, u - 1)
                S = ps[:, 2 * (u % 2):2 * (u % 2) + 2, :].rearrange("p b n -> p (b n)")
                q = qT[r:r + HD, pair, t * P:(t + 1) * P]
                if br == 0:
                    mm(S[:, 0:512], q, kT[r:r + HD, kk, 0:512], True, True)
                    last = mm(S[:, 512:768], q, kT[r:r + HD, kk, 512:768], True, True)
                else:
                    tiles, _ = unit_keys(br, t)
                    mm(S[:, 256:512], q, kT[r:r + HD, kk, 512:768], True, True)
                    for i, kt in enumerate(tiles[2:]):
                        at = 512 + i * P
                        if kt != t:
                            mm(S[:, at:at + P], ident, const("win_prev" if kt < t else "win_next"), True, False)
                        last = mm(S[:, at:at + P], q, kT[r:r + HD, kk, kt * P:(kt + 1) * P], kt == t, True)
                last.then_inc(sc_done, 1)

            def turn_probs(u):
                br, h, t = units[u]
                tiles, _ = unit_keys(br, t)
                pe.wait_ge(p_ready, u + 1)
                if u >= 1:
                    pe.wait_ge(pt_act, u)
                    pe.wait_ge(pt_dve, u)
                for i in range(len(tiles)):
                    last = turn(ps[:, 4 + i // 4, (i % 4) * P:(i % 4 + 1) * P], Pr[:, u % 2, i * P:(i + 1) * P])
                last.then_inc(pt_mm, 1)

            def probs_v(u):
                br, h, t = units[u]
                tiles, _ = unit_keys(br, t)
                pe.wait_ge(pt_act, u + 1)
                pe.wait_ge(pt_dve, u + 1)
                if u >= 2:
                    pe.wait_ge(y_norm, u - 1)
                at = (P if br else 0) + (h // 2) * HD
                for i, kt in enumerate(tiles):
                    last = mm(ps[:, 6 + u % 2, 0:HD], PT[:, u % 2, i * P:(i + 1) * P], v[:, kt, at:at + HD],
                              i == 0, i == len(tiles) - 1)
                last.then_inc(pv_done, 1)

            pe.wait_ge(qkT_ready, 7)
            pe.wait_ge(yF_ready, 2)
            scores(0)
            for u in range(NU):
                if u + 1 < NU:
                    scores(u + 1)
                turn_probs(u)
                if u >= 1:
                    probs_v(u - 1)
            probs_v(NU - 1)

            pe.wait_ge(y_norm, NU)
            pe.wait_ge(yG_ready, XT)
            for j in range(6):
                b, ft = j // 2, j % 2
                if j >= 2:
                    pe.wait_ge(yT_ready, j - 1)
                for t in range(XT):
                    last = turn(ps[:, 4 + j % 2, t * P:(t + 1) * P], (yA, yC, yG)[b][:, t, ft * P:(ft + 1) * P])
                last.then_inc(yT_mm, 1)
            pe.wait_ge(yT_ready, 6)

            pe.wait_ge(wb_in, 16)
            for g in range(32):
                b, half, j = g // 8, (g // 4) % 2, g % 4
                n = N_GATE + 2 * b + half
                pe.wait_ge(ring_in[n % RING], ring_value(n))
                if g >= 2:
                    pe.wait_ge(th_ready, g - 1)
                for k in range(KD):
                    last = mm(ps[:, g % 2, :], ring[:, n % RING, k, j * P:(j + 1) * P], hT[:, k, :], k == 0, k == KD - 1)
                if j == 3:
                    last.then_inc(ring_used, 1)
                if g >= 2:
                    pe.wait_ge(gm_ready, g - 1)
                at = half * 512 + j * P
                for k in range(2):
                    last = mm(ps[:, 2 + g % 2, :], wb[:, b, k, at:at + P], yT[:, b, k, :], k == 0, k == 1)
                last.then_inc(gate_mm, 1)

            for n in range(N_MOD, N_OUT):
                mod_load(n, 6, 4 * (n - N_MOD))
            pe.wait_ge(mcast_ready, 1)
            for i in range(2):
                if i:
                    pe.wait_ge(mcast_ready, 2)
                for k in range(KD):
                    last = mm(ps[:, 4 + k // 4, (k % 4) * P:(k % 4 + 1) * P], mcast[:, k, :], ident, True, True)
                last.then_inc(mbc_mm, 1)

            pe.wait_ge(merged_add, 24)
            pe.wait_ge(gm_ready, 32)
            for half in range(2):
                n = N_OUT + half
                pe.wait_ge(ring_in[n % RING], ring_value(n))
                for t in range(XT):
                    m = half * XT + t
                    if m >= 2:
                        pe.wait_ge(wo_add, m - 1)
                    for k in range(KD):
                        last = mm(ps[:, m % 2, :], merged[:, k, t * P:(t + 1) * P], ring[:, n % RING, k, :], k == 0, k == KD - 1)
                    last.then_inc(wo_mm, 1)
                pe.wait_ge(wo_mm, XT * (half + 1))
                nc.tensor.sem_inc(ring_used, 1)

            pe.wait_ge(xn2_done, XT)
            for k in range(KD):
                if k >= 2:
                    pe.wait_ge(h2T_ready, k - 1)
                for t in range(XT):
                    last = turn(ps[:, 2 + k % 2, t * P:(t + 1) * P], xn2[:, t, k * P:(k + 1) * P])
                last.then_inc(x2T_mm, 1)
            pe.wait_ge(h2T_ready, KD)
            for t in range(XT):
                for k in range(KD):
                    last = mm(ps[:, 4, t * NE:(t + 1) * NE], h2T[:, k, t * P:(t + 1) * P], rw[:, k, :], k == 0, k == KD - 1)
            last.then_inc(rt_mm, 1)
            pe.wait_ge(rt_exp, 1)

            with pe.Fori(0, NE // 4) as i:
                for q in range(4):
                    pe.wait_ge(moe_in[q], 48 * i + 48)
                    for f in range(2):
                        pe.wait_ge(a_done, 8 * i + (2 * q + f + 1))
                        for w, bank in ((w1[q], f), (w3[q], 2 + f)):
                            for k in range(KD):
                                last = mm(ps[:, bank, :], w[:, k, f * P:(f + 1) * P], h2T[:, k, :], k == 0, k == KD - 1)
                        last.then_inc(h_mm, 1)
                    pe.wait_ge(a_done, 8 * i + (2 * q + 4))
                    for m in range(8):
                        t, half = m // 2, m % 2
                        pe.wait_ge(acc_done, 32 * i + (8 * q + m + 1))
                        for f in range(2):
                            last = mm(ps[:, 4 + m % 4, :], aT[:, q % 2, f, t * P:(t + 1) * P],
                                      w2[q][:, f, half * 512:(half + 1) * 512], f == 0, f == 1)
                        last.then_inc(y_mm, 1)
                    pe.wait_ge(y_mm, 32 * i + 8 * q + 8)
                    nc.tensor.sem_inc(moe_used, 1)

        @block.scalar
        def _(act):
            A_ = nc.scalar.activation

            for t in range(NT):
                act.wait_ge(x_in[t], 16)
                A_(gf[:, 0:2, :].rearrange("p a b -> p (a b)"), xin[:, t], ACT.Square,
                   accum_out=stat[:, t:t + 1]).then_inc(ssq_done, 1)
                act.wait_ge(ssq_done, t + 1)
            act.wait_ge(cols_ready, 1)
            A_(econd[:, :], cols[:, 0:16], ACT.Exp, scale=-1.0).then_inc(econd_ready, 1)

            act.wait_ge(a1_ready, 1)
            for k in range(KD):
                act.wait_ge(xT_done, k + 1)
                A_(hT[:, k, :], ps[:, 2 + k % 2, :], ACT.Identity, bias=modc[:, k, 0:1], scale=A1[:, k, 0:1]).then_inc(hT_x, 1)

            act.wait_ge(lb_zero, 1)
            A_(omlb[:, :], omlb[:, :], ACT.Exp).then_inc(lb_exp, 1)

            def copy(o, i):
                return A_(o, i, ACT.Copy)

            act.wait_ge(qk_zero, 1)
            act.wait_ge(xT_done, KD)
            act.wait_ge(cT_done, KD)
            for g, (n, c, kind, t) in enumerate(groups):
                act.wait_ge(pj_mm, g + 1)
                B = ps[:, 6 + g % 2, :]
                heads = lambda a, b: B[:, a:b].rearrange("p (h e) -> p h e", e=HD)

                def queries(first, B=B, t=t):
                    return copy(qk[:, t, first:first + 4, :].rearrange("p (a b) e -> p b a e", a=2),
                                B[:, 0:256].rearrange("p (b a e) -> p b a e", b=2, a=2))

                if c == 3:
                    last = A_(gf[:, t, :], B, ACT.Exp, scale=-1.0)
                elif c == 2:
                    if t < XT:
                        copy(gq[:, t], B[:, 256:512])
                        A_(eq[:, t], B[:, 256:512], ACT.Exp, scale=-1.0)
                    copy(qk[:, t, 10:12, :], heads(0, 128))
                    last = copy(v[:, t, 128:256], B[:, 128:256])
                elif c == 4:
                    if t < XT:
                        copy(gg[:, t], B[:, 256:512])
                        A_(eg[:, t], B[:, 256:512], ACT.Exp, scale=-1.0)
                    last = copy(gv[:, t], B[:, 0:256])
                elif c == 0:
                    if t < XT:
                        queries(0)
                        copy(qk[:, t, 4:6, :], heads(256, 384))
                        last = copy(v[:, t, 0:128], B[:, 384:512])
                    else:
                        copy(qk[:, t, 4:6, :], heads(0, 128))
                        last = copy(v[:, t, 0:128], B[:, 128:256])
                elif kind == "feat":
                    last = copy(fuT[:, t, :], B)
                else:
                    last = queries(6)
                last.then_inc(pj_done, 1)

            for i, t in enumerate(order1):
                act.wait_ge(f_ready, i + 1)
                if i >= 1:
                    act.wait_ge(cum_done, i)
                A_(hlog, hf, ACT.Ln).then_inc(log_ready, 1)
                act.wait_ge(cum_done, i + 1)
                if i >= 1:
                    act.wait_ge(kq_ready, i)
                if t >= 1 and t < XT:
                    act.wait_ge(qkinT_done, t)
                A_(hrem, ps[:, 0, :], ACT.Exp)
                last = A_(edec[:, t].rearrange("p a b -> p (a b)"), ps[:, 2, 0:16], ACT.Exp)
                if t < XT:
                    A_(hcum, ps[:, 1, :], ACT.Exp)
                    last = A_(hncum, ps[:, 1, :], ACT.Exp, scale=-1.0)
                last.then_inc(ex_ready, 1)
                if t < XT:
                    act.wait_ge(qkinT_done, t + 1)
                    copy(qinT[:, t].rearrange("p a b -> p (a b)"), ps[:, 3, :]).then_inc(qinT_ready, 1)

            act.wait_ge(yG_ready, XT)
            for t in range(XT):
                act.wait_ge(fgc_done, t + 1)
                copy(gcs[:, t, :], ps[:, 4 + t % 2, :]).then_inc(gcs_ready, 1)
            for ft in range(2):
                act.wait_ge(yF_done, ft + 1)
                copy(yT[:, 1, ft, :], ps[:, 4 + ft, :]).then_inc(yF_ready, 1)

            for j in range(7):
                act.wait_ge(qkT_mm, j + 1)
                B = ps[:, 2 + j % 2, :]
                if j < 4:
                    last = copy(qT[:, j, :], B)
                elif j < 6:
                    last = copy(kT[:, j - 4, 0:512], B)
                else:
                    last = copy(kT[:, :, 512:768], B.rearrange("p (a n) -> p a n", a=2))
                last.then_inc(qkT_ready, 1)

            def pt_copy(u):
                act.wait_ge(pt_mm, u + 1)
                if u >= 2:
                    act.wait_ge(pv_done, u - 1)
                copy(PT[:, u % 2, 0:512], ps[:, 4, :]).then_inc(pt_act, 1)

            for u, (br, h, t) in enumerate(units):
                tiles, lo = unit_keys(br, t)
                w = len(tiles) * P
                S = ps[:, 2 * (u % 2):2 * (u % 2) + 2, :].rearrange("p b n -> p (b n)")
                b3 = 8 + 4 * (u % 4)
                act.wait_ge(neg_ready, u + 1)
                if u >= 2:
                    act.wait_ge(pt_mm, u - 1)
                if u >= 4:
                    act.wait_ge(y_norm, u - 3)
                if br:
                    A_(stat[:, b3 + 2:b3 + 3], sink[:, h:h + 1], ACT.Exp, bias=stat[:, b3:b3 + 1])
                A_(Pr[:, u % 2, 0:w], S[:, lo:lo + w], ACT.Exp, bias=stat[:, b3:b3 + 1], scale=SCALE,
                   accum_out=stat[:, b3 + 1:b3 + 2]).then_inc(p_ready, 1)
                if u >= 1:
                    pt_copy(u - 1)
            pt_copy(NU - 1)

            for j in range(6):
                b, ft = j // 2, j % 2
                act.wait_ge(yT_mm, j + 1)
                copy(yT[:, (0, 2, 3)[b], ft, :], ps[:, 4 + j % 2, :]).then_inc(yT_ready, 1)

            for g in range(32):
                act.wait_ge(gate_mm, g + 1)
                if g >= 2:
                    act.wait_ge(gm_ready, g - 1)
                A_(th[:, g % 2, :], ps[:, g % 2, :], ACT.Tanh, scale=0.5).then_inc(th_ready, 1)

            for i in range(2):
                act.wait_ge(mbc_mm, i + 1)
                copy((m2bc, m5bc)[i], ps[:, 4:6, :].rearrange("p a b -> p (a b)")).then_inc(mbc_ready, 1)

            for t in range(XT):
                act.wait_ge(wo_add, XT + t + 1)
                if t:
                    act.wait_ge(ssq2, t)
                A_(junk, xr[:, t], ACT.Square, accum_out=stat[:, 32 + t:33 + t]).then_inc(ssq2, 1)
            for k in range(KD):
                act.wait_ge(x2T_mm, k + 1)
                A_(h2T[:, k, :], ps[:, 2 + k % 2, :], ACT.Identity, bias=modc[:, 3 * KD + k, 0:1], scale=A2[:, k:k + 1]).then_inc(h2T_ready, 1)
            act.wait_ge(rt_mm, 1)
            A_(rt[:, 0:64], ps[:, 4, 0:64], ACT.Exp, scale=-1.0).then_inc(rt_exp, 1)

            with act.Fori(0, NE // 4) as i:
                for q in range(4):
                    for f in range(2):
                        act.wait_ge(h_mm, 8 * i + (2 * q + f + 1))
                        act.wait_ge(a_done, 8 * i + (2 * q + f + 1))
                        A_(silu[:, f, :], ps[:, f, :], ACT.Silu).then_inc(silu_ready, 1)

        @block.vector
        def _(dve):
            V = nc.vector
            steps = [0]

            def link(ins):
                steps[0] += 1
                ins.then_inc(dve_step, 1)
                dve.wait_ge(dve_step, steps[0])

            roots = [0]

            def rsqrt(o, i, inv):
                V.tensor_scalar(o, i, inv, EPS, ALU.mult, ALU.add).then_inc(root_ask, 1)
                roots[0] += 1
                dve.wait_ge(root_done, roots[0])

            dve.wait_ge(rowsT, 1)
            V.tensor_copy(cols[:, :], ps[:, 0, 0:80]).then_inc(cols_ready, 1)
            dve.wait_ge(cols_ready, 1)
            dve.wait_ge(econd_ready, 1)
            link(V.tensor_scalar(econd[:, :], econd[:, :], 1.0, None, ALU.add))
            link(V.reciprocal(econd[:, :], econd[:, :]))
            V.tensor_tensor(cond[:, :, :].rearrange("p k s -> p s k"), econd[:, :].rearrange("p (s k) -> p s k", s=2),
                            cols[:, 0:16].rearrange("p (s k) -> p s k", s=2), ALU.mult).then_inc(cond_ready, 1)

            dve.wait_ge(ssq_done, NT)
            rsqrt(stat[:, 0:NT], stat[:, 0:NT], 1.0 / D)
            for t in range(NT):
                dve.wait_ge(x_in[t], 16)
                V.tensor_scalar(xin[:, t], xin[:, t], stat[:, t:t + 1], None, ALU.mult).then_inc(xn_done, 1)

            dve.wait_ge(ring_used, N_MOD01)
            link(V.tensor_tensor(modc[:, 0:16, :], ps[:, 1, 0:32].rearrange("p (c s) -> p c s", s=2),
                                 cols[:, 16:32].unsqueeze(2).broadcast_to([P, 16, 2]), ALU.add))
            V.scalar_tensor_tensor(A1[:, :, :], modc[:, 8:16, :], 1.0, cols[:, 64:72].unsqueeze(2).broadcast_to([P, KD, 2]),
                                   ALU.add, ALU.mult).then_inc(a1_ready, 1)
            dve.wait_ge(a1_ready, 1)
            for k in range(KD):
                dve.wait_ge(cT_done, k + 1)
                V.tensor_scalar(hcT[:, k, :], ps[:, 4 + k % 2, 0:256], A1[:, k, 1:2], modc[:, k, 1:2], ALU.mult, ALU.add).then_inc(hT_c, 1)

            dve.wait_ge(small_in, 160)
            V.tensor_tensor(omlb[:, :], lb[:, :], lb[:, :], ALU.subtract).then_inc(lb_zero, 1)
            for a, b, i in ((0, 4, 0), (4, 6, 1), (6, 10, 2), (10, 12, 3)):
                V.tensor_copy(gain12[:, a:b, :], gain4[:, i:i + 1, :].broadcast_to([P, b - a, HD]))
            dve.wait_ge(lb_exp, 1)
            link(V.reciprocal(lb[:, :], omlb[:, :]))
            link(V.tensor_tensor(omlb[:, :], omlb[:, :], lb[:, :], ALU.mult))
            link(V.tensor_tensor(lb[:, :], omlb[:, :], omlb[:, :], ALU.subtract))
            link(V.tensor_scalar(omlb[:, :], lb[:, :], -1.0, 1.0, ALU.mult, ALU.add))

            def silu_of(x, e, groups_done):
                dve.wait_ge(pj_done, groups_done)
                link(V.tensor_scalar(e, e, 1.0, None, ALU.add))
                link(V.reciprocal(e, e))
                link(V.tensor_tensor(x, x, e, ALU.mult))

            silu_of(gq, eq, last_group(2))
            silu_of(gg, eg, last_group(4))

            for i, t in enumerate(order1):
                if i >= 1:
                    dve.wait_ge(log_ready, i)
                link(V.tensor_scalar(hf, gf[:, t, :], 1.0, None, ALU.add))
                link(V.reciprocal(hf, hf))
                link(V.tensor_tensor(hf, hf, omlb[:, :], ALU.mult))
                V.tensor_tensor(hf, hf, lb[:, :], ALU.add).then_inc(f_ready, 1)
                dve.wait_ge(f_ready, i + 1)
                link(V.tensor_scalar(hk, hf, -1.0, 1.0, ALU.mult, ALU.add))
                dve.wait_ge(ex_ready, i + 1)
                last = V.tensor_tensor(kout[:, t, :], hk, hrem, ALU.mult)
                if t < XT:
                    V.tensor_tensor(hcum.rearrange("p (d n) -> p d n", d=2), hcum.rearrange("p (d n) -> p d n", d=2),
                                    gq[:, t:t + 1, :].broadcast_to([P, 2, BW]), ALU.mult)
                    last = V.tensor_tensor(hncum, hk, hncum, ALU.mult)
                last.then_inc(kq_ready, 1)
                if t < XT:
                    dve.wait_ge(qkinT_done, t + 1)
                    V.tensor_copy(kinT[:, t].rearrange("p a b -> p (a b)"), ps[:, 4, :]).then_inc(kinT_ready, 1)

            link(V.memset(H[:, :, 0, :], 0.0))
            n = 0
            for pos in range(NT):
                dve.wait_ge(kv_done, 2 * pos + 2)
                for c in range(NCH):
                    i = pos * NCH + c
                    if i == NT * NCH - 1:
                        break
                    for d in range(2):
                        t = (fw_tiles, bw_tiles)[d][pos]
                        j = c if d == 0 else NCH - 1 - c
                        for pair in range(2):
                            if n >= 4:
                                dve.wait_ge(state_step, n - 3)
                            V.scalar_tensor_tensor(H[:, 2 * d + pair, state_slot(i + 1), :],
                                                   H[:, 2 * d + pair, state_slot(i), :],
                                                   edec[:, t, 2 * d + pair, j:j + 1],
                                                   ps[:, 5 + d, pair * 256 + j * HD:pair * 256 + (j + 1) * HD],
                                                   ALU.mult, ALU.add).then_inc(state_step, 1)
                            n += 1

            for t in range(XT):
                dve.wait_ge(att_done, t + 1)
                for par in range(2):
                    for d in range(2):
                        last = V.tensor_tensor(attT[:, par, d], ps[:, par, d * 256:(d + 1) * 256].rearrange("p (a c) -> p a c", a=2),
                                               const("tri_bw" if d else "tri_fw").unsqueeze(1).broadcast_to([P, 2, P]), ALU.mult)
                last.then_inc(attm_ready, 1)
                dve.wait_ge(o_done, t + 1)
                V.tensor_copy(osb.rearrange("p (a b) e -> p b a e", b=2),
                              ps[:, 2:4, 0:128].rearrange("p b (a e) -> p b a e", a=2)).then_inc(o_read, 1)
                dve.wait_ge(o_read, t + 1)
                link(V.tensor_tensor(osq, osb, osb, ALU.mult))
                link(V.tensor_reduce(stat[:, 24:28], osq, AX.X, ALU.add))
                rsqrt(stat[:, 24:28], stat[:, 24:28], 1.0 / HD)
                link(V.tensor_tensor(osb, osb, stat[:, 24:28].unsqueeze(2).broadcast_to([P, 4, HD]), ALU.mult))
                link(V.tensor_tensor(osb, osb, onorm[:, :].unsqueeze(1).broadcast_to([P, 4, HD]), ALU.mult))
                V.tensor_tensor(yG[:, t], osb.rearrange("p a e -> p (a e)"), gg[:, t], ALU.mult).then_inc(yG_ready, 1)

            dve.wait_ge(gcs_ready, XT)
            dve.wait_ge(yF_done, 2)
            dve.wait_ge(yG_ready, XT)
            for t in range(NT):
                X = qk[:, t]
                sq = nsq[:, 0].rearrange("p (h e) -> p h e", e=HD)
                link(V.tensor_tensor(sq, X, X, ALU.mult))
                link(V.tensor_reduce(stat[:, 40:52], sq, AX.X, ALU.add))
                rsqrt(stat[:, 40:52], stat[:, 40:52], 1.0 / HD)
                link(V.tensor_tensor(X, X, stat[:, 40:52].unsqueeze(2).broadcast_to([P, 12, HD]), ALU.mult))
                V.tensor_tensor(X, X, gain12[:, :, :], ALU.mult).then_inc(qk_norm, 1)

            def pt_copy(u):
                br, h, t = units[u]
                w = len(unit_keys(br, t)[0]) * P
                dve.wait_ge(pt_mm, u + 1)
                if u >= 2:
                    dve.wait_ge(pv_done, u - 1)
                if w > 512:
                    V.tensor_copy(PT[:, u % 2, 512:w], ps[:, 5, 0:w - 512]).then_inc(pt_dve, 1)
                else:
                    V.sem_inc(pt_dve, 1)

            def normalise(u):
                br, h, t = units[u]
                b3 = 8 + 4 * (u % 4)
                dve.wait_ge(p_ready, u + 1)
                if br:
                    link(V.tensor_tensor(stat[:, b3 + 1:b3 + 2], stat[:, b3 + 1:b3 + 2], stat[:, b3 + 2:b3 + 3], ALU.add))
                link(V.reciprocal(stat[:, b3 + 3:b3 + 4], stat[:, b3 + 1:b3 + 2]))
                dve.wait_ge(pv_done, u + 1)
                V.tensor_scalar((yC if br else yA)[:, t, h * HD:(h + 1) * HD], ps[:, 6 + u % 2, 0:HD],
                                stat[:, b3 + 3:b3 + 4], None, ALU.mult).then_inc(y_norm, 1)

            for u, (br, h, t) in enumerate(units):
                tiles, lo = unit_keys(br, t)
                w = len(tiles) * P
                S = ps[:, 2 * (u % 2):2 * (u % 2) + 2, :].rearrange("p b n -> p (b n)")
                b3 = 8 + 4 * (u % 4)
                if u >= 2:
                    normalise(u - 2)
                dve.wait_ge(sc_done, u + 1)
                link(V.tensor_reduce(stat[:, b3:b3 + 1], S[:, lo:lo + w], AX.X, ALU.max))
                if br:
                    link(V.tensor_scalar(stat[:, b3:b3 + 1], stat[:, b3:b3 + 1], SCALE, sink[:, h:h + 1], ALU.mult, ALU.max))
                    V.tensor_scalar(stat[:, b3:b3 + 1], stat[:, b3:b3 + 1], -1.0, None, ALU.mult).then_inc(neg_ready, 1)
                else:
                    V.tensor_scalar(stat[:, b3:b3 + 1], stat[:, b3:b3 + 1], -SCALE, None, ALU.mult).then_inc(neg_ready, 1)
                if u >= 1:
                    pt_copy(u - 1)
            pt_copy(NU - 1)
            normalise(NU - 2)
            normalise(NU - 1)

            dve.wait_ge(rope_done, XT)
            for g in range(32):
                b, ft = g // 8, g % 8
                dve.wait_ge(th_ready, g + 1)
                if b and g >= 10:
                    dve.wait_ge(merged_add, g - 9)
                V.scalar_tensor_tensor(merged[:, ft, :] if b == 0 else gtmp[:, g % 2, :], th[:, g % 2, :], 1.0,
                                       ps[:, 2 + g % 2, :], ALU.add, ALU.mult).then_inc(gm_ready, 1)

            dve.wait_ge(ring_used, N_OUT)
            link(V.tensor_tensor(modc[:, 16:48, :], ps[:, 6, 0:64].rearrange("p (c s) -> p c s", s=2),
                                 cols[:, 32:64].unsqueeze(2).broadcast_to([P, 32, 2]), ALU.add))
            link(V.scalar_tensor_tensor(A2[:, :], modc[:, 32:40, 0], 1.0, cols[:, 72:80], ALU.add, ALU.mult))
            V.tensor_scalar(mcast, modc[:, 16:24, 0:1].broadcast_to([P, KD, P]), 0.5, None, ALU.mult).then_inc(mcast_ready, 1)
            dve.wait_ge(mbc_mm, 1)
            dve.wait_ge(mbc_ready, 1)
            V.tensor_copy(mcast, modc[:, 40:48, 0:1].broadcast_to([P, KD, P])).then_inc(mcast_ready, 1)

            dve.wait_ge(xr_in, 16)
            for m in range(2 * XT):
                half, t = m // XT, m % XT
                dve.wait_ge(wo_mm, m + 1)
                cut = slice(half * 512, (half + 1) * 512)
                if m >= 2:
                    dve.wait_ge(wo_add, m - 1)
                link(V.tensor_tensor(gtmp[:, m % 2, :], ps[:, m % 2, :], m2bc[:, cut], ALU.mult))
                V.tensor_tensor(xr[:, t, cut], xr[:, t, cut], gtmp[:, m % 2, :], ALU.add).then_inc(wo_add, 1)

            dve.wait_ge(ssq2, XT)
            rsqrt(stat[:, 32:36], stat[:, 32:36], 1.0 / D)
            for t in range(XT):
                V.tensor_scalar(xn2[:, t], xr[:, t], stat[:, 32 + t:33 + t], None, ALU.mult).then_inc(xn2_done, 1)

            def rank(o, x, n, work):
                g, eqm = (rt[:, work + a * 256:work + a * 256 + n * 16].rearrange("p (n e j) -> p n e j", e=4, j=4) for a in range(2))
                xj = x.unsqueeze(2).broadcast_to([P, n, 4, 4])
                xe = x.unsqueeze(3).broadcast_to([P, n, 4, 4])
                low = tab[:, LOW:LOW + 16].rearrange("p (e j) -> p e j", e=4).unsqueeze(1).broadcast_to([P, n, 4, 4])
                V.tensor_tensor(g, xj, xe, ALU.is_gt)
                link(V.tensor_tensor(eqm, xj, xe, ALU.is_equal))
                link(V.tensor_tensor(eqm, eqm, low, ALU.mult))
                link(V.tensor_tensor(g, g, eqm, ALU.add))
                link(V.tensor_reduce(o, g, AX.X, ALU.add))

            dve.wait_ge(rt_exp, 1)
            sc, bi, sel = rt[:, 0:64], rt[:, 64:128], rt[:, 128:192]
            g16 = lambda a: a.rearrange("p (n e) -> p n e", e=4)
            link(V.tensor_scalar(sc, sc, 1.0, None, ALU.add))
            link(V.reciprocal(sc, sc))
            link(V.tensor_tensor(bi.rearrange("p (t e) -> p t e", t=XT), sc.rearrange("p (t e) -> p t e", t=XT),
                                 rbias[:, :].unsqueeze(1).broadcast_to([P, XT, NE]), ALU.add))
            rank(g16(sel), g16(bi), 16, 512)
            link(V.tensor_scalar(sel, sel, 1.5, None, ALU.is_lt))
            link(V.tensor_tensor(bi, bi, sel, ALU.mult))
            gs, gr = rt[:, 192:208], rt[:, 208:224]
            link(V.tensor_reduce(gs, g16(bi), AX.X, ALU.add))
            rank(g16(gr), g16(gs), 4, 512)
            link(V.tensor_scalar(gr, gr, 0.5, None, ALU.is_lt))
            link(V.tensor_tensor(g16(sel), g16(sel), gr.unsqueeze(2).broadcast_to([P, 16, 4]), ALU.mult))
            link(V.tensor_tensor(sc, sc, sel, ALU.mult))
            link(V.tensor_reduce(rt[:, 224:228], sc.rearrange("p (t e) -> p t e", t=XT), AX.X, ALU.add))
            link(V.reciprocal(rt[:, 228:232], rt[:, 224:228]))
            link(V.tensor_tensor(gate[:, :, :], sc.rearrange("p (t e) -> p t e", t=XT),
                                 rt[:, 228:232].unsqueeze(2).broadcast_to([P, XT, NE]), ALU.mult))
            dve.wait_ge(x2T_mm, KD)
            link(V.memset(acc, 0.0))
            V.sem_inc(a_done, 2)
            V.sem_inc(acc_done, 4)

            with dve.Fori(0, NE // 4) as i:
                for q in range(4):
                    for f in range(2):
                        dve.wait_ge(silu_ready, 8 * i + (2 * q + f + 1))
                        V.tensor_tensor(aT[:, q % 2, f, :], silu[:, f, :], ps[:, 2 + f, :], ALU.mult).then_inc(a_done, 1)
                    for m in range(8):
                        t, half = m // 2, m % 2
                        dve.wait_ge(y_mm, 32 * i + (8 * q + m + 1))
                        a = acc[:, t, half * 512:(half + 1) * 512]
                        V.scalar_tensor_tensor(a, ps[:, 4 + m % 4, :], gate[:, t, bass.ds(4 * i + q, 1)], a, ALU.mult, ALU.add).then_inc(acc_done, 1)

            dve.wait_ge(acc_done, 4 + 8 * NE)
            for t in range(XT):
                link(V.tensor_tensor(acc[:, t], acc[:, t], m5bc, ALU.mult))
                V.tensor_tensor(acc[:, t], acc[:, t], xr[:, t], ALU.add).then_inc(res_ready, 1)

        @block.gpsimd
        def _(pool):
            G = nc.gpsimd
            steps = [0]

            def link(ins):
                steps[0] += 1
                ins.then_inc(pool_step, 1)
                pool.wait_ge(pool_step, steps[0])

            roots = [0]

            def root(o):
                roots[0] += 1
                pool.wait_ge(root_ask, roots[0])
                G.tensor_tensor(o, o, mhalf[:, 0:o.shape[1]], ALU.pow).then_inc(root_done, 1)

            link(G.memset(mhalf[:, :], -0.5))
            link(G.memset(qk[:, XT:NT, 0:4, :], 0.0))
            G.memset(qk[:, XT:NT, 6:10, :], 0.0).then_inc(qk_zero, 1)
            root(stat[:, 0:NT])

            pool.wait_ge(table_in, 16)
            pool.wait_ge(kq_ready, NT)
            pool.wait_ge(qkinT_done, XT)
            pool.wait_ge(pj_done, last_group(4))
            for s in range(2 * NT):
                t = (fw_tiles, bw_tiles)[s % 2][s // 2]
                if s >= 2:
                    pool.wait_ge(kv_done, s - 1)
                G.tensor_tensor(Vexp[:, s % 2], gv[:, t].rearrange("p (h e) -> p h e", h=4).unsqueeze(2).broadcast_to([P, 4, NCH, HD]),
                                tab[:, IND:IND + NCH].unsqueeze(1).unsqueeze(3).broadcast_to([P, 4, NCH, HD]),
                                ALU.mult).then_inc(vexp_ready, 1)

            for t in range(XT):
                root(stat[:, 24:28])

            pool.wait_ge(small_in, 160)
            for t in range(NT):
                root(stat[:, 40:52])
                if t >= XT:
                    continue
                pool.wait_ge(qk_norm, t + 1)
                x1, x2 = qk[:, t, :, 0:32], qk[:, t, :, 32:64]
                co = rope[:, t, 0:1, :].broadcast_to([P, 12, 32])
                si = rope[:, t, 1:2, :].broadcast_to([P, 12, 32])
                G.tensor_tensor(rtmp[:, 0], x1, co, ALU.mult)
                G.tensor_tensor(rtmp[:, 1], x2, si, ALU.mult)
                G.tensor_tensor(rtmp[:, 2], x1, si, ALU.mult)
                link(G.tensor_tensor(rtmp[:, 3], x2, co, ALU.mult))
                G.tensor_tensor(x1, rtmp[:, 0], rtmp[:, 1], ALU.subtract)
                last = G.tensor_tensor(x2, rtmp[:, 2], rtmp[:, 3], ALU.add)
                last.then_inc(rope_done, 1)
                pool.wait_ge(rope_done, t + 1)

            for g in range(8, 32):
                pool.wait_ge(gm_ready, g + 1)
                G.tensor_tensor(merged[:, g % 8, :], merged[:, g % 8, :], gtmp[:, g % 2, :], ALU.add).then_inc(merged_add, 1)
            root(stat[:, 32:36])


_INS = ['x', 'c', 'ctx', 'c_ctx', 'mod_w', 'mod_b', 'norm1_g', 'norm2_g', 'w_in', 'qnorm_a', 'knorm_a', 'qnorm_c',
        'knorm_c', 'sink_c', 'hgrn_lb_logits', 'hgrn_onorm_g', 'w_branch', 'w_out', 'router_w', 'router_b',
        'moe_w1', 'moe_w3', 'moe_w2']


def shape_tables():
    s, t = np.meshgrid(np.arange(P), np.arange(P), indexing="ij")
    same = s // CH == t // CH
    parts = {
        "ident": s == t,
        "tri_fw": same & (s <= t), "tri_bw": same & (s >= t),
        "rem_fw": same & (s > t), "rem_bw": same & (s < t),
        "win_prev": np.where(t >= s, 0.0, NEG), "win_next": np.where(t <= s, 0.0, NEG),
    }
    table = np.zeros((P, TABW), np.float64)
    for i, name in enumerate(TABLE):
        table[:, i * P:(i + 1) * P] = parts[name]
    table[:, IND:IND + NCH] = np.arange(P)[:, None] // CH == np.arange(NCH)[None]
    e, j = np.meshgrid(np.arange(4), np.arange(4), indexing="ij")
    table[:, LOW:LOW + 16] = (j < e).reshape(1, 16)
    a = 2 * np.pi * (np.outer(np.arange(HD), np.arange(HD)) % HD) / HD
    for g in range(2):
        r = slice(g * HD, (g + 1) * HD)
        table[r, DFT + g * HD:DFT + (g + 1) * HD] = np.cos(a)
        table[r, DFT + P + g * HD:DFT + P + (g + 1) * HD] = -np.sin(a)
    b = 2 * np.pi * (np.outer(np.arange(SEQ), np.arange(SEQ)) % SEQ) / SEQ
    norm = (SEQ * HD) ** -0.5
    dft_long = np.stack([np.cos(b), np.sin(b)]) * norm
    pos = np.arange(SEQ)
    freq = (np.float32(10000.0) ** (-np.arange(16, dtype=np.float32) / np.float32(16))).astype(np.float32)
    ang = np.concatenate([(pos // GRID_W).astype(np.float32)[:, None] * freq,
                          (pos % GRID_W).astype(np.float32)[:, None] * freq], axis=1)
    rope = np.concatenate([np.cos(ang), np.sin(ang)], axis=1)
    return {"table": table.astype(np.float32), "dft_long": dft_long.astype(np.float32), "rope": rope.astype(np.float32)}


def kernel(**inputs):
    import concourse.bacc as _bacc
    from concourse.bass_utils import run_bass_kernel_spmd as _run

    nc = _bacc.Bacc("TRN2", target_bir_lowering=False, num_devices=1)
    arrays, args = {}, {}
    for name in _INS:
        arrays[f"in_{name}"] = np.ascontiguousarray(inputs[name])
    for name, a in shape_tables().items():
        arrays[f"in_{name}"] = a
    for key, a in arrays.items():
        args[key[3:]] = nc.dram_tensor(key, a.shape, mybir.dt.from_np(a.dtype), kind="ExternalInput").ap()
    out = nc.dram_tensor("out_0", (1, SEQ, D), F32, kind="ExternalOutput").ap()
    build(nc, args, out)
    r = _run(nc, [arrays], core_ids=[0])
    return r.results[0]["out_0"]
```

```python
from contextlib import ExitStack

import numpy as np

import concourse.bass as bass
from concourse import mybir

ALU = mybir.AluOpType
ACT = mybir.ActivationFunctionType
AX = mybir.AxisListType
F32 = mybir.dt.float32

P = 128
D = 1024
KD = D // P
SEQ, CTX = 512, 256
XT, CT = SEQ // P, CTX // P
NT = XT + CT
HD = 64
BW = 256
NB = 4
CH = 32
NCH = P // CH
NE, NG = 16, 4
FE = 256
GATE0 = 2560
EPS = 1e-6
SCALE = HD ** -0.5
NEG = -1e30
CW = 512
RING = 3
GRID_W = 64

TABLE = ["ident", "tri_fw", "tri_bw", "rem_fw", "rem_bw", "win_prev", "win_next", "before", "ones", "iota"]
IND = len(TABLE) * P
LOW = IND + NCH
DFT = LOW + 16
TOK = DFT + 256
EOFF = TOK + 2 * XT
TABW = EOFF + NE
CAP = P

LOADS = ([("mod", c) for c in range(4)]
         + [("in", 3), ("mod", 4), ("in", 2), ("mod", 5), ("in", 0), ("mod", 6), ("in", 4), ("mod", 7), ("in", 1)]
         + [("mod", 8), ("mod", 9), ("gate", 3, 0), ("mod", 10), ("mod", 11), ("gate", 3, 1), ("gate", 1, 0), ("gate", 1, 1)]
         + [("gate", 0, 0), ("gate", 0, 1), ("gate", 2, 0), ("gate", 2, 1), ("out", 0), ("out", 1)])
N_LOADS = len(LOADS)
GATE_ORDER = [3, 1, 0, 2]


def proj_groups():
    out = []
    for n, load in enumerate(LOADS):
        if load[0] != "in":
            continue
        c = load[1]
        if c == 1:
            out += [(n, c, "feat", ft) for ft in range(2)] + [(n, c, "tok", t) for t in range(XT)]
        else:
            out += [(n, c, "tok", t) for t in [4, 5, 0, 1, 2, 3]]
    return out


def gate_steps():
    return [(b, half, j, LOADS.index(("gate", b, half))) for b in GATE_ORDER for half in range(2) for j in range(4)]


def gate_bank(g):
    if 8 <= g <= 16:
        return 6, 1
    return (0 if g % 2 else 6), 2


def fillers():
    out = []
    for g in range(8, 16):
        out += [(g, 0), None, (g, 1), None]
    return out


def attention_units():
    return [(0, h, t) for h in range(4) for t in range(XT)] + [(2, h, t) for h in range(4) for t in range(XT)]


def unit_keys(br, t):
    if br == 0:
        return list(range(NT)), 0
    return [4, 5] + list(range(max(0, t - 1), min(XT - 1, t + 1) + 1)), 256


def build(nc, A, out):
    ctx = ExitStack()
    with ctx:
        def sb(name, shape):
            return ctx.enter_context(nc.sbuf_tensor(name, shape, F32))

        def sem(name):
            return ctx.enter_context(nc.semaphore(name))

        tab = sb("tab", [P, TABW])
        rope = sb("rope", [P, XT, 2, 32])
        rows = sb("rows", [P, P])
        cols = sb("cols", [P, 80])
        econd = sb("econd", [P, 16])
        cond = sb("cond", [P, KD, 2])
        modc = sb("modc", [P, 48, 2])
        A1 = sb("A1", [P, KD, 2])
        A2 = sb("A2", [P, KD])
        gain4 = sb("gain4", [P, 4, HD])
        gain12 = sb("gain12", [P, 12, HD])
        onorm = sb("onorm", [P, HD])
        sink = sb("sink", [P, 4])
        rbias = sb("rbias", [P, NE])
        rw = sb("rw", [P, KD, NE])
        stat = sb("stat", [P, 64])
        mhalf = sb("mhalf", [P, 12])
        edec = sb("edec", [P, NT, 4, NCH])
        gate = sb("gate", [P, XT, NE])
        slot_of = ctx.enter_context(nc.sbuf_tensor("slot_of", [P, XT, 2], mybir.dt.int32))
        tokb = ctx.enter_context(nc.sbuf_tensor("tokb", [P, 2 * XT], mybir.dt.bfloat16))
        tok_of = ctx.enter_context(nc.sbuf_tensor("tok_of", [P, NE], mybir.dt.int32))
        extra = ctx.enter_context(nc.sbuf_tensor("extra", [P, 1], mybir.dt.int32))
        xd = nc.dram_tensor("xd", (SEQ, D), F32, kind="Internal").ap()
        ye = nc.dram_tensor("ye", (NE * P, D), F32, kind="Internal").ap()

        arena = sb("arena", [P, 49152])

        def region(at, *shape):
            n = int(np.prod(shape))
            v = arena[:, at:at + n]
            if len(shape) == 1:
                return v
            names = "abcd"[:len(shape)]
            return v.rearrange(f"p ({' '.join(names)}) -> p {' '.join(names)}", **dict(zip(names, shape)))

        SLOT = (KD + 2) * CW
        R_RING, R_HT, R_HC, R1 = 0, 15360, 19456, 21504
        R_YT, R_QK, R_V, R_G = 27648, 31744, 36352, 37888
        ring = region(R_RING, RING, KD + 2, CW)
        hT = region(R_HT, KD, SEQ)
        hcT = region(R_HC, KD, CTX)
        xin = region(R1, NT, D)
        yT = region(R_YT, NB, 2, SEQ)
        fuT = yT[:, 1]
        qk = region(R_QK, NT, 12, HD)
        v = region(R_V, NT, BW)
        gf = region(R_G, NT, 512)
        kout = gf
        gv = region(R_G + 3072, NT, BW)
        qinT = region(R_G + 4608, XT, 4, P)
        H = region(R_G + 6656, 4, 18, HD)
        kinT = region(R_HC, XT, 4, P)
        gq = region(R_YT, XT, BW)
        gg = region(R_YT + 2048, XT, BW)
        yG = gg
        hf, hlog, hrem, hcum, hncum = (region(R1 + a * 512, 512) for a in range(5))
        hk = region(R1 + 2560, 2, 512)
        egate = region(R1 + 3584, XT, BW)
        lb, omlb = region(R1 + 4608, 512), region(R1 + 5120, 512)
        Vexp = region(R1, 2, 4, NCH, HD)
        attT = region(R1 + 2048, 2, 2, 2, P)
        osb = region(R1 + 3072, 4, HD)
        osq = region(R1 + 3328, 4, HD)
        mrow = region(R_YT, 4, CW)
        macc = region(R_YT + 3072, 2, CW)
        nsq = region(R_G + 3584, 768)
        rtmp = region(R_G + 4352, 4, 12, 32)
        qT = region(R_G, 4, SEQ)
        kT = region(R_G + 2048, 2, SEQ + CTX)
        Pr = region(R1, 2, 768)
        PT = region(R1 + 1536, 2, 768)
        yA = region(R1 + 3072, XT, BW)
        yC = region(R1 + 4096, XT, BW)
        dftL = region(R1, 2, XT, SEQ)
        gcs = region(R1 + 4096, XT, 512)
        merged = region(R_G + 6656, KD, SEQ)
        th = region(R_HC, 2, SEQ)
        gtmp = region(R_HC + 1024, 2, SEQ)
        m2bc = region(R1, D)
        mcast = region(R1 + 1024, KD, P)
        junk = region(R1 + 4096, D)
        m5bc = region(R1 + 5120, D)
        xr = region(R_QK, XT, D)
        xn2 = region(R_YT, XT, D)
        h2T = hT
        hg = region(R_HT, 2, D)
        hgT = region(R_HT + 2048, KD, P)
        PICKS = 4
        pick = region(R_HT + 3072, PICKS * XT * P // 2).bitcast(mybir.dt.bfloat16).rearrange("p (a t n) -> p a t n", a=PICKS, t=XT)
        ys = region(R_YT, 2, D)
        sl = region(R_YT + 2048, 2 * P)
        aT = region(R_YT + 2304, 2, P)
        a_tok = region(R_YT + 2560, 2 * P)
        yg = region(R_G + 6656, 2, 2, D)
        WE = KD * FE
        at1 = [R_G, 0, SLOT, 2 * SLOT]
        w13 = [region(a, 2, KD, FE) for a in at1]
        w2 = [[region(a, D), region(b, D)] for a, b in
              ((R_G + 2 * WE, R_G + 2 * WE + D), (R1 + 2048, R1 + 3072), (2 * WE, SLOT + 2 * WE), (2 * SLOT + 2 * WE, R_V))]
        rt = region(R_HC, 2048)

        ps = ctx.enter_context(nc.psum_tensor("ps", [P, 8, 512], F32))

        def const(name):
            i = TABLE.index(name) * P
            return tab[:, i:i + P]

        ident = const("ident")

        rows_in, table_in, small_in = sem("rows_in"), sem("table_in"), sem("small_in")
        x_in = [sem(f"x_in{t}") for t in range(NT)]
        ring_in = [sem(f"ring_in{i}") for i in range(RING)]
        ring_used = [sem(f"ring_used{i}") for i in range(RING)]
        mrow_mm, mrow_ready, mrowT = sem("mrow_mm"), sem("mrow_ready"), sem("mrowT")
        macc_ready, macc_mm = sem("macc_ready"), sem("macc_mm")
        dft_in, wb_in, xr_in, out_done = sem("dft_in"), sem("wb_in"), sem("xr_in"), sem("out_done")
        moe_in = [sem(f"moe_in{q}") for q in range(4)]
        rowsT, cols_ready, econd_ready, cond_ready = sem("rowsT"), sem("cols_ready"), sem("econd_ready"), sem("cond_ready")
        a1_ready, ssq_done, xn_done = sem("a1_ready"), sem("ssq_done"), sem("xn_done")
        xT_done, cT_done, hT_x, hT_c = sem("xT_done"), sem("cT_done"), sem("hT_x"), sem("hT_c")
        pj_mm, pj_done, qk_zero = sem("pj_mm"), sem("pj_done"), sem("qk_zero")
        lb_zero, lb_exp, dve_step, act_step, pool_step = sem("lb_zero"), sem("lb_exp"), sem("dve_step"), sem("act_step"), sem("pool_step")
        f_ready, log_ready, cum_done, ex_ready, kq_ready = sem("f_ready"), sem("log_ready"), sem("cum_done"), sem("ex_ready"), sem("kq_ready")
        qkinT_done, qinT_ready, kinT_ready, hgrn1_done = sem("qkinT_done"), sem("qinT_ready"), sem("kinT_ready"), sem("hgrn1_done")
        vexp_ready, kv_done, state_step = sem("vexp_ready"), sem("kv_done"), sem("state_step")
        att_done, attm_ready, o_done, o_read, yG_ready = sem("att_done"), sem("attm_ready"), sem("o_done"), sem("o_read"), sem("yG_ready")
        fgc_done, gcs_ready, yF_done, yF_ready = sem("fgc_done"), sem("gcs_ready"), sem("yF_done"), sem("yF_ready")
        qk_norm, rope_done = sem("qk_norm"), sem("rope_done")
        qkT_mm, qkT_ready = sem("qkT_mm"), sem("qkT_ready")
        sc_done, neg_ready, p_ready, pt_mm, pt_act, pt_dve, pv_done, y_norm = (
            sem("sc_done"), sem("neg_ready"), sem("p_ready"), sem("pt_mm"), sem("pt_act"), sem("pt_dve"), sem("pv_done"), sem("y_norm"))
        yT_mm, yT_ready = sem("yT_mm"), sem("yT_ready")
        silu_q = sem("silu_q")
        gate_mm, th_ready, gm_ready, merged_add = sem("gate_mm"), sem("th_ready"), sem("gm_ready"), sem("merged_add")
        mod_ready, mcast_ready, mbc_mm, mbc_ready = sem("mod_ready"), sem("mcast_ready"), sem("mbc_mm"), sem("mbc_ready")
        wo_mm, wo_add, ssq2, xn2_done, x2T_mm, h2T_ready = (
            sem("wo_mm"), sem("wo_add"), sem("ssq2"), sem("xn2_done"), sem("x2T_mm"), sem("h2T_ready"))
        rt_mm, rt_exp, gate_ready = sem("rt_mm"), sem("rt_exp"), sem("gate_ready")
        xs_done, pos_mm, route_ready, slot_step = sem("xs_done"), sem("pos_mm"), sem("route_ready"), sem("slot_step")
        pick_ready, pick_mm, tok_ready, tok_step = sem("pick_ready"), sem("pick_mm"), sem("tok_ready"), sem("tok_step")
        hg_in = [sem(f"hg_in{i}") for i in range(2)]
        ys_out = [sem(f"ys_out{i}") for i in range(2)]
        yg_in = [sem(f"yg_in{i}") for i in range(2)]
        hg_mm, hgT_act, hgT_dve = sem("hg_mm"), sem("hgT_act"), sem("hgT_dve")
        a_mm, aT_ready, tokb_ready = sem("a_mm"), sem("aT_ready"), sem("tokb_ready")
        h_mm, silu_ready, a_done, y_mm, ys_done = sem("h_mm"), sem("silu_ready"), sem("a_done"), sem("y_mm"), sem("ys_done")
        shift_done = sem("shift_done")
        add_done, gather_go = sem("add_done"), sem("gather_go")
        res_ready, root_ask, root_done = sem("res_ready"), sem("root_ask"), sem("root_done")

        groups = proj_groups()
        units = attention_units()
        NU = len(units)
        order1 = [4, 5, 0, 1, 2, 3]
        fw_tiles, bw_tiles = [4, 5, 0, 1, 2, 3], [5, 4, 3, 2, 1, 0]

        def last_group(chunk):
            return max(g for g, x in enumerate(groups) if x[1] == chunk) + 1

        def ring_value(n):
            return sum(32 if LOADS[m][0] == "gate" else 16 for m in range(n % RING, n + 1, RING))

        def used_value(n):
            return n // RING + 1

        gates = gate_steps()
        fill = fillers()
        N_OUT = LOADS.index(("out", 0))
        mods_late = [n for n, x in enumerate(LOADS) if x[0] == "mod"][4:]

        def mod_acc(m):
            return (macc if m < 6 else gtmp)[:, m % 2, :]

        def extra_rounds(eng, body):
            eng.wait_ge(route_ready, 1)
            n = eng.value_load(extra[0:1, 0:1], min_val=0, max_val=3)
            with eng.If(n > 0):
                with eng.Fori(1, n + 1) as r:
                    body(r)

        def over_experts(eng, body):
            body(0, 0)
            with eng.Fori(0, NE // 4 - 1) as i:
                for o in range(1, 5):
                    body(i, o)
            for o in range(1, 4):
                body(NE // 4 - 1, o)

        def is_last(i, o):
            return isinstance(i, int) and 4 * i + o == NE - 1

        def nth(r, i, o, period=1):
            return (NE // period) * r + (4 // period) * i + (o // period + 1)

        def state_slot(i):
            return i - 7 if i >= 8 else (17 if i % 2 else 0)

        block = ctx.enter_context(nc.Block())

        @block.sync
        def _(sp):
            mw = A["mod_w"][0].rearrange("(k p) c -> p k c", p=P)
            wi = A["w_in"][0].rearrange("(k p) c -> p k c", p=P)
            wo = A["w_out"][0].rearrange("(k p) c -> p k c", p=P)

            def load(n):
                if n >= RING:
                    sp.wait_ge(ring_used[n % RING], used_value(n - RING))
                what, c = LOADS[n][0], LOADS[n][1]
                dst, ready = ring[:, n % RING, 0:KD, :], ring_in[n % RING]
                if what == "gate":
                    half = LOADS[n][2]
                    at = GATE0 + c * D + half * CW
                    sp.dma_start(dst, wi[:, :, at:at + CW]).then_inc(ready, 16)
                    sp.dma_start(ring[:, n % RING, KD:KD + 2, :],
                                 A["w_branch"][0, c].rearrange("(k p) n -> p k n", p=P)[:, :, half * CW:(half + 1) * CW]).then_inc(ready, 16)
                else:
                    src = {"mod": mw, "in": wi, "out": wo}[what]
                    sp.dma_start(dst, src[:, :, c * CW:(c + 1) * CW]).then_inc(ready, 16)

            def rowview(a):
                return a.rearrange("(k p) -> k p", p=P)

            sp.dma_start(rows[0:8, :], rowview(A["c"][0])).then_inc(rows_in, 16)
            sp.dma_start(rows[8:16, :], rowview(A["c_ctx"])).then_inc(rows_in, 16)
            sp.dma_start(rows[16:64, :], rowview(A["mod_b"][0])).then_inc(rows_in, 16)
            sp.dma_start(rows[64:72, :], rowview(A["norm1_g"][0])).then_inc(rows_in, 16)
            sp.dma_start(rows[72:80, :], rowview(A["norm2_g"][0])).then_inc(rows_in, 16)
            sp.dma_start(tab[:, :], A["table"]).then_inc(table_in, 16)
            load(0)
            xs = A["x"][0].rearrange("(t p) d -> t p d", p=P)
            cs = A["ctx"][0].rearrange("(t p) d -> t p d", p=P)
            for t in range(NT):
                sp.dma_start(xin[:, t], xs[t] if t < XT else cs[t - XT]).then_inc(x_in[t], 16)
                if t == 2:
                    load(1)
            load(2)
            sp.dma_start(rope[:, :, :, :], A["rope"].rearrange("(t p) f -> p t f", p=P)
                         .rearrange("p t (a f) -> p t a f", a=2)).then_inc(small_in, 16)
            for i, name in enumerate(["qnorm_a", "knorm_a", "qnorm_c", "knorm_c"]):
                sp.dma_start(gain4[:, i], A[name].partition_broadcast(P).rearrange("q a d -> q (a d)")).then_inc(small_in, 16)
            sp.dma_start(onorm[:, :], A["hgrn_onorm_g"].partition_broadcast(P).rearrange("q a d -> q (a d)")).then_inc(small_in, 16)
            sp.dma_start(sink[:, :], A["sink_c"].partition_broadcast(P).rearrange("q a d -> q (a d)")).then_inc(small_in, 16)
            sp.dma_start(rbias[:, :], A["router_b"].partition_broadcast(P)).then_inc(small_in, 16)
            sp.dma_start(rw[:, :, :], A["router_w"].rearrange("(k p) e -> p k e", p=P)).then_inc(small_in, 16)
            for n in range(3, 6):
                load(n)
            sp.wait_ge(xT_done, KD)
            sp.wait_ge(cT_done, KD)
            sp.dma_start(lb, A["hgrn_lb_logits"].partition_broadcast(P).rearrange("q a b d -> q (a b d)")).then_inc(small_in, 16)
            second_gate = LOADS.index(("gate", 3, 1))
            for n in range(6, second_gate):
                load(n)
            sp.wait_ge(yG_ready, XT)
            sp.dma_start(dftL, A["dft_long"].rearrange("c (s p) t -> p c s t", p=P)).then_inc(dft_in, 16)
            load(second_gate)
            load(second_gate + 1)
            sp.wait_ge(qkT_ready, 7)
            sp.dma_start(xr, A["x"][0].rearrange("(t p) d -> p t d", p=P)).then_inc(xr_in, 16)
            for n in range(second_gate + 2, N_OUT - 2):
                load(n)

            def load_expert(q, e):
                e = bass.ds(e, 1)
                sp.dma_start(w13[q][:, 0], A["moe_w1"][0, e].rearrange("e (k p) f -> p (e k) f", p=P)).then_inc(moe_in[q], 16)
                sp.dma_start(w13[q][:, 1], A["moe_w3"][0, e].rearrange("e (k p) f -> p (e k) f", p=P)).then_inc(moe_in[q], 16)
                for f in range(2):
                    sp.dma_start(w2[q][f], A["moe_w2"][0, e, f * P:(f + 1) * P].rearrange("e p d -> p (e d)")).then_inc(moe_in[q], 16)

            sp.wait_ge(y_norm, NU)
            load_expert(0, 0)
            for n in range(N_OUT - 2, N_LOADS):
                load(n)
            sp.wait_ge(ring_used[(N_OUT - 1) % RING], used_value(N_OUT - 1))
            sp.wait_ge(yT_ready, 6)
            load_expert(1, 1)
            sp.wait_ge(xn2_done, XT)
            sp.dma_start(xd.rearrange("(t p) d -> p t d", p=P), xn2).then_inc(xs_done, 16)
            for n in range(N_OUT, N_LOADS):
                sp.wait_ge(ring_used[n % RING], used_value(n))
            load_expert(2, 2)
            load_expert(3, 3)

            def weights(r, first=0):
                with sp.Fori(first, NE // 4) as i:
                    for q in range(4):
                        sp.wait_ge(y_mm, NE * r + 4 * i + (q - 3))
                        load_expert(q, 4 * i + q)

            weights(0, first=1)
            extra_rounds(sp, weights)
            os = out[0].rearrange("(t p) d -> t p d", p=P)
            for t in range(XT):
                if t == 0:
                    sp.wait_ge(res_ready, 1)
                sp.dma_start(os[t], xr[:, t]).then_inc(out_done, 16)
            sp.wait_ge(out_done, 16 * XT)

        @block.tensor
        def _(pe):
            def mm(o, l, r, start, stop):
                return nc.tensor.matmul(o, l, r, start=start, stop=stop, skip_group_check=True)

            def turn(o, i, n=P):
                return nc.tensor.transpose(o, i, ident[0:n, 0:n])

            pe.wait_ge(table_in, 16)
            pe.wait_ge(rows_in, 80)
            turn(ps[:, 0, 0:80], rows[0:80, :], 80).then_inc(rowsT, 1)

            pe.wait_ge(cond_ready, 1)
            for n in range(4):
                pe.wait_ge(ring_in[n % RING], ring_value(n))
                for k in range(KD):
                    last = mm(ps[0:2, 4 + n, :], cond[:, k, :], ring[:, n % RING, k, :], k == 0, k == KD - 1)
                last.then_inc(mrow_mm, 1)
                pe.wait_ge(mrow_mm, n + 1)
                nc.tensor.sem_inc(ring_used[n % RING], 1)
            for ct in range(16):
                if ct % 4 == 0:
                    pe.wait_ge(mrow_ready, ct // 4 + 1)
                last = turn(ps[:, 1, 2 * ct:2 * ct + 2], mrow[0:2, ct // 4, (ct % 4) * P:(ct % 4 + 1) * P], 2)
            last.then_inc(mrowT, 1)

            def mod_sum(m):
                pe.wait_ge(macc_ready, m + 1)
                for j in range(4):
                    last = mm(ps[:, 5, 4 * m + j:4 * m + j + 1], mod_acc(m)[:, j * P:(j + 1) * P], const("ones")[:, 0:1], True, True)
                last.then_inc(macc_mm, 1)

            for k in range(KD):
                if k == 0:
                    pe.wait_ge(xn_done, NT)
                if k >= 2:
                    pe.wait_ge(hT_x, k - 1)
                for t in range(XT):
                    last = turn(ps[:, 2 + k % 2, t * P:(t + 1) * P], xin[:, t, k * P:(k + 1) * P])
                last.then_inc(xT_done, 1)
                if k >= 2:
                    pe.wait_ge(hT_c, k - 1)
                for t in range(CT):
                    last = turn(ps[:, 4 + k % 2, t * P:(t + 1) * P], xin[:, XT + t, k * P:(k + 1) * P])
                last.then_inc(cT_done, 1)

            def proj(g):
                n, c, kind, t = groups[g]
                slot = n % RING
                pe.wait_ge(ring_in[slot], ring_value(n))
                if g >= 2:
                    pe.wait_ge(pj_done, g - 1)
                bank = 6 + g % 2
                lo, hi = {0: (256, 512), 2: (0, 256), 4: (0, 256)}.get(c, (0, 512)) if t >= XT else {1: (256, 512)}.get(c, (0, 512))
                for k in range(KD):
                    w = ring[:, slot, k, :]
                    if kind == "feat":
                        last = mm(ps[:, bank, :], w[:, t * P:(t + 1) * P], hT[:, k, :], k == 0, k == KD - 1)
                    elif t >= XT:
                        last = mm(ps[:, bank, 0:hi - lo], hcT[:, k, (t - XT) * P:(t - XT + 1) * P], w[:, lo:hi], k == 0, k == KD - 1)
                    else:
                        last = mm(ps[:, bank, 0:hi - lo], hT[:, k, t * P:(t + 1) * P], w[:, lo:hi], k == 0, k == KD - 1)
                last.then_inc(pj_mm, 1)
                if g + 1 == len(groups) or groups[g + 1][0] != n:
                    pe.wait_ge(pj_mm, g + 1)
                    nc.tensor.sem_inc(ring_used[slot], 1)

            def log_sums(i):
                t = order1[i]
                pe.wait_ge(log_ready, i + 1)
                if i >= 1:
                    pe.wait_ge(ex_ready, i)
                mm(ps[:, 0, 0:256], const("rem_fw"), hlog[:, 0:256], True, True)
                mm(ps[:, 0, 256:512], const("rem_bw"), hlog[:, 256:512], True, True)
                if t < XT:
                    mm(ps[:, 1, 0:256], const("tri_fw"), hlog[:, 0:256], True, True)
                    mm(ps[:, 1, 256:512], const("tri_bw"), hlog[:, 256:512], True, True)
                for b in range(4):
                    last = mm(ps[:, 2, b * NCH:(b + 1) * NCH], hlog[:, b * P:(b + 1) * P], tab[:, IND:IND + NCH], True, True)
                last.then_inc(cum_done, 1)

            def turn_qk_in(i):
                t = order1[i]
                if t >= XT:
                    return
                pe.wait_ge(kq_ready, i + 1)
                if t >= 1:
                    pe.wait_ge(qinT_ready, t)
                    pe.wait_ge(kinT_ready, t)
                for b in range(4):
                    turn(ps[:, 3, b * P:(b + 1) * P], hcum[:, b * P:(b + 1) * P])
                for b in range(4):
                    last = turn(ps[:, 4, b * P:(b + 1) * P], hncum[:, b * P:(b + 1) * P])
                last.then_inc(qkinT_done, 1)

            def chunk_kv(pos):
                if pos == 0:
                    pe.wait_ge(qinT_ready, XT)
                    pe.wait_ge(kinT_ready, XT)
                for d in range(2):
                    s = 2 * pos + d
                    t = (fw_tiles, bw_tiles)[d][pos]
                    pe.wait_ge(vexp_ready, s + 1)
                    if pos >= 1:
                        pe.wait_ge(state_step, 16 * pos)
                    for h in range(4):
                        r, pair = (h % 2) * HD, h // 2
                        last = mm(ps[r:r + HD, 3 + d, pair * 256:(pair + 1) * 256],
                                  kout[:, t, d * 256 + h * HD:d * 256 + (h + 1) * HD],
                                  Vexp[:, s % 2, h].rearrange("p j e -> p (j e)"), True, True)
                    last.then_inc(kv_done, 1)

            def chunk_att(t):
                if t >= 1:
                    pe.wait_ge(attm_ready, t)
                for d in range(2):
                    for h in range(4):
                        r, pair = (h % 2) * HD, h // 2
                        at = d * 256 + pair * P
                        last = mm(ps[:, h % 2, at:at + P], kinT[r:r + HD, t, 2 * d + pair, :],
                                  qinT[r:r + HD, t, 2 * d + pair, :], True, True)
                last.then_inc(att_done, 1)

            def chunk_out(t):
                if t == 0:
                    pe.wait_ge(state_step, 16 * (NT - 1) + 12)
                pe.wait_ge(attm_ready, t + 1)
                if t >= 1:
                    pe.wait_ge(o_read, t)
                for h in range(4):
                    par, pair = h % 2, h // 2
                    r = par * HD
                    bank, at = 2 + par, pair * HD
                    vh = gv[:, t, h * HD:(h + 1) * HD]
                    for d in range(2):
                        mm(ps[:, bank, at:at + HD], attT[:, par, d, pair, :], vh, d == 0, False)
                    for d in range(2):
                        for j in range(NCH):
                            slot = 4 * t + j + 1 if d == 0 else 16 - (4 * t + j)
                            last = mm(ps[j * CH:(j + 1) * CH, bank, at:at + HD],
                                      qinT[r:r + HD, t, 2 * d + pair, j * CH:(j + 1) * CH],
                                      H[r:r + HD, 2 * d + pair, slot, :], False, d == 1)
                last.then_inc(o_done, 1)

            def gate_part(g, part):
                b, half, j, n = gates[g]
                bank, flight = gate_bank(g)
                at = j * P
                if part == 0:
                    pe.wait_ge(ring_in[n % RING], ring_value(n))
                    if g >= flight:
                        pe.wait_ge(th_ready, g - flight + 1)
                for k in range(4 * part, 4 * part + 4):
                    last = mm(ps[:, bank, :], ring[:, n % RING, k, at:at + P], hT[:, k, :], k == 0, k == KD - 1)
                if part == 0:
                    return
                if g >= flight:
                    pe.wait_ge(gm_ready, g - flight + 1)
                for k in range(2):
                    last = mm(ps[:, bank + 1, :], ring[:, n % RING, KD + k, at:at + P], yT[:, b, k, :], k == 0, k == 1)
                last.then_inc(gate_mm, 1)
                if j == 3:
                    pe.wait_ge(gate_mm, g + 1)
                    nc.tensor.sem_inc(ring_used[n % RING], 1)

            def gate(g):
                gate_part(g, 0)
                gate_part(g, 1)

            def turn_y(j, bank):
                y, ft = (yG, yA, yC)[j // 2], j % 2
                for t in range(XT):
                    last = turn(ps[:, bank, t * P:(t + 1) * P], y[:, t, ft * P:(ft + 1) * P])
                last.then_inc(yT_mm, 1)

            pe.wait_ge(hT_x, KD)
            pe.wait_ge(hT_c, KD)
            for g in range(18):
                proj(g)
                if g in (9, 13, 17):
                    mod_sum((g - 9) // 4)
            for i in range(NT):
                log_sums(i)
                proj(18 + i)
                turn_qk_in(i)
                if i == 4:
                    mod_sum(3)
            for pos in range(NT):
                proj(24 + pos)
                chunk_kv(pos)
                if pos in (2, 3):
                    mod_sum(pos + 2)
            chunk_att(0)
            for t in range(XT):
                chunk_out(t)
                if t + 1 < XT:
                    chunk_att(t + 1)

            pe.wait_ge(yG_ready, XT)
            for j in range(2):
                turn_y(j, 2 + 2 * j)
            pe.wait_ge(yT_ready, 2)
            for g in range(4):
                gate(g)
            for t in range(XT):
                if t >= 2:
                    pe.wait_ge(gcs_ready, t - 1)
                for ft in range(2):
                    last = mm(ps[:, 2 + 2 * (t % 2), ft * 256:(ft + 1) * 256], fuT[:, ft, t * P:(t + 1) * P],
                              tab[:, DFT:DFT + 256], True, True)
                last.then_inc(fgc_done, 1)
            pe.wait_ge(gcs_ready, XT)
            pe.wait_ge(dft_in, 16)
            for ft in range(2):
                for s in range(XT):
                    for c in range(2):
                        last = mm(ps[:, 2 + 2 * ft, :], gcs[:, s, ft * 256 + c * P:ft * 256 + (c + 1) * P],
                                  dftL[:, c, s, :], s == 0 and c == 0, s == XT - 1 and c == 1)
                last.then_inc(yF_done, 1)
            for g in range(4, 8):
                gate(g)
                if g >= 6:
                    mod_sum(g)

            pe.wait_ge(rope_done, XT)
            pe.wait_ge(qk_norm, NT)
            pe.wait_ge(yF_ready, 2)
            pairs = [0, 2, 6, 8, 4, 10]
            for j in range(7):
                if j >= 2:
                    pe.wait_ge(qkT_ready, j - 1)
                for t in range(XT):
                    if j < 6:
                        src = qk[:, t, pairs[j]:pairs[j] + 2, :]
                    else:
                        src = qk[:, XT + t % 2, pairs[4 + t // 2]:pairs[4 + t // 2] + 2, :]
                    last = turn(ps[:, 2 + j % 2, t * P:(t + 1) * P], src.rearrange("p h e -> p (h e)"))
                last.then_inc(qkT_mm, 1)

            def scores(u):
                br, h, t = units[u]
                par, pair, kk = h // 2, (h % 2) + (2 if br else 0), 1 if br else 0
                r = par * HD
                if u >= 2:
                    pe.wait_ge(pt_act, u - 1)
                    pe.wait_ge(pt_dve, u - 1)
                S = ps[:, 2 * (u % 2):2 * (u % 2) + 2, :].rearrange("p b n -> p (b n)")
                q = qT[r:r + HD, pair, t * P:(t + 1) * P]
                if br == 0:
                    mm(S[:, 0:512], q, kT[r:r + HD, kk, 0:512], True, True)
                    last = mm(S[:, 512:768], q, kT[r:r + HD, kk, 512:768], True, True)
                else:
                    tiles, _ = unit_keys(br, t)
                    mm(S[:, 256:512], q, kT[r:r + HD, kk, 512:768], True, True)
                    for i, kt in enumerate(tiles[2:]):
                        at = 512 + i * P
                        if kt != t:
                            mm(S[:, at:at + P], ident, const("win_prev" if kt < t else "win_next"), True, False)
                        last = mm(S[:, at:at + P], q, kT[r:r + HD, kk, kt * P:(kt + 1) * P], kt == t, True)
                last.then_inc(sc_done, 1)

            def turn_probs(u):
                br, h, t = units[u]
                tiles, _ = unit_keys(br, t)
                pe.wait_ge(p_ready, u + 1)
                for i in range(len(tiles)):
                    last = turn(ps[:, 2 * (u % 2) + i // 4, (i % 4) * P:(i % 4 + 1) * P], Pr[:, u % 2, i * P:(i + 1) * P])
                last.then_inc(pt_mm, 1)

            def probs_v(u):
                br, h, t = units[u]
                tiles, _ = unit_keys(br, t)
                pe.wait_ge(pt_act, u + 1)
                pe.wait_ge(pt_dve, u + 1)
                if u >= 1:
                    pe.wait_ge(y_norm, u)
                at = (P if br else 0) + (h // 2) * HD
                for i, kt in enumerate(tiles):
                    last = mm(ps[:, 4, 0:HD], PT[:, u % 2, i * P:(i + 1) * P], v[:, kt, at:at + HD],
                              i == 0, i == len(tiles) - 1)
                last.then_inc(pv_done, 1)

            pe.wait_ge(qkT_ready, 7)
            pe.wait_ge(th_ready, 8)
            pe.wait_ge(gm_ready, 8)
            scores(0)
            for u in range(NU):
                if u + 1 < NU:
                    scores(u + 1)
                turn_probs(u)
                if u >= 1:
                    probs_v(u - 1)
                if u < len(fill) and fill[u]:
                    gate_part(*fill[u])
            probs_v(NU - 1)

            pe.wait_ge(y_norm, NU)
            for j in range(2, 6):
                if j >= 4:
                    pe.wait_ge(yT_ready, j - 1)
                turn_y(j, 2 + j % 2)
            pe.wait_ge(yT_ready, 6)
            for g in range(16, 32):
                if g in (20, 24):
                    pe.wait_ge(mcast_ready, (g - 20) // 4 + 1)
                    for k in range(KD):
                        last = mm(ps[:, 4 + k // 4, (k % 4) * P:(k % 4 + 1) * P], mcast[:, k, :], ident, True, True)
                    last.then_inc(mbc_mm, 1)
                gate(g)

            pe.wait_ge(merged_add, 24)
            pe.wait_ge(gm_ready, 32)
            for half in range(2):
                n = N_OUT + half
                pe.wait_ge(ring_in[n % RING], ring_value(n))
                for t in range(XT):
                    m = half * XT + t
                    if m >= 2:
                        pe.wait_ge(wo_add, m - 1)
                    for k in range(KD):
                        last = mm(ps[:, m % 2, :], merged[:, k, t * P:(t + 1) * P], ring[:, n % RING, k, :], k == 0, k == KD - 1)
                    last.then_inc(wo_mm, 1)
                pe.wait_ge(wo_mm, XT * (half + 1))
                nc.tensor.sem_inc(ring_used[n % RING], 1)

            pe.wait_ge(xn2_done, XT)
            for k in range(KD):
                if k >= 2:
                    pe.wait_ge(h2T_ready, k - 1)
                for t in range(XT):
                    last = turn(ps[:, 2 + k % 2, t * P:(t + 1) * P], xn2[:, t, k * P:(k + 1) * P])
                last.then_inc(x2T_mm, 1)
            pe.wait_ge(h2T_ready, KD)
            for t in range(XT):
                for k in range(KD):
                    last = mm(ps[:, 4, t * NE:(t + 1) * NE], h2T[:, k, t * P:(t + 1) * P], rw[:, k, :], k == 0, k == KD - 1)
            last.then_inc(rt_mm, 1)

            pe.wait_ge(gate_ready, 1)
            sel = rt[:, 128:192].rearrange("p (t e) -> p t e", t=XT)
            for t in range(XT + 1):
                for s_ in range(min(t, XT - 1) + 1):
                    last = mm(ps[:, 5, t * NE:(t + 1) * NE], const("before") if s_ == t else const("ones"), sel[:, s_, :],
                              s_ == 0, s_ == min(t, XT - 1))
            last.then_inc(pos_mm, 1)

            def experts(r):
                if isinstance(r, int):
                    pe.wait_ge(tokb_ready, 1)
                else:
                    pe.wait_ge(aT_ready, NE * r)
                for e in range(NE):
                    pe.wait_ge(pick_ready, NE * r + (e + 1))
                    for t in range(XT):
                        last = mm(ps[:, 3, 2 * e:2 * e + 2], pick[:, e % PICKS, t, :], tokb[:, 2 * t:2 * t + 2], t == 0, t == XT - 1)
                    last.then_inc(pick_mm, 1)

                def turn_tokens(i, o):
                    pe.wait_ge(hg_in[o % 2], 16 * nth(r, i, o, 2))
                    for k in range(KD):
                        last = turn(ps[:, k // 4, (k % 4) * P:(k % 4 + 1) * P], hg[:, o % 2, k * P:(k + 1) * P])
                    last.then_inc(hg_mm, 1)

                def outputs(i, o):
                    pe.wait_ge(aT_ready, nth(r, i, o))
                    pe.wait_ge(ys_done, nth(r, i, o))
                    for half in range(2):
                        for f in range(2):
                            last = mm(ps[:, 4 + 2 * (o % 2) + half, :], aT[:, f, :], w2[o % 4][f][:, half * 512:(half + 1) * 512],
                                      f == 0, f == 1)
                    last.then_inc(y_mm, 1)

                def step(i, o):
                    pe.wait_ge(moe_in[o % 4], 64 * nth(r, i, o, 4))
                    pe.wait_ge(hgT_act, nth(r, i, o))
                    pe.wait_ge(hgT_dve, nth(r, i, o))
                    for k in range(KD):
                        last = mm(ps[:, 2, :].rearrange("p (w f) -> p w f", w=2), hgT[:, k, :], w13[o % 4][:, :, k, :],
                                  k == 0, k == KD - 1)
                    last.then_inc(h_mm, 1)
                    if not is_last(i, o):
                        turn_tokens(i, o + 1)
                    if o >= 1:
                        outputs(i, o - 1)
                    pe.wait_ge(a_done, nth(r, i, o))
                    for f in range(2):
                        last = turn(ps[:, 3, f * P:(f + 1) * P], a_tok[:, f * P:(f + 1) * P])
                    last.then_inc(a_mm, 1)

                turn_tokens(0, 0)
                over_experts(pe, step)
                outputs(NE // 4 - 1, 3)

            experts(0)
            extra_rounds(pe, experts)

        @block.scalar
        def _(act):
            A_ = nc.scalar.activation

            act.wait_ge(cols_ready, 1)
            A_(econd[:, :], cols[:, 0:16], ACT.Exp, scale=-1.0).then_inc(econd_ready, 1)
            for t in range(NT):
                act.wait_ge(x_in[t], 16)
                A_(gf[:, 0:2, :].rearrange("p a b -> p (a b)"), xin[:, t], ACT.Square,
                   accum_out=stat[:, t:t + 1]).then_inc(ssq_done, 1)
                act.wait_ge(ssq_done, t + 1)
            for n in range(4):
                act.wait_ge(mrow_mm, n + 1)
                A_(mrow[0:2, n, :], ps[0:2, 4 + n, :], ACT.Copy).then_inc(mrow_ready, 1)

            act.wait_ge(a1_ready, 1)
            for k in range(KD):
                act.wait_ge(xT_done, k + 1)
                A_(hT[:, k, :], ps[:, 2 + k % 2, :], ACT.Identity, bias=modc[:, k, 0:1], scale=A1[:, k, 0:1]).then_inc(hT_x, 1)

            act.wait_ge(lb_zero, 1)
            A_(omlb, omlb, ACT.Exp).then_inc(lb_exp, 1)

            def copy(o, i):
                return A_(o, i, ACT.Copy)

            def take(g):
                n, c, kind, t = groups[g]
                act.wait_ge(pj_mm, g + 1)
                B = ps[:, 6 + g % 2, :]
                heads = lambda a, b: B[:, a:b].rearrange("p (h e) -> p h e", e=HD)

                def queries(first):
                    return copy(qk[:, t, first:first + 4, :].rearrange("p (a b) e -> p b a e", a=2),
                                B[:, 0:256].rearrange("p (b a e) -> p b a e", b=2, a=2))

                if c == 3:
                    last = A_(gf[:, t, :], B, ACT.Exp, scale=-1.0)
                elif c == 2:
                    if t < XT:
                        copy(gq[:, t], B[:, 256:512])
                        A_(egate[:, t], B[:, 256:512], ACT.Exp, scale=-1.0)
                    copy(qk[:, t, 10:12, :], heads(0, 128))
                    last = copy(v[:, t, 128:256], B[:, 128:256])
                elif c == 4:
                    if t < XT:
                        copy(gg[:, t], B[:, 256:512])
                        act.wait_ge(silu_q, 1)
                        A_(egate[:, t], B[:, 256:512], ACT.Exp, scale=-1.0)
                    last = copy(gv[:, t], B[:, 0:256])
                elif c == 0:
                    if t < XT:
                        queries(0)
                        copy(qk[:, t, 4:6, :], heads(256, 384))
                        last = copy(v[:, t, 0:128], B[:, 384:512])
                    else:
                        copy(qk[:, t, 4:6, :], heads(0, 128))
                        last = copy(v[:, t, 0:128], B[:, 128:256])
                elif kind == "feat":
                    last = copy(fuT[:, t, :], B)
                else:
                    last = queries(6)
                last.then_inc(pj_done, 1)

            def log_f(i):
                act.wait_ge(f_ready, i + 1)
                if i >= 1:
                    act.wait_ge(cum_done, i)
                A_(hlog, hf, ACT.Ln).then_inc(log_ready, 1)

            def exp_sums(i):
                t = order1[i]
                act.wait_ge(cum_done, i + 1)
                if i >= 1:
                    act.wait_ge(kq_ready, i)
                if t >= 1 and t < XT:
                    act.wait_ge(qkinT_done, t)
                A_(hrem, ps[:, 0, :], ACT.Exp)
                last = A_(edec[:, t].rearrange("p a b -> p (a b)"), ps[:, 2, 0:16], ACT.Exp)
                if t < XT:
                    A_(hcum, ps[:, 1, :], ACT.Exp)
                    last = A_(hncum, ps[:, 1, :], ACT.Exp, scale=-1.0)
                last.then_inc(ex_ready, 1)

            act.wait_ge(qk_zero, 1)
            act.wait_ge(xT_done, KD)
            act.wait_ge(cT_done, KD)
            for g in range(18):
                take(g)
            log_f(0)
            for i, t in enumerate(order1):
                exp_sums(i)
                if i + 1 < NT:
                    log_f(i + 1)
                take(18 + i)
                if t < XT:
                    act.wait_ge(qkinT_done, t + 1)
                    copy(qinT[:, t].rearrange("p a b -> p (a b)"), ps[:, 3, :]).then_inc(qinT_ready, 1)
            for g in range(24, 30):
                take(g)

            def take_y(j, bank):
                act.wait_ge(yT_mm, j + 1)
                copy(yT[:, (3, 0, 2)[j // 2], j % 2, :], ps[:, bank, :]).then_inc(yT_ready, 1)

            def tanh(g):
                act.wait_ge(gate_mm, g + 1)
                if g >= 2:
                    act.wait_ge(gm_ready, g - 1)
                A_(th[:, g % 2, :], ps[:, gate_bank(g)[0], :], ACT.Tanh, scale=0.5).then_inc(th_ready, 1)

            for j in range(2):
                take_y(j, 2 + 2 * j)
            for g in range(4):
                tanh(g)
            for t in range(XT):
                act.wait_ge(fgc_done, t + 1)
                copy(gcs[:, t, :], ps[:, 2 + 2 * (t % 2), :]).then_inc(gcs_ready, 1)
            for ft in range(2):
                act.wait_ge(yF_done, ft + 1)
                copy(yT[:, 1, ft, :], ps[:, 2 + 2 * ft, :]).then_inc(yF_ready, 1)
            for g in range(4, 8):
                tanh(g)

            for j in range(7):
                act.wait_ge(qkT_mm, j + 1)
                B = ps[:, 2 + j % 2, :]
                if j < 4:
                    last = copy(qT[:, j, :], B)
                elif j < 6:
                    last = copy(kT[:, j - 4, 0:512], B)
                else:
                    last = copy(kT[:, :, 512:768], B.rearrange("p (a n) -> p a n", a=2))
                last.then_inc(qkT_ready, 1)

            def pt_copy(u):
                act.wait_ge(pt_mm, u + 1)
                if u >= 2:
                    act.wait_ge(pv_done, u - 1)
                copy(PT[:, u % 2, 0:512], ps[:, 2 * (u % 2), :]).then_inc(pt_act, 1)

            def filler_tanh(u):
                if 0 <= u < len(fill) and fill[u] and fill[u][1] == 1:
                    tanh(fill[u][0])

            for u, (br, h, t) in enumerate(units):
                tiles, lo = unit_keys(br, t)
                w = len(tiles) * P
                S = ps[:, 2 * (u % 2):2 * (u % 2) + 2, :].rearrange("p b n -> p (b n)")
                b3 = 8 + 4 * (u % 4)
                if u >= 1:
                    pt_copy(u - 1)
                act.wait_ge(neg_ready, u + 1)
                if u >= 2:
                    act.wait_ge(pt_mm, u - 1)
                if u >= 4:
                    act.wait_ge(y_norm, u - 3)
                if br:
                    A_(stat[:, b3 + 2:b3 + 3], sink[:, h:h + 1], ACT.Exp, bias=stat[:, b3:b3 + 1])
                A_(Pr[:, u % 2, 0:w], S[:, lo:lo + w], ACT.Exp, bias=stat[:, b3:b3 + 1], scale=SCALE,
                   accum_out=stat[:, b3 + 1:b3 + 2]).then_inc(p_ready, 1)
                filler_tanh(u - 1)
            pt_copy(NU - 1)
            filler_tanh(NU - 1)

            for j in range(2, 6):
                take_y(j, 2 + j % 2)

            for g in range(16, 32):
                tanh(g)
                if g in (20, 24):
                    i = (g - 20) // 4
                    act.wait_ge(mbc_mm, i + 1)
                    copy((m2bc, m5bc)[i], ps[:, 4:6, :].rearrange("p a b -> p (a b)")).then_inc(mbc_ready, 1)

            for t in range(XT):
                act.wait_ge(wo_add, XT + t + 1)
                if t:
                    act.wait_ge(ssq2, t)
                A_(junk, xr[:, t], ACT.Square, accum_out=stat[:, 32 + t:33 + t]).then_inc(ssq2, 1)
            for k in range(KD):
                act.wait_ge(x2T_mm, k + 1)
                A_(h2T[:, k, :], ps[:, 2 + k % 2, :], ACT.Identity, bias=modc[:, 3 * KD + k, 0:1], scale=A2[:, k:k + 1]).then_inc(h2T_ready, 1)
            act.wait_ge(rt_mm, 1)
            A_(rt[:, 0:64], ps[:, 4, 0:64], ACT.Exp, scale=-1.0).then_inc(rt_exp, 1)

            def experts(r):
                if not isinstance(r, int):
                    act.wait_ge(add_done, 2 * XT * r)

                def modulate(i, o):
                    act.wait_ge(hg_mm, nth(r, i, o))
                    for k in range(KD // 2):
                        last = A_(hgT[:, k, :], ps[:, 0, k * P:(k + 1) * P], ACT.Identity,
                                  bias=modc[:, 3 * KD + k, 0:1], scale=A2[:, k:k + 1])
                    last.then_inc(hgT_act, 1)

                def store(i, o):
                    act.wait_ge(ys_done, nth(r, i, o) + 2)
                    act.dma_start(ye[bass.ds(P * (4 * i + o), P), :], ys[:, o % 2]).then_inc(ys_out[o % 2], 16)

                def step(i, o):
                    act.wait_ge(h_mm, nth(r, i, o))
                    A_(sl, ps[:, 2, 0:256], ACT.Silu).then_inc(silu_ready, 1)
                    if not is_last(i, o):
                        modulate(i, o + 1)
                    act.wait_ge(a_mm, nth(r, i, o))
                    copy(aT.rearrange("p f n -> p (f n)"), ps[:, 3, 0:256]).then_inc(aT_ready, 1)
                    if o >= 1:
                        store(i, o - 1)

                modulate(0, 0)
                over_experts(act, step)
                store(NE // 4 - 1, 3)

            experts(0)
            extra_rounds(act, experts)

        @block.vector
        def _(dve):
            V = nc.vector
            steps = [0]

            def link(ins):
                steps[0] += 1
                ins.then_inc(dve_step, 1)
                dve.wait_ge(dve_step, steps[0])

            roots = [0]

            def rsqrt(o, i, inv):
                V.tensor_scalar(o, i, inv, EPS, ALU.mult, ALU.add).then_inc(root_ask, 1)
                roots[0] += 1
                dve.wait_ge(root_done, roots[0])

            dve.wait_ge(rowsT, 1)
            V.tensor_copy(cols[:, :], ps[:, 0, 0:80]).then_inc(cols_ready, 1)
            dve.wait_ge(cols_ready, 1)
            dve.wait_ge(econd_ready, 1)
            link(V.tensor_scalar(econd[:, :], econd[:, :], 1.0, None, ALU.add))
            link(V.reciprocal(econd[:, :], econd[:, :]))
            V.tensor_tensor(cond[:, :, :].rearrange("p k s -> p s k"), econd[:, :].rearrange("p (s k) -> p s k", s=2),
                            cols[:, 0:16].rearrange("p (s k) -> p s k", s=2), ALU.mult).then_inc(cond_ready, 1)

            dve.wait_ge(ssq_done, NT)
            rsqrt(stat[:, 0:NT], stat[:, 0:NT], 1.0 / D)
            for t in range(NT):
                dve.wait_ge(x_in[t], 16)
                V.tensor_scalar(xin[:, t], xin[:, t], stat[:, t:t + 1], None, ALU.mult).then_inc(xn_done, 1)

            dve.wait_ge(mrowT, 1)
            link(V.tensor_tensor(modc[:, 0:16, :], ps[:, 1, 0:32].rearrange("p (c s) -> p c s", s=2),
                                 cols[:, 16:32].unsqueeze(2).broadcast_to([P, 16, 2]), ALU.add))
            V.scalar_tensor_tensor(A1[:, :, :], modc[:, 8:16, :], 1.0, cols[:, 64:72].unsqueeze(2).broadcast_to([P, KD, 2]),
                                   ALU.add, ALU.mult).then_inc(a1_ready, 1)
            dve.wait_ge(a1_ready, 1)
            for k in range(KD):
                dve.wait_ge(cT_done, k + 1)
                V.tensor_scalar(hcT[:, k, :], ps[:, 4 + k % 2, 0:256], A1[:, k, 1:2], modc[:, k, 1:2], ALU.mult, ALU.add).then_inc(hT_c, 1)

            dve.wait_ge(small_in, 160)
            V.tensor_tensor(omlb, lb, lb, ALU.subtract).then_inc(lb_zero, 1)
            for a, b, i in ((0, 4, 0), (4, 6, 1), (6, 10, 2), (10, 12, 3)):
                V.tensor_copy(gain12[:, a:b, :], gain4[:, i:i + 1, :].broadcast_to([P, b - a, HD]))
            dve.wait_ge(lb_exp, 1)
            link(V.reciprocal(lb, omlb))
            link(V.tensor_tensor(omlb, omlb, lb, ALU.mult))
            link(V.tensor_tensor(lb, omlb, omlb, ALU.subtract))
            link(V.tensor_scalar(omlb, lb, -1.0, 1.0, ALU.mult, ALU.add))

            def silu_of(x, e, groups_done):
                dve.wait_ge(pj_done, groups_done)
                link(V.tensor_scalar(e, e, 1.0, None, ALU.add))
                link(V.reciprocal(e, e))
                link(V.tensor_tensor(x, x, e, ALU.mult))

            def mod_partial(m):
                n = mods_late[m]
                slot, acc = n % RING, mod_acc(m)
                dve.wait_ge(ring_in[slot], ring_value(n))
                if m >= 2:
                    dve.wait_ge(macc_mm, m - 1)
                link(V.tensor_scalar(acc, ring[:, slot, 0, :], cond[:, 0, 0:1], None, ALU.mult))
                for k in range(1, KD):
                    last = V.scalar_tensor_tensor(acc, ring[:, slot, k, :], cond[:, k, 0:1], acc, ALU.mult, ALU.add)
                    if k < KD - 1:
                        link(last)
                last.then_inc(macc_ready, 1)
                dve.wait_ge(macc_ready, m + 1)
                V.sem_inc(ring_used[slot], 1)

            mod_partial(0)
            mod_partial(1)
            silu_of(gq, egate, last_group(2))
            V.sem_inc(silu_q, 1)

            def forget(i):
                t = order1[i]
                if i >= 1:
                    dve.wait_ge(log_ready, i)
                link(V.tensor_scalar(hf, gf[:, t, :], 1.0, None, ALU.add))
                link(V.reciprocal(hf, hf))
                link(V.tensor_tensor(hf, hf, omlb, ALU.mult))
                V.tensor_tensor(hf, hf, lb, ALU.add).then_inc(f_ready, 1)
                dve.wait_ge(f_ready, i + 1)
                link(V.tensor_scalar(hk[:, i % 2], hf, -1.0, 1.0, ALU.mult, ALU.add))

            forget(0)
            mod_partial(2)
            for i, t in enumerate(order1):
                if i + 1 < NT:
                    forget(i + 1)
                if i == 3:
                    mod_partial(3)
                dve.wait_ge(ex_ready, i + 1)
                last = V.tensor_tensor(kout[:, t, :], hk[:, i % 2], hrem, ALU.mult)
                if t < XT:
                    V.tensor_tensor(hcum.rearrange("p (d n) -> p d n", d=2), hcum.rearrange("p (d n) -> p d n", d=2),
                                    gq[:, t:t + 1, :].broadcast_to([P, 2, BW]), ALU.mult)
                    last = V.tensor_tensor(hncum, hk[:, i % 2], hncum, ALU.mult)
                last.then_inc(kq_ready, 1)
                if t < XT:
                    dve.wait_ge(qkinT_done, t + 1)
                    V.tensor_copy(kinT[:, t].rearrange("p a b -> p (a b)"), ps[:, 4, :]).then_inc(kinT_ready, 1)
            mod_partial(4)
            mod_partial(5)
            silu_of(gg, egate, last_group(4))

            link(V.memset(H[:, :, 0, :], 0.0))
            n = 0
            for pos in range(NT):
                dve.wait_ge(kv_done, 2 * pos + 2)
                for c in range(NCH):
                    i = pos * NCH + c
                    if i == NT * NCH - 1:
                        break
                    for d in range(2):
                        t = (fw_tiles, bw_tiles)[d][pos]
                        j = c if d == 0 else NCH - 1 - c
                        for pair in range(2):
                            if n >= 4:
                                dve.wait_ge(state_step, n - 3)
                            V.scalar_tensor_tensor(H[:, 2 * d + pair, state_slot(i + 1), :],
                                                   H[:, 2 * d + pair, state_slot(i), :],
                                                   edec[:, t, 2 * d + pair, j:j + 1],
                                                   ps[:, 3 + d, pair * 256 + j * HD:pair * 256 + (j + 1) * HD],
                                                   ALU.mult, ALU.add).then_inc(state_step, 1)
                            n += 1

            for t in range(XT):
                dve.wait_ge(att_done, t + 1)
                for par in range(2):
                    for d in range(2):
                        last = V.tensor_tensor(attT[:, par, d], ps[:, par, d * 256:(d + 1) * 256].rearrange("p (a c) -> p a c", a=2),
                                               const("tri_bw" if d else "tri_fw").unsqueeze(1).broadcast_to([P, 2, P]), ALU.mult)
                last.then_inc(attm_ready, 1)
                dve.wait_ge(o_done, t + 1)
                V.tensor_copy(osb.rearrange("p (a b) e -> p b a e", b=2),
                              ps[:, 2:4, 0:128].rearrange("p b (a e) -> p b a e", a=2)).then_inc(o_read, 1)
                dve.wait_ge(o_read, t + 1)
                link(V.tensor_tensor(osq, osb, osb, ALU.mult))
                link(V.tensor_reduce(stat[:, 24:28], osq, AX.X, ALU.add))
                rsqrt(stat[:, 24:28], stat[:, 24:28], 1.0 / HD)
                link(V.tensor_tensor(osb, osb, stat[:, 24:28].unsqueeze(2).broadcast_to([P, 4, HD]), ALU.mult))
                link(V.tensor_tensor(osb, osb, onorm[:, :].unsqueeze(1).broadcast_to([P, 4, HD]), ALU.mult))
                V.tensor_tensor(yG[:, t], osb.rearrange("p a e -> p (a e)"), gg[:, t], ALU.mult).then_inc(yG_ready, 1)

            def gated(g):
                b, half, j, n = gates[g]
                dve.wait_ge(th_ready, g + 1)
                if g >= 10:
                    dve.wait_ge(merged_add, g - 9)
                V.scalar_tensor_tensor(merged[:, half * 4 + j, :] if g < 8 else gtmp[:, g % 2, :], th[:, g % 2, :], 1.0,
                                       ps[:, gate_bank(g)[0] + 1, :], ALU.add, ALU.mult).then_inc(gm_ready, 1)

            dve.wait_ge(yG_ready, XT)
            for t in range(8):
                if t < NT:
                    X = qk[:, t]
                    sq = nsq.rearrange("p (h e) -> p h e", e=HD)
                    link(V.tensor_tensor(sq, X, X, ALU.mult))
                    link(V.tensor_reduce(stat[:, 40:52], sq, AX.X, ALU.add))
                    rsqrt(stat[:, 40:52], stat[:, 40:52], 1.0 / HD)
                    link(V.tensor_tensor(X, X, stat[:, 40:52].unsqueeze(2).broadcast_to([P, 12, HD]), ALU.mult))
                    V.tensor_tensor(X, X, gain12[:, :, :], ALU.mult).then_inc(qk_norm, 1)
                gated(t)
                if t in (2, 4):
                    mod_partial(5 + t // 2)

            def pt_copy(u):
                br, h, t = units[u]
                w = len(unit_keys(br, t)[0]) * P
                dve.wait_ge(pt_mm, u + 1)
                if u >= 2:
                    dve.wait_ge(pv_done, u - 1)
                if w > 512:
                    V.tensor_copy(PT[:, u % 2, 512:w], ps[:, 2 * (u % 2) + 1, 0:w - 512]).then_inc(pt_dve, 1)
                else:
                    V.sem_inc(pt_dve, 1)

            def normalise(u):
                br, h, t = units[u]
                b3 = 8 + 4 * (u % 4)
                dve.wait_ge(p_ready, u + 1)
                if br:
                    link(V.tensor_tensor(stat[:, b3 + 1:b3 + 2], stat[:, b3 + 1:b3 + 2], stat[:, b3 + 2:b3 + 3], ALU.add))
                link(V.reciprocal(stat[:, b3 + 3:b3 + 4], stat[:, b3 + 1:b3 + 2]))
                dve.wait_ge(pv_done, u + 1)
                V.tensor_scalar((yC if br else yA)[:, t, h * HD:(h + 1) * HD], ps[:, 4, 0:HD],
                                stat[:, b3 + 3:b3 + 4], None, ALU.mult).then_inc(y_norm, 1)

            def filler_gated(u):
                if 0 <= u < len(fill) and fill[u] and fill[u][1] == 1:
                    gated(fill[u][0])

            for u, (br, h, t) in enumerate(units):
                tiles, lo = unit_keys(br, t)
                w = len(tiles) * P
                S = ps[:, 2 * (u % 2):2 * (u % 2) + 2, :].rearrange("p b n -> p (b n)")
                b3 = 8 + 4 * (u % 4)
                dve.wait_ge(sc_done, u + 1)
                link(V.tensor_reduce(stat[:, b3:b3 + 1], S[:, lo:lo + w], AX.X, ALU.max))
                if br:
                    link(V.tensor_scalar(stat[:, b3:b3 + 1], stat[:, b3:b3 + 1], SCALE, sink[:, h:h + 1], ALU.mult, ALU.max))
                    V.tensor_scalar(stat[:, b3:b3 + 1], stat[:, b3:b3 + 1], -1.0, None, ALU.mult).then_inc(neg_ready, 1)
                else:
                    V.tensor_scalar(stat[:, b3:b3 + 1], stat[:, b3:b3 + 1], -SCALE, None, ALU.mult).then_inc(neg_ready, 1)
                if u >= 1:
                    pt_copy(u - 1)
                if u >= 2:
                    normalise(u - 2)
                filler_gated(u - 1)
            pt_copy(NU - 1)
            normalise(NU - 2)
            normalise(NU - 1)
            filler_gated(NU - 1)

            dve.wait_ge(macc_mm, 8)
            link(V.tensor_tensor(modc[:, 16:48, 0:1], ps[:, 5, 0:32].unsqueeze(2), cols[:, 32:64].unsqueeze(2), ALU.add))
            link(V.scalar_tensor_tensor(A2[:, :], modc[:, 32:40, 0], 1.0, cols[:, 72:80], ALU.add, ALU.mult))
            dve.wait_ge(yT_ready, 6)
            V.tensor_scalar(mcast, modc[:, 16:24, 0:1].broadcast_to([P, KD, P]), 0.5, None, ALU.mult).then_inc(mcast_ready, 1)
            for g in range(16, 32):
                if g == 22:
                    dve.wait_ge(mbc_mm, 1)
                    dve.wait_ge(mbc_ready, 1)
                    V.tensor_copy(mcast, modc[:, 40:48, 0:1].broadcast_to([P, KD, P])).then_inc(mcast_ready, 1)
                gated(g)

            dve.wait_ge(xr_in, 16)
            for m in range(2 * XT):
                half, t = m // XT, m % XT
                dve.wait_ge(wo_mm, m + 1)
                cut = slice(half * 512, (half + 1) * 512)
                if m >= 2:
                    dve.wait_ge(wo_add, m - 1)
                link(V.tensor_tensor(gtmp[:, m % 2, :], ps[:, m % 2, :], m2bc[:, cut], ALU.mult))
                V.tensor_tensor(xr[:, t, cut], xr[:, t, cut], gtmp[:, m % 2, :], ALU.add).then_inc(wo_add, 1)

            dve.wait_ge(ssq2, XT)
            rsqrt(stat[:, 32:36], stat[:, 32:36], 1.0 / D)
            for t in range(XT):
                V.tensor_scalar(xn2[:, t], xr[:, t], stat[:, 32 + t:33 + t], None, ALU.mult).then_inc(xn2_done, 1)

            def rank(o, x, n, work):
                g, eqm = (rt[:, work + a * 256:work + a * 256 + n * 16].rearrange("p (n e j) -> p n e j", e=4, j=4) for a in range(2))
                xj = x.unsqueeze(2).broadcast_to([P, n, 4, 4])
                xe = x.unsqueeze(3).broadcast_to([P, n, 4, 4])
                low = tab[:, LOW:LOW + 16].rearrange("p (e j) -> p e j", e=4).unsqueeze(1).broadcast_to([P, n, 4, 4])
                V.tensor_tensor(g, xj, xe, ALU.is_gt)
                link(V.tensor_tensor(eqm, xj, xe, ALU.is_equal))
                link(V.tensor_tensor(eqm, eqm, low, ALU.mult))
                link(V.tensor_tensor(g, g, eqm, ALU.add))
                link(V.tensor_reduce(o, g, AX.X, ALU.add))

            dve.wait_ge(rt_exp, 1)
            sc, bi, sel = rt[:, 0:64], rt[:, 64:128], rt[:, 128:192]
            g16 = lambda a: a.rearrange("p (n e) -> p n e", e=4)
            link(V.tensor_scalar(sc, sc, 1.0, None, ALU.add))
            link(V.reciprocal(sc, sc))
            link(V.tensor_tensor(bi.rearrange("p (t e) -> p t e", t=XT), sc.rearrange("p (t e) -> p t e", t=XT),
                                 rbias[:, :].unsqueeze(1).broadcast_to([P, XT, NE]), ALU.add))
            rank(g16(sel), g16(bi), 16, 512)
            link(V.tensor_scalar(sel, sel, 1.5, None, ALU.is_lt))
            link(V.tensor_tensor(bi, bi, sel, ALU.mult))
            gs, gr = rt[:, 192:208], rt[:, 208:224]
            link(V.tensor_reduce(gs, g16(bi), AX.X, ALU.add))
            rank(g16(gr), g16(gs), 4, 512)
            link(V.tensor_scalar(gr, gr, 0.5, None, ALU.is_lt))
            link(V.tensor_tensor(g16(sel), g16(sel), gr.unsqueeze(2).broadcast_to([P, 16, 4]), ALU.mult))
            link(V.tensor_tensor(sc, sc, sel, ALU.mult))
            link(V.tensor_reduce(rt[:, 224:228], sc.rearrange("p (t e) -> p t e", t=XT), AX.X, ALU.add))
            link(V.reciprocal(rt[:, 228:232], rt[:, 224:228]))
            link(V.tensor_tensor(gate[:, :, :], sc.rearrange("p (t e) -> p t e", t=XT),
                                 rt[:, 228:232].unsqueeze(2).broadcast_to([P, XT, NE]), ALU.mult))
            dve.wait_ge(dve_step, steps[0])
            V.sem_inc(gate_ready, 1)
            tE = lambda a: a.rearrange("p (t e) -> p t e", t=XT)
            over_e = lambda a: a.unsqueeze(2).broadcast_to([P, XT, NE])
            posm, sv, eqm, eqs = rt[:, 256:320], rt[:, 320:384], rt[:, 400:464], rt[:, 480:544]
            hi, nmax = rt[:, 384:388], rt[:, 464:468]
            place, base, wt, cut_, win = (rt[:, 560 + 8 * a:568 + 8 * a].rearrange("p (t c) -> p t c", c=2) for a in range(5))
            dve.wait_ge(pos_mm, 1)
            eoff = tab[:, EOFF:EOFF + NE].unsqueeze(1).broadcast_to([P, XT, NE])
            link(V.tensor_scalar(tE(sv), eoff, 1.0, None, ALU.add))
            link(V.tensor_tensor(sv, sv, sel, ALU.mult))
            link(V.tensor_reduce(hi, tE(sv), AX.X, ALU.max))
            link(V.tensor_tensor(tE(eqm), tE(sv), over_e(hi), ALU.is_equal))
            for to, val in ((place, tE(ps[:, 5, 0:64])), (base, eoff), (wt, gate[:, :, :])):
                link(V.tensor_tensor(tE(eqs), tE(eqm), val, ALU.mult))
                link(V.tensor_reduce(to[:, :, 1], tE(eqs), AX.X, ALU.add))
                link(V.tensor_tensor(tE(eqs), tE(sel), val, ALU.mult))
                link(V.tensor_reduce(to[:, :, 0], tE(eqs), AX.X, ALU.add))
                link(V.tensor_tensor(to[:, :, 0], to[:, :, 0], to[:, :, 1], ALU.subtract))
            link(V.scalar_tensor_tensor(posm, ps[:, 5, 0:64], 1.0, sel, ALU.add, ALU.mult))
            link(V.tensor_scalar(posm, posm, -1.0, None, ALU.add))
            link(V.tensor_reduce(nmax[:, 0:1], ps[:, 5, 64:80], AX.X, ALU.max))
            for m in range(1, 4):
                link(V.tensor_scalar(nmax[:, m:m + 1], nmax[:, 0:1], CAP * m + 0.5, None, ALU.is_gt))
            link(V.tensor_reduce(nmax[:, 0:1], nmax[:, 1:4], AX.X, ALU.add))
            V.tensor_copy(extra[:, :], nmax[:, 0:1]).then_inc(route_ready, 1)
            dve.wait_ge(xs_done, 16)
            V.sem_inc(ys_done, 2)
            V.sem_inc(ys_out[0], 16)
            V.sem_inc(ys_out[1], 16)

            tok_sum = rt[:, 600:604]
            V.tensor_copy(tokb[:, :], tab[:, TOK:TOK + 2 * XT]).then_inc(tokb_ready, 1)

            def experts(r):
                if not isinstance(r, int):
                    for par in range(2):
                        dve.wait_ge(hg_in[par], 16 * (NE // 2 * r))
                    dve.wait_ge(add_done, 2 * XT * r)
                    V.tensor_scalar(posm, posm, -float(CAP), None, ALU.add).then_inc(shift_done, 1)
                    V.tensor_scalar(place, place, -float(CAP), None, ALU.add).then_inc(shift_done, 1)
                    dve.wait_ge(shift_done, 2 * r)
                for e in range(NE):
                    if e >= PICKS or not isinstance(r, int):
                        dve.wait_ge(pick_mm, NE * r + (e + 1 - PICKS))
                    V.tensor_tensor(pick[:, e % PICKS], const("iota").unsqueeze(1).broadcast_to([P, XT, P]),
                                    tE(posm)[:, :, e:e + 1].broadcast_to([P, XT, P]), ALU.is_equal).then_inc(pick_ready, 1)
                    if e % 4 == 3:
                        dve.wait_ge(pick_mm, NE * r + (e + 1))
                        V.tensor_reduce(tok_sum, ps[:, 3, 2 * (e - 3):2 * (e + 1)].rearrange("p (e c) -> p e c", c=2),
                                        AX.X, ALU.add).then_inc(tok_step, 1)
                        dve.wait_ge(tok_step, 4 * r + (e // 4 + 1))
                        V.tensor_copy(tok_of[:, e - 3:e + 1], tok_sum).then_inc(tok_ready, 1)
                        dve.wait_ge(tok_ready, 4 * r + (e // 4 + 1))
                V.tensor_scalar(cut_, place, 0.0, CAP - 1.0, ALU.max, ALU.min).then_inc(slot_step, 1)
                dve.wait_ge(slot_step, 4 * r + 1)
                V.tensor_tensor(win, cut_, place, ALU.is_equal).then_inc(slot_step, 1)
                dve.wait_ge(slot_step, 4 * r + 2)
                V.tensor_tensor(win, win, wt, ALU.mult).then_inc(slot_step, 1)
                V.tensor_tensor(slot_of[:, :, :], cut_, base, ALU.add).then_inc(slot_step, 1)
                def modulate(i, o):
                    dve.wait_ge(hg_mm, nth(r, i, o))
                    for k in range(KD // 2, KD):
                        last = V.tensor_scalar(hgT[:, k, :], ps[:, 1, (k - 4) * P:(k - 3) * P], A2[:, k:k + 1],
                                               modc[:, 3 * KD + k, 0:1], ALU.mult, ALU.add)
                    last.then_inc(hgT_dve, 1)

                def scale_outputs(i, o):
                    dve.wait_ge(y_mm, nth(r, i, o))
                    dve.wait_ge(ys_out[o % 2], 16 * nth(r, i, o, 2))
                    bank = 4 + 2 * (o % 2)
                    V.tensor_tensor(ys[:, o % 2], ps[:, bank:bank + 2, :].rearrange("p b n -> p (b n)"), m5bc,
                                    ALU.mult).then_inc(ys_done, 1)

                def step(i, o):
                    dve.wait_ge(silu_ready, nth(r, i, o))
                    V.tensor_tensor(a_tok, sl, ps[:, 2, 256:512], ALU.mult).then_inc(a_done, 1)
                    if not is_last(i, o):
                        modulate(i, o + 1)
                    if o >= 1:
                        scale_outputs(i, o - 1)

                modulate(0, 0)
                over_experts(dve, step)
                scale_outputs(NE // 4 - 1, 3)

                dve.wait_ge(slot_step, 4 * r + 4)
                for t in range(XT):
                    dve.wait_ge(yg_in[t % 2], 64 * r + 32 * (t // 2 + 1))
                    for c in range(2):
                        V.scalar_tensor_tensor(xr[:, t], yg[:, t % 2, c], win[:, t, c:c + 1], xr[:, t], ALU.mult, ALU.add).then_inc(add_done, 1)
                        dve.wait_ge(add_done, 2 * XT * r + 2 * t + c + 1)

            experts(0)
            extra_rounds(dve, experts)
            V.sem_inc(res_ready, 1)

        @block.gpsimd
        def _(pool):
            G = nc.gpsimd
            steps = [0]

            def link(ins):
                steps[0] += 1
                ins.then_inc(pool_step, 1)
                pool.wait_ge(pool_step, steps[0])

            roots = [0]

            def root(o):
                roots[0] += 1
                pool.wait_ge(root_ask, roots[0])
                G.tensor_tensor(o, o, mhalf[:, 0:o.shape[1]], ALU.pow).then_inc(root_done, 1)

            link(G.memset(mhalf[:, :], -0.5))
            link(G.memset(qk[:, XT:NT, 0:4, :], 0.0))
            G.memset(qk[:, XT:NT, 6:10, :], 0.0).then_inc(qk_zero, 1)
            root(stat[:, 0:NT])

            pool.wait_ge(table_in, 16)
            pool.wait_ge(kq_ready, NT)
            pool.wait_ge(qkinT_done, XT)
            pool.wait_ge(pj_done, last_group(4))
            for s in range(2 * NT):
                t = (fw_tiles, bw_tiles)[s % 2][s // 2]
                if s >= 2:
                    pool.wait_ge(kv_done, s - 1)
                G.tensor_tensor(Vexp[:, s % 2], gv[:, t].rearrange("p (h e) -> p h e", h=4).unsqueeze(2).broadcast_to([P, 4, NCH, HD]),
                                tab[:, IND:IND + NCH].unsqueeze(1).unsqueeze(3).broadcast_to([P, 4, NCH, HD]),
                                ALU.mult).then_inc(vexp_ready, 1)

            for t in range(XT):
                root(stat[:, 24:28])

            pool.wait_ge(small_in, 160)
            for t in range(NT):
                root(stat[:, 40:52])
                if t >= XT:
                    continue
                pool.wait_ge(qk_norm, t + 1)
                x1, x2 = qk[:, t, :, 0:32], qk[:, t, :, 32:64]
                co = rope[:, t, 0:1, :].broadcast_to([P, 12, 32])
                si = rope[:, t, 1:2, :].broadcast_to([P, 12, 32])
                G.tensor_tensor(rtmp[:, 0], x1, co, ALU.mult)
                G.tensor_tensor(rtmp[:, 1], x2, si, ALU.mult)
                G.tensor_tensor(rtmp[:, 2], x1, si, ALU.mult)
                link(G.tensor_tensor(rtmp[:, 3], x2, co, ALU.mult))
                G.tensor_tensor(x1, rtmp[:, 0], rtmp[:, 1], ALU.subtract)
                last = G.tensor_tensor(x2, rtmp[:, 2], rtmp[:, 3], ALU.add)
                last.then_inc(rope_done, 1)
                pool.wait_ge(rope_done, t + 1)

            for g in range(8, 32):
                b, half, j, n = gates[g]
                ft = half * 4 + j
                pool.wait_ge(gm_ready, g + 1)
                G.tensor_tensor(merged[:, ft, :], merged[:, ft, :], gtmp[:, g % 2, :], ALU.add).then_inc(merged_add, 1)
            root(stat[:, 32:36])

            pool.wait_ge(xs_done, 16)

            def experts(r):
                for e in range(NE):
                    pool.wait_ge(tok_ready, 4 * r + (e // 4 + 1))
                    if e >= 2 or not isinstance(r, int):
                        pool.wait_ge(hg_mm, NE * r + (e - 1))
                    G.sem_inc(gather_go, 1)
                    G.indirect_dma_start(hg[:, e % 2], None, xd, bass.IndirectOffsetOnAxis(ap=tok_of[:, e:e + 1], axis=0))\
                        .then_inc(hg_in[e % 2], 16)

                for par in range(2):
                    pool.wait_ge(ys_out[par], 16 * (NE // 2) * r + 16 * (NE // 2 + 1))
                for t in range(XT):
                    if t >= 2 or not isinstance(r, int):
                        pool.wait_ge(add_done, 2 * XT * r + 2 * (t - 1) if t >= 2 else 2 * XT * r)
                    G.sem_inc(gather_go, 1)
                    for c in range(2):
                        G.indirect_dma_start(yg[:, t % 2, c], None, ye, bass.IndirectOffsetOnAxis(ap=slot_of[:, t, c:c + 1], axis=0))\
                            .then_inc(yg_in[t % 2], 16)

            experts(0)
            extra_rounds(pool, experts)


_INS = ['x', 'c', 'ctx', 'c_ctx', 'mod_w', 'mod_b', 'norm1_g', 'norm2_g', 'w_in', 'qnorm_a', 'knorm_a', 'qnorm_c',
        'knorm_c', 'sink_c', 'hgrn_lb_logits', 'hgrn_onorm_g', 'w_branch', 'w_out', 'router_w', 'router_b',
        'moe_w1', 'moe_w3', 'moe_w2']


def shape_tables():
    s, t = np.meshgrid(np.arange(P), np.arange(P), indexing="ij")
    same = s // CH == t // CH
    parts = {
        "ident": s == t,
        "tri_fw": same & (s <= t), "tri_bw": same & (s >= t),
        "rem_fw": same & (s > t), "rem_bw": same & (s < t),
        "before": s < t, "ones": np.ones((P, P)), "iota": t,
        "win_prev": np.where(t >= s, 0.0, NEG), "win_next": np.where(t <= s, 0.0, NEG),
    }
    table = np.zeros((P, TABW), np.float64)
    for i, name in enumerate(TABLE):
        table[:, i * P:(i + 1) * P] = parts[name]
    table[:, IND:IND + NCH] = np.arange(P)[:, None] // CH == np.arange(NCH)[None]
    e, j = np.meshgrid(np.arange(4), np.arange(4), indexing="ij")
    table[:, LOW:LOW + 16] = (j < e).reshape(1, 16)
    table[:, TOK:TOK + 2 * XT:2] = np.arange(P)[:, None]
    table[:, TOK + 1:TOK + 2 * XT:2] = P * np.arange(XT)
    table[:, EOFF:EOFF + NE] = P * np.arange(NE)
    a = 2 * np.pi * (np.outer(np.arange(HD), np.arange(HD)) % HD) / HD
    for g in range(2):
        r = slice(g * HD, (g + 1) * HD)
        table[r, DFT + g * HD:DFT + (g + 1) * HD] = np.cos(a)
        table[r, DFT + P + g * HD:DFT + P + (g + 1) * HD] = -np.sin(a)
    b = 2 * np.pi * (np.outer(np.arange(SEQ), np.arange(SEQ)) % SEQ) / SEQ
    norm = (SEQ * HD) ** -0.5
    dft_long = np.stack([np.cos(b), np.sin(b)]) * norm
    pos = np.arange(SEQ)
    freq = (np.float32(10000.0) ** (-np.arange(16, dtype=np.float32) / np.float32(16))).astype(np.float32)
    ang = np.concatenate([(pos // GRID_W).astype(np.float32)[:, None] * freq,
                          (pos % GRID_W).astype(np.float32)[:, None] * freq], axis=1)
    rope = np.concatenate([np.cos(ang), np.sin(ang)], axis=1)
    return {"table": table.astype(np.float32), "dft_long": dft_long.astype(np.float32), "rope": rope.astype(np.float32)}


def kernel(**inputs):
    import concourse.bacc as _bacc
    from concourse.bass_utils import run_bass_kernel_spmd as _run

    nc = _bacc.Bacc("TRN2", target_bir_lowering=False, num_devices=1)
    arrays, args = {}, {}
    for name in _INS:
        arrays[f"in_{name}"] = np.ascontiguousarray(inputs[name])
    for name, a in shape_tables().items():
        arrays[f"in_{name}"] = a
    for key, a in arrays.items():
        args[key[3:]] = nc.dram_tensor(key, a.shape, mybir.dt.from_np(a.dtype), kind="ExternalInput").ap()
    out = nc.dram_tensor("out_0", (1, SEQ, D), F32, kind="ExternalOutput").ap()
    build(nc, args, out)
    r = _run(nc, [arrays], core_ids=[0])
    return r.results[0]["out_0"]
```

```python
from contextlib import ExitStack

import numpy as np

import concourse.bass as bass
from concourse import mybir

ALU = mybir.AluOpType
ACT = mybir.ActivationFunctionType
AX = mybir.AxisListType
F32 = mybir.dt.float32

P = 128
D = 1024
KD = D // P
SEQ, CTX = 512, 256
XT, CT = SEQ // P, CTX // P
NT = XT + CT
HD = 64
BW = 256
NB = 4
CH = 32
NCH = P // CH
NE, NG = 16, 4
FE = 256
GATE0 = 2560
EPS = 1e-6
SCALE = HD ** -0.5
NEG = -1e30
CW = 512
RING = 3
GRID_W = 64

TABLE = ["ident", "tri_fw", "tri_bw", "rem_fw", "rem_bw", "win_prev", "win_next", "before", "ones", "iota"]
IND = len(TABLE) * P
LOW = IND + NCH
DFT = LOW + 16
TOK = DFT + 256
EOFF = TOK + 2 * XT
TABW = EOFF + NE
CAP = P

LOADS = ([("mod", c) for c in range(4)]
         + [("in", 3), ("mod", 4), ("in", 2), ("mod", 5), ("in", 4), ("mod", 6), ("in", 0), ("mod", 7), ("in", 1)]
         + [("mod", 8), ("mod", 9), ("gate", 3, 0), ("mod", 10), ("mod", 11), ("gate", 3, 1), ("gate", 1, 0), ("gate", 1, 1)]
         + [("gate", 0, 0), ("gate", 0, 1), ("gate", 2, 0), ("gate", 2, 1), ("out", 0), ("out", 1)])
N_LOADS = len(LOADS)
GATE_ORDER = [3, 1, 0, 2]


def proj_groups():
    out = []
    for n, load in enumerate(LOADS):
        if load[0] != "in":
            continue
        c = load[1]
        if c == 1:
            out += [(n, c, "feat", ft) for ft in range(2)] + [(n, c, "tok", t) for t in range(XT)]
        else:
            out += [(n, c, "tok", t) for t in [4, 5, 0, 1, 2, 3]]
    return out


def gate_steps():
    return [(b, half, j, LOADS.index(("gate", b, half))) for b in GATE_ORDER for half in range(2) for j in range(4)]


def gate_bank(g):
    if 8 <= g <= 16:
        return 6, 1
    return (0 if g % 2 else 6), 2


def fillers():
    return 4 * XT * [None] + [(g, part) for g in range(8, 16) for part in range(2)]


def attention_units():
    return [(0, h, t) for h in range(4) for t in range(XT)] + [(2, h, t) for h in range(4) for t in range(XT)]


def unit_keys(br, t):
    if br == 0:
        return list(range(NT)), 0
    return [4, 5] + list(range(max(0, t - 1), min(XT - 1, t + 1) + 1)), 256


def build(nc, A, out):
    ctx = ExitStack()
    with ctx:
        def sb(name, shape):
            return ctx.enter_context(nc.sbuf_tensor(name, shape, F32))

        def sem(name):
            return ctx.enter_context(nc.semaphore(name))

        tab = sb("tab", [P, TABW])
        rope = sb("rope", [P, XT, 2, 32])
        rows = sb("rows", [P, P])
        cols = sb("cols", [P, 80])
        econd = sb("econd", [P, 16])
        cond = sb("cond", [P, KD, 2])
        modc = sb("modc", [P, 48, 2])
        A1 = sb("A1", [P, KD, 2])
        A2 = sb("A2", [P, KD])
        gain4 = sb("gain4", [P, 4, HD])
        gain12 = sb("gain12", [P, 12, HD])
        onorm = sb("onorm", [P, HD])
        sink = sb("sink", [P, 4])
        rbias = sb("rbias", [P, NE])
        rw = sb("rw", [P, KD, NE])
        stat = sb("stat", [P, 64])
        mhalf = sb("mhalf", [P, 12])
        edec = sb("edec", [P, NT, 4, NCH])
        gate = sb("gate", [P, XT, NE])
        slot_of = ctx.enter_context(nc.sbuf_tensor("slot_of", [P, XT, 2], mybir.dt.int32))
        tokb = ctx.enter_context(nc.sbuf_tensor("tokb", [P, 2 * XT], mybir.dt.bfloat16))
        tok_of = ctx.enter_context(nc.sbuf_tensor("tok_of", [P, NE], mybir.dt.int32))
        extra = ctx.enter_context(nc.sbuf_tensor("extra", [P, 1], mybir.dt.int32))
        xd = nc.dram_tensor("xd", (SEQ, D), F32, kind="Internal").ap()
        ye = nc.dram_tensor("ye", (NE * P, D), F32, kind="Internal").ap()

        arena = sb("arena", [P, 49152])

        def region(at, *shape):
            n = int(np.prod(shape))
            v = arena[:, at:at + n]
            if len(shape) == 1:
                return v
            names = "abcd"[:len(shape)]
            return v.rearrange(f"p ({' '.join(names)}) -> p {' '.join(names)}", **dict(zip(names, shape)))

        SLOT = (KD + 2) * CW
        R_RING, R_HT, R_HC, R1 = 0, 15360, 19456, 21504
        R_YT, R_QK, R_V, R_G = 27648, 31744, 36352, 37888
        ring = region(R_RING, RING, KD + 2, CW)
        hT = region(R_HT, KD, SEQ)
        hcT = region(R_HC, KD, CTX)
        xin = region(R1, NT, D)
        yT = region(R_YT, NB, 2, SEQ)
        fuT = yT[:, 1]
        qk = region(R_QK, NT, 12, HD)
        v = region(R_V, NT, BW)
        gf = region(R_G, NT, 512)
        kout = gf
        gv = region(R_G + 3072, NT, BW)
        qinT = region(R_G + 4608, XT, 4, P)
        H = region(R_G + 6656, 4, 18, HD)
        kinT = [region(R_RING + (1 + t // 2) * SLOT + KD * CW + (t % 2) * 4 * P, 4, P) for t in range(XT)]
        gq = region(R_YT, XT, BW)
        gg = region(R_YT + 2048, XT, BW)
        yG = gg
        hf, hlog, hrem, hcum, hncum = (region(R1 + a * 512, 512) for a in range(5))
        hk = region(R1 + 2560, 2, 512)
        egate = region(R1 + 3584, XT, BW)
        lb, omlb = region(R1 + 4608, 512), region(R1 + 5120, 512)
        Vexp = region(R1, 2, 4, NCH, HD)
        attT = region(R1 + 2048, 2, 2, 2, P)
        osb = region(R1 + 3072, 4, HD)
        osq = region(R1 + 3328, 4, HD)
        mrow = region(R_YT, 4, CW)
        macc = region(R_YT + 3072, 2, CW)
        nsq = region(R_G + 3584, 768)
        rtmp = region(R_G + 4352, 4, 12, 32)
        qT = region(R_G, 4, SEQ)
        kT = region(R_G + 2048, 2, SEQ + CTX)
        Pr = region(R1, 2, 768)
        PT = region(R1 + 1536, 2, 768)
        yA = region(R1 + 3072, XT, BW)
        yC = region(R1 + 4096, XT, BW)
        dftL = region(R1, 2, XT, SEQ)
        gcs = region(R1 + 4096, XT, 512)
        merged = region(R_G + 6656, KD, SEQ)
        th = region(R_HC, 2, SEQ)
        gtmp = region(R_HC + 1024, 2, SEQ)
        m2bc = region(R1, D)
        mcast = region(R1 + 1024, KD, P)
        junk = region(R1 + 4096, D)
        m5bc = region(R1 + 5120, D)
        xr = region(R_QK, XT, D)
        xn2 = region(R_YT, XT, D)
        h2T = hT
        hg = region(R_HT, 2, D)
        hgT = region(R_HT + 2048, KD, P)
        PICKS = 4
        pick = region(R_HT + 3072, PICKS * XT * P // 2).bitcast(mybir.dt.bfloat16).rearrange("p (a t n) -> p a t n", a=PICKS, t=XT)
        ys = region(R_YT, 2, D)
        sl = region(R_YT + 2048, 2 * P)
        aT = region(R_YT + 2304, 2, P)
        a_tok = region(R_YT + 2560, 2 * P)
        yg = [region(a, 2, D) for a in (R_G + 6656, R_G + 6656 + 2 * D, R_HT, R1)]
        WE = KD * FE
        at1 = [R_G, 0, SLOT, 2 * SLOT]
        w13 = [region(a, 2, KD, FE) for a in at1]
        w2 = [[region(a, D), region(b, D)] for a, b in
              ((R_G + 2 * WE, R_G + 2 * WE + D), (R1 + 2048, R1 + 3072), (2 * WE, SLOT + 2 * WE), (2 * SLOT + 2 * WE, R_V))]
        rt = region(R_HC, 2048)
        masks = region(R_HC + 1280, P).bitcast(mybir.dt.bfloat16).rearrange("p (a n) -> p a n", a=2)
        selb = region(R_HC + 1408, XT * NE // 2).bitcast(mybir.dt.bfloat16)

        ps = ctx.enter_context(nc.psum_tensor("ps", [P, 8, 512], F32))

        def const(name):
            i = TABLE.index(name) * P
            return tab[:, i:i + P]

        ident = const("ident")

        rows_in, table_in, small_in = sem("rows_in"), sem("table_in"), sem("small_in")
        x_in = [sem(f"x_in{t}") for t in range(NT)]
        ring_in = [sem(f"ring_in{i}") for i in range(RING)]
        ring_used = [sem(f"ring_used{i}") for i in range(RING)]
        mrow_mm, mrow_ready, mrowT = sem("mrow_mm"), sem("mrow_ready"), sem("mrowT")
        macc_ready, macc_mm = sem("macc_ready"), sem("macc_mm")
        dft_in, wb_in, xr_in, out_done = sem("dft_in"), sem("wb_in"), sem("xr_in"), sem("out_done")
        moe_in = [sem(f"moe_in{q}") for q in range(4)]
        rowsT, cols_ready, econd_ready, cond_ready = sem("rowsT"), sem("cols_ready"), sem("econd_ready"), sem("cond_ready")
        a1_ready, ssq_done, xn_done = sem("a1_ready"), sem("ssq_done"), sem("xn_done")
        xT_done, cT_done, hT_x, hT_c = sem("xT_done"), sem("cT_done"), sem("hT_x"), sem("hT_c")
        pj_mm, pj_done, qk_zero = sem("pj_mm"), sem("pj_done"), sem("qk_zero")
        lb_zero, lb_exp, dve_step, act_step, pool_step = sem("lb_zero"), sem("lb_exp"), sem("dve_step"), sem("act_step"), sem("pool_step")
        f_ready, log_ready, cum_done, ex_ready, kq_ready = sem("f_ready"), sem("log_ready"), sem("cum_done"), sem("ex_ready"), sem("kq_ready")
        qkinT_done, qinT_ready, kinT_ready, hgrn1_done = sem("qkinT_done"), sem("qinT_ready"), sem("kinT_ready"), sem("hgrn1_done")
        vexp_ready, kv_done, state_step = sem("vexp_ready"), sem("kv_done"), sem("state_step")
        att_done, attm_ready, o_done, o_read, yG_ready = sem("att_done"), sem("attm_ready"), sem("o_done"), sem("o_read"), sem("yG_ready")
        fgc_done, gcs_ready, yF_done, yF_ready = sem("fgc_done"), sem("gcs_ready"), sem("yF_done"), sem("yF_ready")
        qk_norm, rope_done = sem("qk_norm"), sem("rope_done")
        qkT_mm, qkT_ready = sem("qkT_mm"), sem("qkT_ready")
        sc_done, neg_ready, p_ready, pt_mm, pt_act, pt_dve, pv_done, y_norm = (
            sem("sc_done"), sem("neg_ready"), sem("p_ready"), sem("pt_mm"), sem("pt_act"), sem("pt_dve"), sem("pv_done"), sem("y_norm"))
        yT_mm, yT_ready = sem("yT_mm"), sem("yT_ready")
        silu_q = sem("silu_q")
        gate_mm, th_ready, gm_ready, merged_add = sem("gate_mm"), sem("th_ready"), sem("gm_ready"), sem("merged_add")
        mod_ready, mcast_ready, mbc_mm, mbc_ready = sem("mod_ready"), sem("mcast_ready"), sem("mbc_mm"), sem("mbc_ready")
        wo_mm, wo_add, ssq2, xn2_done, x2T_mm, h2T_act, h2T_dve, masks_ready = (
            sem("wo_mm"), sem("wo_add"), sem("ssq2"), sem("xn2_done"), sem("x2T_mm"), sem("h2T_act"), sem("h2T_dve"), sem("masks_ready"))
        rt_mm, rt_exp, gate_ready = sem("rt_mm"), sem("rt_exp"), sem("gate_ready")
        xs_done, pos_mm, route_ready, slot_step = sem("xs_done"), sem("pos_mm"), sem("route_ready"), sem("slot_step")
        pick_ready, pick_mm, tok_ready, tok_step = sem("pick_ready"), sem("pick_mm"), sem("tok_ready"), sem("tok_step")
        hg_in = [sem(f"hg_in{i}") for i in range(2)]
        ys_out = [sem(f"ys_out{i}") for i in range(2)]
        yg_in = [[sem(f"yg_in{t}_{c}") for c in range(2)] for t in range(XT)]
        hg_mm, hgT_act, hgT_dve = sem("hg_mm"), sem("hgT_act"), sem("hgT_dve")
        a_mm, aT_ready, tokb_ready = sem("a_mm"), sem("aT_ready"), sem("tokb_ready")
        h_mm, silu_ready, a_done, y_mm, ys_done = sem("h_mm"), sem("silu_ready"), sem("a_done"), sem("y_mm"), sem("ys_done")
        shift_done = sem("shift_done")
        add_done, gather_go = sem("add_done"), sem("gather_go")
        root_ask, root_done = sem("root_ask"), sem("root_done")

        groups = proj_groups()
        units = attention_units()
        NU = len(units)
        order1 = [4, 5, 0, 1, 2, 3]
        fw_tiles, bw_tiles = [4, 5, 0, 1, 2, 3], [5, 4, 3, 2, 1, 0]

        def last_group(chunk):
            return max(g for g, x in enumerate(groups) if x[1] == chunk) + 1

        def ring_value(n):
            return sum(32 if LOADS[m][0] == "gate" else 16 for m in range(n % RING, n + 1, RING))

        def used_value(n):
            return n // RING + 1

        gates = gate_steps()
        fill = fillers()
        N_OUT = LOADS.index(("out", 0))
        mods_late = [n for n, x in enumerate(LOADS) if x[0] == "mod"][4:]

        def mod_acc(m):
            return (macc if m < 3 else gtmp)[:, m % 2, :]

        def extra_rounds(eng, body):
            eng.wait_ge(route_ready, 1)
            n = eng.value_load(extra[0:1, 0:1], min_val=0, max_val=3)
            with eng.If(n > 0):
                with eng.Fori(1, n + 1) as r:
                    body(r)

        def over_experts(eng, body):
            body(0, 0)
            with eng.Fori(0, NE // 4 - 1) as i:
                for o in range(1, 5):
                    body(i, o)
            for o in range(1, 4):
                body(NE // 4 - 1, o)

        def is_last(i, o):
            return isinstance(i, int) and 4 * i + o == NE - 1

        def nth(r, i, o, period=1):
            return (NE // period) * r + (4 // period) * i + (o // period + 1)

        def state_slot(i):
            return i - 7 if i >= 8 else (17 if i % 2 else 0)

        block = ctx.enter_context(nc.Block())

        @block.sync
        def _(sp):
            mw = A["mod_w"][0].rearrange("(k p) c -> p k c", p=P)
            wi = A["w_in"][0].rearrange("(k p) c -> p k c", p=P)
            wo = A["w_out"][0].rearrange("(k p) c -> p k c", p=P)

            def load(n):
                if n >= RING:
                    sp.wait_ge(ring_used[n % RING], used_value(n - RING))
                what, c = LOADS[n][0], LOADS[n][1]
                dst, ready = ring[:, n % RING, 0:KD, :], ring_in[n % RING]
                if what == "gate":
                    half = LOADS[n][2]
                    at = GATE0 + c * D + half * CW
                    sp.dma_start(dst, wi[:, :, at:at + CW]).then_inc(ready, 16)
                    sp.dma_start(ring[:, n % RING, KD:KD + 2, :],
                                 A["w_branch"][0, c].rearrange("(k p) n -> p k n", p=P)[:, :, half * CW:(half + 1) * CW]).then_inc(ready, 16)
                else:
                    src = {"mod": mw, "in": wi, "out": wo}[what]
                    sp.dma_start(dst, src[:, :, c * CW:(c + 1) * CW]).then_inc(ready, 16)

            def rowview(a):
                return a.rearrange("(k p) -> k p", p=P)

            sp.dma_start(rows[0:8, :], rowview(A["c"][0])).then_inc(rows_in, 16)
            sp.dma_start(rows[8:16, :], rowview(A["c_ctx"])).then_inc(rows_in, 16)
            sp.dma_start(rows[16:64, :], rowview(A["mod_b"][0])).then_inc(rows_in, 16)
            sp.dma_start(rows[64:72, :], rowview(A["norm1_g"][0])).then_inc(rows_in, 16)
            sp.dma_start(rows[72:80, :], rowview(A["norm2_g"][0])).then_inc(rows_in, 16)
            sp.dma_start(tab[:, 0:P], A["table"][:, 0:P]).then_inc(rows_in, 16)
            for n in range(3):
                load(n)
            sp.dma_start(tab[:, P:], A["table"][:, P:]).then_inc(table_in, 16)
            xs = A["x"][0].rearrange("(t p) d -> t p d", p=P)
            cs = A["ctx"][0].rearrange("(t p) d -> t p d", p=P)
            for t in range(NT):
                sp.dma_start(xin[:, t], xs[t] if t < XT else cs[t - XT]).then_inc(x_in[t], 16)
                if t == 1:
                    load(3)
            sp.dma_start(rope[:, :, :, :], A["rope"].rearrange("(t p) f -> p t f", p=P)
                         .rearrange("p t (a f) -> p t a f", a=2)).then_inc(small_in, 16)
            for i, name in enumerate(["qnorm_a", "knorm_a", "qnorm_c", "knorm_c"]):
                sp.dma_start(gain4[:, i], A[name].partition_broadcast(P).rearrange("q a d -> q (a d)")).then_inc(small_in, 16)
            sp.dma_start(onorm[:, :], A["hgrn_onorm_g"].partition_broadcast(P).rearrange("q a d -> q (a d)")).then_inc(small_in, 16)
            sp.dma_start(sink[:, :], A["sink_c"].partition_broadcast(P).rearrange("q a d -> q (a d)")).then_inc(small_in, 16)
            sp.dma_start(rbias[:, :], A["router_b"].partition_broadcast(P)).then_inc(small_in, 16)
            sp.dma_start(rw[:, :, :], A["router_w"].rearrange("(k p) e -> p k e", p=P)).then_inc(small_in, 16)
            for n in range(4, 6):
                load(n)
            sp.wait_ge(xT_done, KD)
            sp.wait_ge(cT_done, KD)
            sp.dma_start(lb, A["hgrn_lb_logits"].partition_broadcast(P).rearrange("q a b d -> q (a b d)")).then_inc(small_in, 16)
            second_gate = LOADS.index(("gate", 3, 1))
            for n in range(6, second_gate):
                load(n)
            sp.wait_ge(yG_ready, XT)
            sp.dma_start(dftL, A["dft_long"].rearrange("c (s p) t -> p c s t", p=P)).then_inc(dft_in, 16)
            load(second_gate)
            load(second_gate + 1)
            sp.wait_ge(qkT_ready, 7)
            sp.dma_start(xr, A["x"][0].rearrange("(t p) d -> p t d", p=P)).then_inc(xr_in, 16)
            for n in range(second_gate + 2, N_OUT - 2):
                load(n)

            def load_expert(q, e):
                e = bass.ds(e, 1)
                sp.dma_start(w13[q][:, 0], A["moe_w1"][0, e].rearrange("e (k p) f -> p (e k) f", p=P)).then_inc(moe_in[q], 16)
                sp.dma_start(w13[q][:, 1], A["moe_w3"][0, e].rearrange("e (k p) f -> p (e k) f", p=P)).then_inc(moe_in[q], 16)
                for f in range(2):
                    sp.dma_start(w2[q][f], A["moe_w2"][0, e, f * P:(f + 1) * P].rearrange("e p d -> p (e d)")).then_inc(moe_in[q], 16)

            sp.wait_ge(y_norm, NU)
            load_expert(0, 0)
            for n in range(N_OUT - 2, N_LOADS):
                load(n)
            sp.wait_ge(ring_used[(N_OUT - 1) % RING], used_value(N_OUT - 1))
            sp.wait_ge(yT_ready, 6)
            load_expert(1, 1)
            xds = xd.rearrange("(t p) d -> t p d", p=P)
            for t in range(XT):
                if t == XT - 1:
                    for n in range(N_OUT, N_LOADS):
                        sp.wait_ge(ring_used[n % RING], used_value(n))
                    load_expert(2, 2)
                sp.wait_ge(xn2_done, t + 1)
                sp.dma_start(xds[t], xn2[:, t]).then_inc(xs_done, 16)
            sp.wait_ge(hg_in[1], 16)
            load_expert(3, 3)

            def weights(r, first=0):
                with sp.Fori(first, NE // 4) as i:
                    for q in range(4):
                        sp.wait_ge(y_mm, NE * r + 4 * i + (q - 3))
                        load_expert(q, 4 * i + q)

            os = out[0].rearrange("(t p) d -> t p d", p=P)

            def store(r):
                for t in range(XT):
                    sp.wait_ge(add_done, 2 * XT * r + 2 * (t + 1))
                    sp.dma_start(os[t], xr[:, t]).then_inc(out_done, 16)
                sp.wait_ge(out_done, 16 * XT * r + 16 * XT)

            def further(r):
                weights(r)
                store(r)

            weights(0, first=1)
            store(0)
            extra_rounds(sp, further)

        @block.tensor
        def _(pe):
            def mm(o, l, r, start, stop):
                return nc.tensor.matmul(o, l, r, start=start, stop=stop, skip_group_check=True)

            def turn(o, i, n=P):
                return nc.tensor.transpose(o, i, ident[0:n, 0:n])

            pe.wait_ge(rows_in, 96)
            turn(ps[:, 0, 0:80], rows[0:80, :], 80).then_inc(rowsT, 1)

            pe.wait_ge(cond_ready, 1)
            for n in range(4):
                pe.wait_ge(ring_in[n % RING], ring_value(n))
                for k in range(KD):
                    last = mm(ps[0:2, 4 + n, :], cond[:, k, :], ring[:, n % RING, k, :], k == 0, k == KD - 1)
                last.then_inc(mrow_mm, 1)
                pe.wait_ge(mrow_mm, n + 1)
                nc.tensor.sem_inc(ring_used[n % RING], 1)
            for ct in range(16):
                if ct % 4 == 0:
                    pe.wait_ge(mrow_ready, ct // 4 + 1)
                last = turn(ps[:, 1, 2 * ct:2 * ct + 2], mrow[0:2, ct // 4, (ct % 4) * P:(ct % 4 + 1) * P], 2)
            last.then_inc(mrowT, 1)

            def mod_sum(m):
                pe.wait_ge(macc_ready, m + 1)
                for j in range(4):
                    last = mm(ps[:, 5, 4 * m + j:4 * m + j + 1], mod_acc(m)[:, j * P:(j + 1) * P], const("ones")[:, 0:1], True, True)
                last.then_inc(macc_mm, 1)

            for k in range(KD):
                if k == 0:
                    pe.wait_ge(xn_done, NT)
                if k >= 2:
                    pe.wait_ge(hT_x, k - 1)
                for t in range(XT):
                    last = turn(ps[:, 2 + k % 2, t * P:(t + 1) * P], xin[:, t, k * P:(k + 1) * P])
                last.then_inc(xT_done, 1)
                if k >= 2:
                    pe.wait_ge(hT_c, k - 1)
                for t in range(CT):
                    last = turn(ps[:, 4 + k % 2, t * P:(t + 1) * P], xin[:, XT + t, k * P:(k + 1) * P])
                last.then_inc(cT_done, 1)

            def proj(g):
                n, c, kind, t = groups[g]
                slot = n % RING
                pe.wait_ge(ring_in[slot], ring_value(n))
                if g >= 2:
                    pe.wait_ge(pj_done, g - 1)
                bank = 6 + g % 2
                lo, hi = {0: (256, 512), 2: (0, 256), 4: (0, 256)}.get(c, (0, 512)) if t >= XT else {1: (256, 512)}.get(c, (0, 512))
                for k in range(KD):
                    w = ring[:, slot, k, :]
                    if kind == "feat":
                        last = mm(ps[:, bank, :], w[:, t * P:(t + 1) * P], hT[:, k, :], k == 0, k == KD - 1)
                    elif t >= XT:
                        last = mm(ps[:, bank, 0:hi - lo], hcT[:, k, (t - XT) * P:(t - XT + 1) * P], w[:, lo:hi], k == 0, k == KD - 1)
                    else:
                        last = mm(ps[:, bank, 0:hi - lo], hT[:, k, t * P:(t + 1) * P], w[:, lo:hi], k == 0, k == KD - 1)
                last.then_inc(pj_mm, 1)
                if g + 1 == len(groups) or groups[g + 1][0] != n:
                    pe.wait_ge(pj_mm, g + 1)
                    nc.tensor.sem_inc(ring_used[slot], 1)

            def log_sums(i):
                t = order1[i]
                pe.wait_ge(log_ready, i + 1)
                if i >= 1:
                    pe.wait_ge(ex_ready, i)
                mm(ps[:, 0, 0:256], const("rem_fw"), hlog[:, 0:256], True, True)
                mm(ps[:, 0, 256:512], const("rem_bw"), hlog[:, 256:512], True, True)
                if t < XT:
                    mm(ps[:, 1, 0:256], const("tri_fw"), hlog[:, 0:256], True, True)
                    mm(ps[:, 1, 256:512], const("tri_bw"), hlog[:, 256:512], True, True)
                for b in range(4):
                    last = mm(ps[:, 2, b * NCH:(b + 1) * NCH], hlog[:, b * P:(b + 1) * P], tab[:, IND:IND + NCH], True, True)
                last.then_inc(cum_done, 1)

            def turn_qk_in(i):
                t = order1[i]
                if t >= XT:
                    return
                pe.wait_ge(kq_ready, i + 1)
                if t >= 1:
                    pe.wait_ge(qinT_ready, t)
                    pe.wait_ge(kinT_ready, t)
                for b in range(4):
                    turn(ps[:, 3, b * P:(b + 1) * P], hcum[:, b * P:(b + 1) * P])
                for b in range(4):
                    last = turn(ps[:, 4, b * P:(b + 1) * P], hncum[:, b * P:(b + 1) * P])
                last.then_inc(qkinT_done, 1)

            def chunk_kv(pos):
                if pos == 0:
                    pe.wait_ge(qinT_ready, XT)
                    pe.wait_ge(kinT_ready, XT)
                for d in range(2):
                    s = 2 * pos + d
                    t = (fw_tiles, bw_tiles)[d][pos]
                    pe.wait_ge(vexp_ready, s + 1)
                    if pos >= 1:
                        pe.wait_ge(state_step, 16 * pos)
                    for h in range(4):
                        r, pair = (h % 2) * HD, h // 2
                        last = mm(ps[r:r + HD, 3 + d, pair * 256:(pair + 1) * 256],
                                  kout[:, t, d * 256 + h * HD:d * 256 + (h + 1) * HD],
                                  Vexp[:, s % 2, h].rearrange("p j e -> p (j e)"), True, True)
                    last.then_inc(kv_done, 1)

            def chunk_att(t):
                if t >= 1:
                    pe.wait_ge(attm_ready, t)
                for d in range(2):
                    for h in range(4):
                        r, pair = (h % 2) * HD, h // 2
                        at = d * 256 + pair * P
                        last = mm(ps[:, h % 2, at:at + P], kinT[t][r:r + HD, 2 * d + pair, :],
                                  qinT[r:r + HD, t, 2 * d + pair, :], True, True)
                last.then_inc(att_done, 1)

            def chunk_out(t):
                if t == 0:
                    pe.wait_ge(state_step, 16 * (NT - 1) + 12)
                pe.wait_ge(attm_ready, t + 1)
                if t >= 1:
                    pe.wait_ge(o_read, t)
                for h in range(4):
                    par, pair = h % 2, h // 2
                    r = par * HD
                    bank, at = 2 + par, pair * HD
                    vh = gv[:, t, h * HD:(h + 1) * HD]
                    for d in range(2):
                        mm(ps[:, bank, at:at + HD], attT[:, par, d, pair, :], vh, d == 0, False)
                    for d in range(2):
                        for j in range(NCH):
                            slot = 4 * t + j + 1 if d == 0 else 16 - (4 * t + j)
                            last = mm(ps[j * CH:(j + 1) * CH, bank, at:at + HD],
                                      qinT[r:r + HD, t, 2 * d + pair, j * CH:(j + 1) * CH],
                                      H[r:r + HD, 2 * d + pair, slot, :], False, d == 1)
                last.then_inc(o_done, 1)

            def gate_part(g, part):
                b, half, j, n = gates[g]
                bank, flight = gate_bank(g)
                at = j * P
                if part == 0:
                    pe.wait_ge(ring_in[n % RING], ring_value(n))
                    if g >= flight:
                        pe.wait_ge(th_ready, g - flight + 1)
                for k in range(4 * part, 4 * part + 4):
                    last = mm(ps[:, bank, :], ring[:, n % RING, k, at:at + P], hT[:, k, :], k == 0, k == KD - 1)
                if part == 0:
                    return
                if g >= flight:
                    pe.wait_ge(gm_ready, g - flight + 1)
                for k in range(2):
                    last = mm(ps[:, bank + 1, :], ring[:, n % RING, KD + k, at:at + P], yT[:, b, k, :], k == 0, k == 1)
                last.then_inc(gate_mm, 1)
                if j == 3:
                    pe.wait_ge(gate_mm, g + 1)
                    nc.tensor.sem_inc(ring_used[n % RING], 1)

            def gate(g):
                gate_part(g, 0)
                gate_part(g, 1)

            def turn_y(j, bank):
                y, ft = (yG, yA, yC)[j // 2], j % 2
                for t in range(XT):
                    last = turn(ps[:, bank, t * P:(t + 1) * P], y[:, t, ft * P:(ft + 1) * P])
                last.then_inc(yT_mm, 1)

            pe.wait_ge(hT_x, KD)
            pe.wait_ge(hT_c, KD)
            pe.wait_ge(table_in, 16)
            for g in range(12):
                proj(g)
                if g == 9:
                    mod_sum(0)
            for i in range(NT):
                log_sums(i)
                proj(12 + i)
                turn_qk_in(i)
                if i in (0, 4):
                    mod_sum(1 + i // 4)
            for pos in range(NT):
                proj(18 + pos)
                chunk_kv(pos)
            chunk_att(0)
            for t in range(XT):
                if t < 3:
                    proj(24 + 2 * t)
                    proj(25 + 2 * t)
                chunk_out(t)
                if t + 1 < XT:
                    chunk_att(t + 1)
                if t < 3:
                    mod_sum(3 + t)

            pe.wait_ge(pj_done, len(groups))
            gate_part(0, 0)
            pe.wait_ge(yG_ready, XT)
            for j in range(2):
                turn_y(j, 2 + 2 * j)
            pe.wait_ge(yT_ready, 2)
            gate_part(0, 1)
            for g in range(1, 4):
                gate(g)
            for t in range(XT):
                if t >= 2:
                    pe.wait_ge(gcs_ready, t - 1)
                for ft in range(2):
                    last = mm(ps[:, 2 + 2 * (t % 2), ft * 256:(ft + 1) * 256], fuT[:, ft, t * P:(t + 1) * P],
                              tab[:, DFT:DFT + 256], True, True)
                last.then_inc(fgc_done, 1)
            pe.wait_ge(gcs_ready, XT)
            pe.wait_ge(dft_in, 16)
            for ft in range(2):
                for s in range(XT):
                    for c in range(2):
                        last = mm(ps[:, 2 + 2 * ft, :], gcs[:, s, ft * 256 + c * P:ft * 256 + (c + 1) * P],
                                  dftL[:, c, s, :], s == 0 and c == 0, s == XT - 1 and c == 1)
                last.then_inc(yF_done, 1)
            for g in range(4, 8):
                gate(g)
                if g in (5, 7):
                    mod_sum(6 + g // 7)

            pe.wait_ge(rope_done, XT)
            pe.wait_ge(qk_norm, NT)
            pe.wait_ge(yF_ready, 2)
            pairs = [0, 2, 6, 8, 4, 10]
            for j in range(7):
                if j >= 2:
                    pe.wait_ge(qkT_ready, j - 1)
                for t in range(XT):
                    if j < 6:
                        src = qk[:, t, pairs[j]:pairs[j] + 2, :]
                    else:
                        src = qk[:, XT + t % 2, pairs[4 + t // 2]:pairs[4 + t // 2] + 2, :]
                    last = turn(ps[:, 2 + j % 2, t * P:(t + 1) * P], src.rearrange("p h e -> p (h e)"))
                last.then_inc(qkT_mm, 1)

            def scores(u):
                br, h, t = units[u]
                par, pair, kk = h // 2, (h % 2) + (2 if br else 0), 1 if br else 0
                r = par * HD
                if u >= 2:
                    pe.wait_ge(pt_act, u - 1)
                    pe.wait_ge(pt_dve, u - 1)
                S = ps[:, 2 * (u % 2):2 * (u % 2) + 2, :].rearrange("p b n -> p (b n)")
                q = qT[r:r + HD, pair, t * P:(t + 1) * P]
                if br == 0:
                    mm(S[:, 0:512], q, kT[r:r + HD, kk, 0:512], True, True)
                    last = mm(S[:, 512:768], q, kT[r:r + HD, kk, 512:768], True, True)
                else:
                    tiles, _ = unit_keys(br, t)
                    mm(S[:, 256:512], q, kT[r:r + HD, kk, 512:768], True, True)
                    for i, kt in enumerate(tiles[2:]):
                        at = 512 + i * P
                        last = mm(S[:, at:at + P], q, kT[r:r + HD, kk, kt * P:(kt + 1) * P], True, True)
                last.then_inc(sc_done, 1)

            def turn_probs(u):
                br, h, t = units[u]
                tiles, _ = unit_keys(br, t)
                pe.wait_ge(p_ready, u + 1)
                for i in range(len(tiles)):
                    last = turn(ps[:, 2 * (u % 2) + i // 4, (i % 4) * P:(i % 4 + 1) * P], Pr[:, u % 2, i * P:(i + 1) * P])
                last.then_inc(pt_mm, 1)

            def probs_v(u):
                br, h, t = units[u]
                tiles, _ = unit_keys(br, t)
                pe.wait_ge(pt_act, u + 1)
                pe.wait_ge(pt_dve, u + 1)
                if u >= 1:
                    pe.wait_ge(y_norm, u)
                at = (P if br else 0) + (h // 2) * HD
                for i, kt in enumerate(tiles):
                    last = mm(ps[:, 4, 0:HD], PT[:, u % 2, i * P:(i + 1) * P], v[:, kt, at:at + HD],
                              i == 0, i == len(tiles) - 1)
                last.then_inc(pv_done, 1)

            pe.wait_ge(qkT_ready, 7)
            pe.wait_ge(th_ready, 8)
            pe.wait_ge(gm_ready, 8)
            scores(0)
            for u in range(NU):
                if u + 1 < NU:
                    scores(u + 1)
                turn_probs(u)
                if u >= 1:
                    probs_v(u - 1)
                if u < len(fill) and fill[u]:
                    gate_part(*fill[u])
            probs_v(NU - 1)

            pe.wait_ge(y_norm, NU)
            for j in range(2, 6):
                if j >= 4:
                    pe.wait_ge(yT_ready, j - 1)
                turn_y(j, 2 + j % 2)
            pe.wait_ge(yT_ready, 6)
            for g in range(16, 32):
                if g in (20, 24):
                    pe.wait_ge(mcast_ready, (g - 20) // 4 + 1)
                    for k in range(KD):
                        last = mm(ps[:, 4 + k // 4, (k % 4) * P:(k % 4 + 1) * P], mcast[:, k, :], ident, True, True)
                    last.then_inc(mbc_mm, 1)
                gate(g)

            def w_out(t):
                for half in range(2):
                    n, m = N_OUT + half, 2 * t + half
                    pe.wait_ge(ring_in[n % RING], ring_value(n))
                    if m >= 2:
                        pe.wait_ge(wo_add, m - 1)
                    for k in range(KD):
                        if m == 0:
                            pe.wait_ge(merged_add, 17 + k)
                        last = mm(ps[:, 2 + m % 2, :], merged[:, k, t * P:(t + 1) * P], ring[:, n % RING, k, :], k == 0, k == KD - 1)
                    last.then_inc(wo_mm, 1)

            def turn_x2(t):
                pe.wait_ge(xn2_done, t + 1)
                if t >= 2:
                    pe.wait_ge(h2T_act, t - 1)
                    pe.wait_ge(h2T_dve, t - 1)
                for k in range(KD):
                    last = turn(ps[:, (0, 6)[t % 2] + k // 4, (k % 4) * P:(k % 4 + 1) * P], xn2[:, t, k * P:(k + 1) * P])
                last.then_inc(x2T_mm, 1)

            def router(t):
                pe.wait_ge(h2T_act, t + 1)
                pe.wait_ge(h2T_dve, t + 1)
                for k in range(KD):
                    last = mm(ps[:, 4, t * NE:(t + 1) * NE], h2T[:, k, t * P:(t + 1) * P], rw[:, k, :], k == 0, k == KD - 1)
                last.then_inc(rt_mm, 1)

            w_out(0)
            w_out(1)
            turn_x2(0)
            w_out(2)
            router(0)
            turn_x2(1)
            w_out(3)
            pe.wait_ge(wo_mm, 2 * XT)
            for n in range(N_OUT, N_LOADS):
                nc.tensor.sem_inc(ring_used[n % RING], 1)
            router(1)
            turn_x2(2)
            turn_x2(3)
            router(2)
            router(3)

            pe.wait_ge(gate_ready, 1)
            pe.wait_ge(masks_ready, 1)
            sel = selb.rearrange("p (t e) -> p t e", t=XT)
            for t in range(XT + 1):
                for s_ in range(min(t, XT - 1) + 1):
                    last = mm(ps[:, 5, t * NE:(t + 1) * NE], masks[:, 0 if s_ == t else 1, :], sel[:, s_, :],
                              s_ == 0, s_ == min(t, XT - 1))
            last.then_inc(pos_mm, 1)

            def experts(r):
                if isinstance(r, int):
                    pe.wait_ge(tokb_ready, 1)
                else:
                    pe.wait_ge(aT_ready, NE * r)

                def picks(first, count):
                    for e in range(first, first + count):
                        f = e // 4
                        if e % 4 == 0 and f >= 2:
                            pe.wait_ge(tok_ready, 4 * r + (f - 1))
                        pe.wait_ge(pick_ready, NE * r + (e + 1))
                        for t in range(XT):
                            last = mm(ps[:, 3 + 4 * (f % 2), 2 * e:2 * e + 2], pick[:, e % PICKS, t, :], tokb[:, 2 * t:2 * t + 2], t == 0, t == XT - 1)
                        last.then_inc(pick_mm, 1)

                def turn_tokens(i, o):
                    pe.wait_ge(hg_in[o % 2], 16 * nth(r, i, o, 2))
                    for k in range(KD):
                        last = turn(ps[:, k // 4, (k % 4) * P:(k % 4 + 1) * P], hg[:, o % 2, k * P:(k + 1) * P])
                    last.then_inc(hg_mm, 1)

                def outputs(i, o):
                    pe.wait_ge(aT_ready, nth(r, i, o))
                    pe.wait_ge(ys_done, nth(r, i, o))
                    for half in range(2):
                        for f in range(2):
                            last = mm(ps[:, 4 + 2 * (o % 2) + half, :], aT[:, f, :], w2[o % 4][f][:, half * 512:(half + 1) * 512],
                                      f == 0, f == 1)
                    last.then_inc(y_mm, 1)

                def step(i, o):
                    pe.wait_ge(moe_in[o % 4], 64 * nth(r, i, o, 4))
                    pe.wait_ge(hgT_act, nth(r, i, o))
                    pe.wait_ge(hgT_dve, nth(r, i, o))
                    for k in range(KD):
                        last = mm(ps[:, 2, :].rearrange("p (w f) -> p w f", w=2), hgT[:, k, :], w13[o % 4][:, :, k, :],
                                  k == 0, k == KD - 1)
                    last.then_inc(h_mm, 1)
                    if o == 0:
                        picks(12, 4)
                    if not is_last(i, o):
                        turn_tokens(i, o + 1)
                    if o >= 1:
                        outputs(i, o - 1)
                    pe.wait_ge(a_done, nth(r, i, o))
                    if o == 0:
                        pe.wait_ge(tok_ready, 4 * r + 4)
                    for f in range(2):
                        last = turn(ps[:, 3, f * P:(f + 1) * P], a_tok[:, f * P:(f + 1) * P])
                    last.then_inc(a_mm, 1)

                picks(0, 8)
                turn_tokens(0, 0)
                picks(8, 4)
                over_experts(pe, step)
                outputs(NE // 4 - 1, 3)

            experts(0)
            extra_rounds(pe, experts)

        @block.scalar
        def _(act):
            A_ = nc.scalar.activation

            act.wait_ge(cols_ready, 1)
            A_(econd[:, :], cols[:, 0:16], ACT.Exp, scale=-1.0).then_inc(econd_ready, 1)
            for t in range(NT):
                act.wait_ge(x_in[t], 16)
                A_(gf[:, 0:2, :].rearrange("p a b -> p (a b)"), xin[:, t], ACT.Square,
                   accum_out=stat[:, t:t + 1]).then_inc(ssq_done, 1)
                act.wait_ge(ssq_done, t + 1)
            for n in range(4):
                act.wait_ge(mrow_mm, n + 1)
                A_(mrow[0:2, n, :], ps[0:2, 4 + n, :], ACT.Copy).then_inc(mrow_ready, 1)

            act.wait_ge(a1_ready, 1)
            for k in range(KD):
                act.wait_ge(xT_done, k + 1)
                A_(hT[:, k, :], ps[:, 2 + k % 2, :], ACT.Identity, bias=modc[:, k, 0:1], scale=A1[:, k, 0:1]).then_inc(hT_x, 1)

            act.wait_ge(lb_zero, 1)
            A_(omlb, omlb, ACT.Exp).then_inc(lb_exp, 1)

            def copy(o, i):
                return A_(o, i, ACT.Copy)

            def take(g):
                n, c, kind, t = groups[g]
                act.wait_ge(pj_mm, g + 1)
                B = ps[:, 6 + g % 2, :]
                heads = lambda a, b: B[:, a:b].rearrange("p (h e) -> p h e", e=HD)

                def queries(first):
                    return copy(qk[:, t, first:first + 4, :].rearrange("p (a b) e -> p b a e", a=2),
                                B[:, 0:256].rearrange("p (b a e) -> p b a e", b=2, a=2))

                if c == 3:
                    last = A_(gf[:, t, :], B, ACT.Exp, scale=-1.0)
                elif c == 2:
                    if t < XT:
                        copy(gq[:, t], B[:, 256:512])
                        A_(egate[:, t], B[:, 256:512], ACT.Exp, scale=-1.0)
                    copy(qk[:, t, 10:12, :], heads(0, 128))
                    last = copy(v[:, t, 128:256], B[:, 128:256])
                elif c == 4:
                    if t < XT:
                        copy(gg[:, t], B[:, 256:512])
                        act.wait_ge(silu_q, 1)
                        A_(egate[:, t], B[:, 256:512], ACT.Exp, scale=-1.0)
                    last = copy(gv[:, t], B[:, 0:256])
                elif c == 0:
                    if t < XT:
                        queries(0)
                        copy(qk[:, t, 4:6, :], heads(256, 384))
                        last = copy(v[:, t, 0:128], B[:, 384:512])
                    else:
                        copy(qk[:, t, 4:6, :], heads(0, 128))
                        last = copy(v[:, t, 0:128], B[:, 128:256])
                elif kind == "feat":
                    last = copy(fuT[:, t, :], B)
                else:
                    last = queries(6)
                last.then_inc(pj_done, 1)

            def log_f(i):
                act.wait_ge(f_ready, i + 1)
                if i >= 1:
                    act.wait_ge(cum_done, i)
                A_(hlog, hf, ACT.Ln).then_inc(log_ready, 1)

            def exp_sums(i):
                t = order1[i]
                act.wait_ge(cum_done, i + 1)
                if i >= 1:
                    act.wait_ge(kq_ready, i)
                if t >= 1 and t < XT:
                    act.wait_ge(qkinT_done, t)
                A_(hrem, ps[:, 0, :], ACT.Exp)
                last = A_(edec[:, t].rearrange("p a b -> p (a b)"), ps[:, 2, 0:16], ACT.Exp)
                if t < XT:
                    A_(hcum, ps[:, 1, :], ACT.Exp)
                    last = A_(hncum, ps[:, 1, :], ACT.Exp, scale=-1.0)
                last.then_inc(ex_ready, 1)

            act.wait_ge(qk_zero, 1)
            act.wait_ge(xT_done, KD)
            act.wait_ge(cT_done, KD)
            for g in range(12):
                take(g)
                if g == 9:
                    log_f(0)
            for i, t in enumerate(order1):
                exp_sums(i)
                if i + 1 < NT:
                    log_f(i + 1)
                take(12 + i)
                if t < XT:
                    act.wait_ge(qkinT_done, t + 1)
                    copy(qinT[:, t].rearrange("p a b -> p (a b)"), ps[:, 3, :]).then_inc(qinT_ready, 1)
            for g in range(18, 30):
                take(g)

            def take_y(j, bank):
                act.wait_ge(yT_mm, j + 1)
                copy(yT[:, (3, 0, 2)[j // 2], j % 2, :], ps[:, bank, :]).then_inc(yT_ready, 1)

            def tanh(g):
                act.wait_ge(gate_mm, g + 1)
                if g >= 2:
                    act.wait_ge(gm_ready, g - 1)
                A_(th[:, g % 2, :], ps[:, gate_bank(g)[0], :], ACT.Tanh, scale=0.5).then_inc(th_ready, 1)

            for j in range(2):
                take_y(j, 2 + 2 * j)
            for g in range(4):
                tanh(g)
            for t in range(XT):
                act.wait_ge(fgc_done, t + 1)
                copy(gcs[:, t, :], ps[:, 2 + 2 * (t % 2), :]).then_inc(gcs_ready, 1)
            for ft in range(2):
                act.wait_ge(yF_done, ft + 1)
                copy(yT[:, 1, ft, :], ps[:, 2 + 2 * ft, :]).then_inc(yF_ready, 1)
            for g in range(4, 8):
                tanh(g)

            for j in range(7):
                act.wait_ge(qkT_mm, j + 1)
                B = ps[:, 2 + j % 2, :]
                if j < 4:
                    last = copy(qT[:, j, :], B)
                elif j < 6:
                    last = copy(kT[:, j - 4, 0:512], B)
                else:
                    last = copy(kT[:, :, 512:768], B.rearrange("p (a n) -> p a n", a=2))
                last.then_inc(qkT_ready, 1)

            def pt_copy(u):
                act.wait_ge(pt_mm, u + 1)
                if u >= 2:
                    act.wait_ge(pv_done, u - 1)
                copy(PT[:, u % 2, 0:512], ps[:, 2 * (u % 2), :]).then_inc(pt_act, 1)

            def filler_tanh(u):
                if 0 <= u < len(fill) and fill[u] and fill[u][1] == 1:
                    tanh(fill[u][0])

            for u, (br, h, t) in enumerate(units):
                tiles, lo = unit_keys(br, t)
                w = len(tiles) * P
                S = ps[:, 2 * (u % 2):2 * (u % 2) + 2, :].rearrange("p b n -> p (b n)")
                b3 = 8 + 4 * (u % 4)
                if u >= 1:
                    pt_copy(u - 1)
                act.wait_ge(neg_ready, u + 1)
                if u >= 2:
                    act.wait_ge(pt_mm, u - 1)
                if u >= 4:
                    act.wait_ge(y_norm, u - 3)
                if br:
                    A_(stat[:, b3 + 2:b3 + 3], sink[:, h:h + 1], ACT.Exp, bias=stat[:, b3:b3 + 1])
                A_(Pr[:, u % 2, 0:w], S[:, lo:lo + w], ACT.Exp, bias=stat[:, b3:b3 + 1], scale=SCALE,
                   accum_out=stat[:, b3 + 1:b3 + 2]).then_inc(p_ready, 1)
                filler_tanh(u - 1)
            pt_copy(NU - 1)
            filler_tanh(NU - 1)

            for j in range(2, 6):
                take_y(j, 2 + j % 2)

            for g in range(16, 32):
                tanh(g)
                if g in (20, 24):
                    i = (g - 20) // 4
                    act.wait_ge(mbc_mm, i + 1)
                    copy((m2bc, m5bc)[i], ps[:, 4:6, :].rearrange("p a b -> p (a b)")).then_inc(mbc_ready, 1)

            def modulate_x2(t):
                act.wait_ge(x2T_mm, t + 1)
                for k in range(KD // 2):
                    last = A_(h2T[:, k, t * P:(t + 1) * P], ps[:, (0, 6)[t % 2], k * P:(k + 1) * P], ACT.Identity,
                              bias=modc[:, 3 * KD + k, 0:1], scale=A2[:, k:k + 1])
                last.then_inc(h2T_act, 1)

            for t in range(XT):
                act.wait_ge(wo_add, 2 * t + 2)
                if t:
                    act.wait_ge(ssq2, t)
                A_(junk, xr[:, t], ACT.Square, accum_out=stat[:, 32 + t:33 + t]).then_inc(ssq2, 1)
                if t:
                    modulate_x2(t - 1)
            modulate_x2(XT - 1)
            act.wait_ge(rt_mm, XT)
            A_(rt[:, 0:64], ps[:, 4, 0:64], ACT.Exp, scale=-1.0).then_inc(rt_exp, 1)

            def experts(r):
                if not isinstance(r, int):
                    act.wait_ge(add_done, 2 * XT * r)

                def modulate(i, o):
                    act.wait_ge(hg_mm, nth(r, i, o))
                    for k in range(KD // 2):
                        last = A_(hgT[:, k, :], ps[:, 0, k * P:(k + 1) * P], ACT.Identity,
                                  bias=modc[:, 3 * KD + k, 0:1], scale=A2[:, k:k + 1])
                    last.then_inc(hgT_act, 1)

                def store(i, o):
                    act.wait_ge(ys_done, nth(r, i, o) + 2)
                    act.dma_start(ye[bass.ds(P * (4 * i + o), P), :], ys[:, o % 2]).then_inc(ys_out[o % 2], 16)

                def step(i, o):
                    act.wait_ge(h_mm, nth(r, i, o))
                    A_(sl, ps[:, 2, 0:256], ACT.Silu).then_inc(silu_ready, 1)
                    if not is_last(i, o):
                        modulate(i, o + 1)
                    act.wait_ge(a_mm, nth(r, i, o))
                    copy(aT.rearrange("p f n -> p (f n)"), ps[:, 3, 0:256]).then_inc(aT_ready, 1)
                    if o >= 1:
                        store(i, o - 1)

                modulate(0, 0)
                over_experts(act, step)
                store(NE // 4 - 1, 3)

            experts(0)
            extra_rounds(act, experts)

        @block.vector
        def _(dve):
            V = nc.vector
            steps = [0]

            def link(ins):
                steps[0] += 1
                ins.then_inc(dve_step, 1)
                dve.wait_ge(dve_step, steps[0])

            roots = [0]

            def rsqrt(o, i, inv):
                V.tensor_scalar(o, i, inv, EPS, ALU.mult, ALU.add).then_inc(root_ask, 1)
                roots[0] += 1
                dve.wait_ge(root_done, roots[0])

            dve.wait_ge(rowsT, 1)
            V.tensor_copy(cols[:, :], ps[:, 0, 0:80]).then_inc(cols_ready, 1)
            dve.wait_ge(cols_ready, 1)
            dve.wait_ge(econd_ready, 1)
            link(V.tensor_scalar(econd[:, :], econd[:, :], 1.0, None, ALU.add))
            link(V.reciprocal(econd[:, :], econd[:, :]))
            V.tensor_tensor(cond[:, :, :].rearrange("p k s -> p s k"), econd[:, :].rearrange("p (s k) -> p s k", s=2),
                            cols[:, 0:16].rearrange("p (s k) -> p s k", s=2), ALU.mult).then_inc(cond_ready, 1)

            for t in range(NT):
                if t % 2 == 0:
                    dve.wait_ge(ssq_done, t + 2)
                    rsqrt(stat[:, t:t + 2], stat[:, t:t + 2], 1.0 / D)
                V.tensor_scalar(xin[:, t], xin[:, t], stat[:, t:t + 1], None, ALU.mult).then_inc(xn_done, 1)

            dve.wait_ge(mrowT, 1)
            link(V.tensor_tensor(modc[:, 0:16, :], ps[:, 1, 0:32].rearrange("p (c s) -> p c s", s=2),
                                 cols[:, 16:32].unsqueeze(2).broadcast_to([P, 16, 2]), ALU.add))
            V.scalar_tensor_tensor(A1[:, :, :], modc[:, 8:16, :], 1.0, cols[:, 64:72].unsqueeze(2).broadcast_to([P, KD, 2]),
                                   ALU.add, ALU.mult).then_inc(a1_ready, 1)
            dve.wait_ge(a1_ready, 1)
            for k in range(KD):
                dve.wait_ge(cT_done, k + 1)
                V.tensor_scalar(hcT[:, k, :], ps[:, 4 + k % 2, 0:256], A1[:, k, 1:2], modc[:, k, 1:2], ALU.mult, ALU.add).then_inc(hT_c, 1)

            dve.wait_ge(small_in, 160)
            V.tensor_tensor(omlb, lb, lb, ALU.subtract).then_inc(lb_zero, 1)
            for a, b, i in ((0, 4, 0), (4, 6, 1), (6, 10, 2), (10, 12, 3)):
                V.tensor_copy(gain12[:, a:b, :], gain4[:, i:i + 1, :].broadcast_to([P, b - a, HD]))
            dve.wait_ge(lb_exp, 1)
            link(V.reciprocal(lb, omlb))
            link(V.tensor_tensor(omlb, omlb, lb, ALU.mult))
            link(V.tensor_tensor(lb, omlb, omlb, ALU.subtract))
            link(V.tensor_scalar(omlb, lb, -1.0, 1.0, ALU.mult, ALU.add))

            def sigmoid(e):
                link(V.tensor_scalar(e, e, 1.0, None, ALU.add))
                link(V.reciprocal(e, e))

            for i, t in enumerate(order1):
                dve.wait_ge(pj_done, i + 1)
                sigmoid(gf[:, t, :])

            def silu_of(x, t, group):
                dve.wait_ge(pj_done, group + 1)
                sigmoid(egate[:, t])
                link(V.tensor_tensor(x[:, t], x[:, t], egate[:, t], ALU.mult))

            def forget(i):
                t = order1[i]
                if i >= 1:
                    dve.wait_ge(log_ready, i)
                link(V.tensor_tensor(hf, gf[:, t, :], omlb, ALU.mult))
                V.tensor_tensor(hf, hf, lb, ALU.add).then_inc(f_ready, 1)
                dve.wait_ge(f_ready, i + 1)
                link(V.tensor_scalar(hk[:, i % 2], hf, -1.0, 1.0, ALU.mult, ALU.add))

            forget(0)
            for t in range(XT):
                silu_of(gq, t, 8 + t)
            V.sem_inc(silu_q, 1)
            for i, t in enumerate(order1):
                if i + 1 < NT:
                    forget(i + 1)
                dve.wait_ge(ex_ready, i + 1)
                last = V.tensor_tensor(kout[:, t, :], hk[:, i % 2], hrem, ALU.mult)
                if t < XT:
                    V.tensor_tensor(hcum.rearrange("p (d n) -> p d n", d=2), hcum.rearrange("p (d n) -> p d n", d=2),
                                    gq[:, t:t + 1, :].broadcast_to([P, 2, BW]), ALU.mult)
                    last = V.tensor_tensor(hncum, hk[:, i % 2], hncum, ALU.mult)
                last.then_inc(kq_ready, 1)
                if t < XT:
                    dve.wait_ge(qkinT_done, t + 1)
                    V.tensor_copy(kinT[t].rearrange("p a b -> p (a b)"), ps[:, 4, :]).then_inc(kinT_ready, 1)
                    if t:
                        silu_of(gg, t - 1, 12 + i - 1)
            silu_of(gg, XT - 1, 17)

            link(V.memset(H[:, :, 0, :], 0.0))
            n = 0
            for pos in range(NT):
                dve.wait_ge(kv_done, 2 * pos + 2)
                for c in range(NCH):
                    i = pos * NCH + c
                    if i == NT * NCH - 1:
                        break
                    for d in range(2):
                        t = (fw_tiles, bw_tiles)[d][pos]
                        j = c if d == 0 else NCH - 1 - c
                        for pair in range(2):
                            if n >= 4:
                                dve.wait_ge(state_step, n - 3)
                            V.scalar_tensor_tensor(H[:, 2 * d + pair, state_slot(i + 1), :],
                                                   H[:, 2 * d + pair, state_slot(i), :],
                                                   edec[:, t, 2 * d + pair, j:j + 1],
                                                   ps[:, 3 + d, pair * 256 + j * HD:pair * 256 + (j + 1) * HD],
                                                   ALU.mult, ALU.add).then_inc(state_step, 1)
                            n += 1

            def mod_partial(m):
                n = mods_late[m]
                slot, acc = n % RING, mod_acc(m)
                dve.wait_ge(ring_in[slot], ring_value(n))
                dve.wait_ge(macc_mm, m - 1)
                link(V.tensor_scalar(acc, ring[:, slot, 0, :], cond[:, 0, 0:1], None, ALU.mult))
                for k in range(1, KD):
                    last = V.scalar_tensor_tensor(acc, ring[:, slot, k, :], cond[:, k, 0:1], acc, ALU.mult, ALU.add)
                    if k < KD - 1:
                        link(last)
                last.then_inc(macc_ready, 1)
                dve.wait_ge(macc_ready, m + 1)
                V.sem_inc(ring_used[slot], 1)

            dve.wait_ge(pj_done, 20)
            for t in range(XT):
                dve.wait_ge(att_done, t + 1)
                for par in range(2):
                    for d in range(2):
                        last = V.tensor_tensor(attT[:, par, d], ps[:, par, d * 256:(d + 1) * 256].rearrange("p (a c) -> p a c", a=2),
                                               const("tri_bw" if d else "tri_fw").unsqueeze(1).broadcast_to([P, 2, P]), ALU.mult)
                last.then_inc(attm_ready, 1)
                if t < 3:
                    mod_partial(3 + t)
                dve.wait_ge(o_done, t + 1)
                V.tensor_copy(osb.rearrange("p (a b) e -> p b a e", b=2),
                              ps[:, 2:4, 0:128].rearrange("p b (a e) -> p b a e", a=2)).then_inc(o_read, 1)
                dve.wait_ge(o_read, t + 1)
                link(V.tensor_tensor(osq, osb, osb, ALU.mult))
                link(V.tensor_reduce(stat[:, 24:28], osq, AX.X, ALU.add))
                rsqrt(stat[:, 24:28], stat[:, 24:28], 1.0 / HD)
                link(V.tensor_tensor(osb, osb, stat[:, 24:28].unsqueeze(2).broadcast_to([P, 4, HD]), ALU.mult))
                link(V.tensor_tensor(osb, osb, onorm[:, :].unsqueeze(1).broadcast_to([P, 4, HD]), ALU.mult))
                V.tensor_tensor(yG[:, t], osb.rearrange("p a e -> p (a e)"), gg[:, t], ALU.mult).then_inc(yG_ready, 1)

            def gated(g):
                b, half, j, n = gates[g]
                dve.wait_ge(th_ready, g + 1)
                if g >= 10:
                    dve.wait_ge(merged_add, g - 9)
                V.scalar_tensor_tensor(merged[:, half * 4 + j, :] if g < 8 else gtmp[:, g % 2, :], th[:, g % 2, :], 1.0,
                                       ps[:, gate_bank(g)[0] + 1, :], ALU.add, ALU.mult).then_inc(gm_ready, 1)

            dve.wait_ge(yG_ready, XT)
            for t in range(8):
                if t < NT:
                    X = qk[:, t]
                    sq = nsq.rearrange("p (h e) -> p h e", e=HD)
                    link(V.tensor_tensor(sq, X, X, ALU.mult))
                    link(V.tensor_reduce(stat[:, 40:52], sq, AX.X, ALU.add))
                    rsqrt(stat[:, 40:52], stat[:, 40:52], 1.0 / HD)
                    link(V.tensor_tensor(X, X, stat[:, 40:52].unsqueeze(2).broadcast_to([P, 12, HD]), ALU.mult))
                    V.tensor_tensor(X, X, gain12[:, :, :], ALU.mult).then_inc(qk_norm, 1)
                gated(t)
                if t in (2, 4):
                    mod_partial(5 + t // 2)

            def pt_copy(u):
                br, h, t = units[u]
                w = len(unit_keys(br, t)[0]) * P
                dve.wait_ge(pt_mm, u + 1)
                if u >= 2:
                    dve.wait_ge(pv_done, u - 1)
                if w > 512:
                    V.tensor_copy(PT[:, u % 2, 512:w], ps[:, 2 * (u % 2) + 1, 0:w - 512]).then_inc(pt_dve, 1)
                else:
                    V.sem_inc(pt_dve, 1)

            def normalise(u):
                br, h, t = units[u]
                b3 = 8 + 4 * (u % 4)
                dve.wait_ge(p_ready, u + 1)
                if br:
                    link(V.tensor_tensor(stat[:, b3 + 1:b3 + 2], stat[:, b3 + 1:b3 + 2], stat[:, b3 + 2:b3 + 3], ALU.add))
                link(V.reciprocal(stat[:, b3 + 3:b3 + 4], stat[:, b3 + 1:b3 + 2]))
                dve.wait_ge(pv_done, u + 1)
                V.tensor_scalar((yC if br else yA)[:, t, h * HD:(h + 1) * HD], ps[:, 4, 0:HD],
                                stat[:, b3 + 3:b3 + 4], None, ALU.mult).then_inc(y_norm, 1)

            def filler_gated(u):
                if 0 <= u < len(fill) and fill[u] and fill[u][1] == 1:
                    gated(fill[u][0])

            for u, (br, h, t) in enumerate(units):
                tiles, lo = unit_keys(br, t)
                w = len(tiles) * P
                S = ps[:, 2 * (u % 2):2 * (u % 2) + 2, :].rearrange("p b n -> p (b n)")
                b3 = 8 + 4 * (u % 4)
                dve.wait_ge(sc_done, u + 1)
                for i, kt in enumerate(tiles[2:] if br else []):
                    if kt != t:
                        block = S[:, 512 + i * P:512 + (i + 1) * P]
                        link(V.tensor_tensor(block, block, const("win_prev" if kt < t else "win_next"), ALU.add))
                link(V.tensor_reduce(stat[:, b3:b3 + 1], S[:, lo:lo + w], AX.X, ALU.max))
                if br:
                    link(V.tensor_scalar(stat[:, b3:b3 + 1], stat[:, b3:b3 + 1], SCALE, sink[:, h:h + 1], ALU.mult, ALU.max))
                    V.tensor_scalar(stat[:, b3:b3 + 1], stat[:, b3:b3 + 1], -1.0, None, ALU.mult).then_inc(neg_ready, 1)
                else:
                    V.tensor_scalar(stat[:, b3:b3 + 1], stat[:, b3:b3 + 1], -SCALE, None, ALU.mult).then_inc(neg_ready, 1)
                if u >= 1:
                    pt_copy(u - 1)
                if u >= 2:
                    normalise(u - 2)
                filler_gated(u - 1)
            pt_copy(NU - 1)
            normalise(NU - 2)
            normalise(NU - 1)
            filler_gated(NU - 1)

            dve.wait_ge(macc_mm, 8)
            link(V.tensor_tensor(modc[:, 16:48, 0:1], ps[:, 5, 0:32].unsqueeze(2), cols[:, 32:64].unsqueeze(2), ALU.add))
            link(V.scalar_tensor_tensor(A2[:, :], modc[:, 32:40, 0], 1.0, cols[:, 72:80], ALU.add, ALU.mult))
            dve.wait_ge(yT_ready, 6)
            V.tensor_scalar(mcast, modc[:, 16:24, 0:1].broadcast_to([P, KD, P]), 0.5, None, ALU.mult).then_inc(mcast_ready, 1)
            for g in range(16, 32):
                if g == 22:
                    dve.wait_ge(mbc_mm, 1)
                    dve.wait_ge(mbc_ready, 1)
                    V.tensor_copy(mcast, modc[:, 40:48, 0:1].broadcast_to([P, KD, P])).then_inc(mcast_ready, 1)
                gated(g)

            dve.wait_ge(xr_in, 16)
            def residual(m):
                t, half = m // 2, m % 2
                dve.wait_ge(wo_mm, m + 1)
                cut = slice(half * 512, (half + 1) * 512)
                if m >= 2:
                    dve.wait_ge(wo_add, m - 1)
                link(V.tensor_tensor(gtmp[:, m % 2, :], ps[:, 2 + m % 2, :], m2bc[:, cut], ALU.mult))
                V.tensor_tensor(xr[:, t, cut], xr[:, t, cut], gtmp[:, m % 2, :], ALU.add).then_inc(wo_add, 1)

            def modulate_x2(t):
                dve.wait_ge(x2T_mm, t + 1)
                for k in range(KD // 2, KD):
                    last = V.tensor_scalar(h2T[:, k, t * P:(t + 1) * P], ps[:, (1, 7)[t % 2], (k - 4) * P:(k - 3) * P],
                                           A2[:, k:k + 1], modc[:, 3 * KD + k, 0:1], ALU.mult, ALU.add)
                last.then_inc(h2T_dve, 1)

            for t in range(XT):
                residual(2 * t)
                residual(2 * t + 1)
                dve.wait_ge(ssq2, t + 1)
                rsqrt(stat[:, 32 + t:33 + t], stat[:, 32 + t:33 + t], 1.0 / D)
                V.tensor_scalar(xn2[:, t], xr[:, t], stat[:, 32 + t:33 + t], None, ALU.mult).then_inc(xn2_done, 1)
                if t:
                    modulate_x2(t - 1)
            modulate_x2(XT - 1)

            def rank(o, x, n, work):
                g, eqm = (rt[:, work + a * 256:work + a * 256 + n * 16].rearrange("p (n e j) -> p n e j", e=4, j=4) for a in range(2))
                xj = x.unsqueeze(2).broadcast_to([P, n, 4, 4])
                xe = x.unsqueeze(3).broadcast_to([P, n, 4, 4])
                low = tab[:, LOW:LOW + 16].rearrange("p (e j) -> p e j", e=4).unsqueeze(1).broadcast_to([P, n, 4, 4])
                V.tensor_tensor(g, xj, xe, ALU.is_gt)
                link(V.tensor_tensor(eqm, xj, xe, ALU.is_equal))
                link(V.tensor_tensor(eqm, eqm, low, ALU.mult))
                link(V.tensor_tensor(g, g, eqm, ALU.add))
                link(V.tensor_reduce(o, g, AX.X, ALU.add))

            dve.wait_ge(rt_exp, 1)
            sc, bi, sel = rt[:, 0:64], rt[:, 64:128], rt[:, 128:192]
            g16 = lambda a: a.rearrange("p (n e) -> p n e", e=4)
            link(V.tensor_scalar(sc, sc, 1.0, None, ALU.add))
            link(V.reciprocal(sc, sc))
            link(V.tensor_tensor(bi.rearrange("p (t e) -> p t e", t=XT), sc.rearrange("p (t e) -> p t e", t=XT),
                                 rbias[:, :].unsqueeze(1).broadcast_to([P, XT, NE]), ALU.add))
            rank(g16(sel), g16(bi), 16, 512)
            link(V.scalar_tensor_tensor(bi, sel, 1.5, bi, ALU.is_lt, ALU.mult))
            gs, gr = rt[:, 192:208], rt[:, 208:224]
            link(V.tensor_reduce(gs, g16(bi), AX.X, ALU.add))
            rank(g16(gr), g16(gs), 4, 512)
            link(V.tensor_scalar(gr, gr, 0.5, None, ALU.is_lt))
            best = gr.unsqueeze(2).broadcast_to([P, 16, 4])
            V.scalar_tensor_tensor(g16(selb), g16(sel), 1.5, best, ALU.is_lt, ALU.mult).then_inc(gate_ready, 1)
            link(V.scalar_tensor_tensor(g16(sel), g16(sel), 1.5, best, ALU.is_lt, ALU.mult))
            link(V.tensor_tensor(sc, sc, sel, ALU.mult))
            link(V.tensor_reduce(rt[:, 224:228], sc.rearrange("p (t e) -> p t e", t=XT), AX.X, ALU.add))
            link(V.reciprocal(rt[:, 228:232], rt[:, 224:228]))
            link(V.tensor_tensor(gate[:, :, :], sc.rearrange("p (t e) -> p t e", t=XT),
                                 rt[:, 228:232].unsqueeze(2).broadcast_to([P, XT, NE]), ALU.mult))
            tE = lambda a: a.rearrange("p (t e) -> p t e", t=XT)
            over_e = lambda a: a.unsqueeze(2).broadcast_to([P, XT, NE])
            posm, sv, eqm, eqs = rt[:, 256:320], rt[:, 320:384], rt[:, 400:464], rt[:, 480:544]
            hi, nmax = rt[:, 384:388], rt[:, 464:468]
            place, base, wt, cut_, win = (rt[:, 560 + 8 * a:568 + 8 * a].rearrange("p (t c) -> p t c", c=2) for a in range(5))
            before, total = rt[:, 704:768], rt[:, 768:784]
            dve.wait_ge(pos_mm, 1)
            link(V.tensor_copy(rt[:, 704:784], ps[:, 5, 0:80]))
            link(V.scalar_tensor_tensor(posm, before, 1.0, sel, ALU.add, ALU.mult))

            def token_places():
                eoff = tab[:, EOFF:EOFF + NE].unsqueeze(1).broadcast_to([P, XT, NE])
                link(V.tensor_scalar(tE(sv), eoff, 1.0, None, ALU.add))
                link(V.tensor_tensor(sv, sv, sel, ALU.mult))
                link(V.tensor_reduce(hi, tE(sv), AX.X, ALU.max))
                link(V.tensor_tensor(tE(eqm), tE(sv), over_e(hi), ALU.is_equal))
                for to, val in ((place, tE(before)), (base, eoff), (wt, gate[:, :, :])):
                    link(V.tensor_tensor(tE(eqs), tE(eqm), val, ALU.mult))
                    link(V.tensor_reduce(to[:, :, 1], tE(eqs), AX.X, ALU.add))
                    link(V.tensor_tensor(tE(eqs), tE(sel), val, ALU.mult))
                    link(V.tensor_reduce(to[:, :, 0], tE(eqs), AX.X, ALU.add))
                    link(V.tensor_tensor(to[:, :, 0], to[:, :, 0], to[:, :, 1], ALU.subtract))
                link(V.tensor_reduce(nmax[:, 0:1], total, AX.X, ALU.max))
                for m in range(1, 4):
                    link(V.tensor_scalar(nmax[:, m:m + 1], nmax[:, 0:1], CAP * m + 0.5, None, ALU.is_gt))
                link(V.tensor_reduce(nmax[:, 0:1], nmax[:, 1:4], AX.X, ALU.add))
                V.tensor_copy(extra[:, :], nmax[:, 0:1]).then_inc(route_ready, 1)

            dve.wait_ge(xs_done, 16 * XT)
            V.sem_inc(ys_done, 2)
            V.sem_inc(ys_out[0], 16)
            V.sem_inc(ys_out[1], 16)

            tok_sum = rt[:, 600:604]
            V.tensor_copy(tokb[:, :], tab[:, TOK:TOK + 2 * XT]).then_inc(tokb_ready, 1)

            def experts(r):
                if not isinstance(r, int):
                    for par in range(2):
                        dve.wait_ge(hg_in[par], 16 * (NE // 2 * r))
                    dve.wait_ge(add_done, 2 * XT * r)
                    V.tensor_scalar(posm, posm, -float(CAP), None, ALU.add).then_inc(shift_done, 1)
                    V.tensor_scalar(place, place, -float(CAP), None, ALU.add).then_inc(shift_done, 1)
                    dve.wait_ge(shift_done, 2 * r)

                def make_picks(first, count):
                    for e in range(first, first + count):
                        if e >= PICKS or not isinstance(r, int):
                            dve.wait_ge(pick_mm, NE * r + (e + 1 - PICKS))
                        V.tensor_tensor(pick[:, e % PICKS], const("iota").unsqueeze(1).broadcast_to([P, XT, P]),
                                        tE(posm)[:, :, e:e + 1].broadcast_to([P, XT, P]), ALU.is_equal).then_inc(pick_ready, 1)

                def take_tokens(f):
                    dve.wait_ge(pick_mm, NE * r + 4 * (f + 1))
                    V.tensor_reduce(tok_sum, ps[:, 3 + 4 * (f % 2), 8 * f:8 * f + 8].rearrange("p (e c) -> p e c", c=2),
                                    AX.X, ALU.add).then_inc(tok_step, 1)
                    dve.wait_ge(tok_step, 4 * r + (f + 1))
                    V.tensor_copy(tok_of[:, 4 * f:4 * f + 4], tok_sum).then_inc(tok_ready, 1)
                    dve.wait_ge(tok_ready, 4 * r + (f + 1))

                def token_rows():
                    if isinstance(r, int):
                        token_places()
                    V.tensor_scalar(cut_, place, 0.0, CAP - 1.0, ALU.max, ALU.min).then_inc(slot_step, 1)
                    dve.wait_ge(slot_step, 4 * r + 1)
                    V.tensor_tensor(win, cut_, place, ALU.is_equal).then_inc(slot_step, 1)
                    dve.wait_ge(slot_step, 4 * r + 2)
                    V.tensor_tensor(win, win, wt, ALU.mult).then_inc(slot_step, 1)
                    V.tensor_tensor(slot_of[:, :, :], cut_, base, ALU.add).then_inc(slot_step, 1)

                def modulate(i, o):
                    dve.wait_ge(hg_mm, nth(r, i, o))
                    for k in range(KD // 2, KD):
                        last = V.tensor_scalar(hgT[:, k, :], ps[:, 1, (k - 4) * P:(k - 3) * P], A2[:, k:k + 1],
                                               modc[:, 3 * KD + k, 0:1], ALU.mult, ALU.add)
                    last.then_inc(hgT_dve, 1)

                def scale_outputs(i, o):
                    dve.wait_ge(y_mm, nth(r, i, o))
                    dve.wait_ge(ys_out[o % 2], 16 * nth(r, i, o, 2))
                    bank = 4 + 2 * (o % 2)
                    V.tensor_tensor(ys[:, o % 2], ps[:, bank:bank + 2, :].rearrange("p b n -> p (b n)"), m5bc,
                                    ALU.mult).then_inc(ys_done, 1)

                def step(i, o):
                    dve.wait_ge(silu_ready, nth(r, i, o))
                    V.tensor_tensor(a_tok, sl, ps[:, 2, 256:512], ALU.mult).then_inc(a_done, 1)
                    if not is_last(i, o):
                        modulate(i, o + 1)
                    if o >= 1:
                        scale_outputs(i, o - 1)
                    else:
                        take_tokens(3)
                        token_rows()

                make_picks(0, 5)
                take_tokens(0)
                make_picks(5, 4)
                take_tokens(1)
                make_picks(9, 3)
                modulate(0, 0)
                take_tokens(2)
                make_picks(12, 4)
                over_experts(dve, step)
                scale_outputs(NE // 4 - 1, 3)

                dve.wait_ge(slot_step, 4 * r + 4)
                if not isinstance(r, int):
                    dve.wait_ge(out_done, 16 * XT * r)
                for t in range(XT):
                    for c in range(2):
                        dve.wait_ge(yg_in[t][c], 16 * r + 16)
                        V.scalar_tensor_tensor(xr[:, t], yg[t][:, c], win[:, t, c:c + 1], xr[:, t], ALU.mult, ALU.add).then_inc(add_done, 1)
                        dve.wait_ge(add_done, 2 * XT * r + 2 * t + c + 1)

            experts(0)
            extra_rounds(dve, experts)

        @block.gpsimd
        def _(pool):
            G = nc.gpsimd
            steps = [0]

            def link(ins):
                steps[0] += 1
                ins.then_inc(pool_step, 1)
                pool.wait_ge(pool_step, steps[0])

            roots = [0]

            def root(o):
                roots[0] += 1
                pool.wait_ge(root_ask, roots[0])
                G.tensor_tensor(o, o, mhalf[:, 0:o.shape[1]], ALU.pow).then_inc(root_done, 1)

            link(G.memset(mhalf[:, :], -0.5))
            link(G.memset(qk[:, XT:NT, 0:4, :], 0.0))
            G.memset(qk[:, XT:NT, 6:10, :], 0.0).then_inc(qk_zero, 1)
            for t in range(0, NT, 2):
                root(stat[:, t:t + 2])

            def mod_partial(m):
                n = mods_late[m]
                slot, acc = n % RING, mod_acc(m)
                pool.wait_ge(cond_ready, 1)
                pool.wait_ge(ring_in[slot], ring_value(n))
                if m >= 2:
                    pool.wait_ge(macc_mm, m - 1)
                w = ring[:, slot, 0:KD, :]
                link(G.tensor_tensor(w, w, cond[:, :, 0:1].broadcast_to([P, KD, CW]), ALU.mult))
                link(G.tensor_tensor(w[:, 0:4], w[:, 0:4], w[:, 4:8], ALU.add))
                link(G.tensor_tensor(w[:, 0:2], w[:, 0:2], w[:, 2:4], ALU.add))
                G.tensor_tensor(acc, w[:, 0], w[:, 1], ALU.add).then_inc(macc_ready, 1)
                pool.wait_ge(macc_ready, m + 1)
                G.sem_inc(ring_used[slot], 1)

            for m in range(3):
                mod_partial(m)

            pool.wait_ge(table_in, 16)
            pool.wait_ge(kq_ready, NT)
            pool.wait_ge(qkinT_done, XT)
            pool.wait_ge(pj_done, last_group(4))
            for s in range(2 * NT):
                t = (fw_tiles, bw_tiles)[s % 2][s // 2]
                if s >= 2:
                    pool.wait_ge(kv_done, s - 1)
                G.tensor_tensor(Vexp[:, s % 2], gv[:, t].rearrange("p (h e) -> p h e", h=4).unsqueeze(2).broadcast_to([P, 4, NCH, HD]),
                                tab[:, IND:IND + NCH].unsqueeze(1).unsqueeze(3).broadcast_to([P, 4, NCH, HD]),
                                ALU.mult).then_inc(vexp_ready, 1)

            for t in range(XT):
                root(stat[:, 24:28])

            pool.wait_ge(small_in, 160)
            for t in range(NT):
                root(stat[:, 40:52])
                if t >= XT:
                    continue
                pool.wait_ge(qk_norm, t + 1)
                x1, x2 = qk[:, t, :, 0:32], qk[:, t, :, 32:64]
                co = rope[:, t, 0:1, :].broadcast_to([P, 12, 32])
                si = rope[:, t, 1:2, :].broadcast_to([P, 12, 32])
                G.tensor_tensor(rtmp[:, 0], x1, co, ALU.mult)
                G.tensor_tensor(rtmp[:, 1], x2, si, ALU.mult)
                G.tensor_tensor(rtmp[:, 2], x1, si, ALU.mult)
                link(G.tensor_tensor(rtmp[:, 3], x2, co, ALU.mult))
                G.tensor_tensor(x1, rtmp[:, 0], rtmp[:, 1], ALU.subtract)
                last = G.tensor_tensor(x2, rtmp[:, 2], rtmp[:, 3], ALU.add)
                last.then_inc(rope_done, 1)
                pool.wait_ge(rope_done, t + 1)

            for g in range(8, 32):
                b, half, j, n = gates[g]
                ft = half * 4 + j
                pool.wait_ge(gm_ready, g + 1)
                G.tensor_tensor(merged[:, ft, :], merged[:, ft, :], gtmp[:, g % 2, :], ALU.add).then_inc(merged_add, 1)
            for t in range(XT):
                root(stat[:, 32 + t:33 + t])
            pool.wait_ge(wo_add, 2 * XT)
            G.tensor_copy(masks[:, 0], const("before"))
            G.tensor_copy(masks[:, 1], const("ones")).then_inc(masks_ready, 1)

            pool.wait_ge(xs_done, 16 * XT)

            def experts(r):
                for e in range(NE):
                    pool.wait_ge(tok_ready, 4 * r + (e // 4 + 1))
                    if e >= 2 or not isinstance(r, int):
                        pool.wait_ge(hg_mm, NE * r + (e - 1))
                    G.sem_inc(gather_go, 1)
                    G.indirect_dma_start(hg[:, e % 2], None, xd, bass.IndirectOffsetOnAxis(ap=tok_of[:, e:e + 1], axis=0))\
                        .then_inc(hg_in[e % 2], 16)

                for par in range(2):
                    pool.wait_ge(ys_out[par], 16 * (NE // 2) * r + 16 * (NE // 2 + 1))
                pool.wait_ge(hg_mm, NE * r + NE)
                if not isinstance(r, int):
                    pool.wait_ge(add_done, 2 * XT * r)
                pool.wait_ge(slot_step, 4 * r + 4)
                G.sem_inc(gather_go, 1)
                for t in range(XT):
                    for c in range(2):
                        G.indirect_dma_start(yg[t][:, c], None, ye, bass.IndirectOffsetOnAxis(ap=slot_of[:, t, c:c + 1], axis=0))\
                            .then_inc(yg_in[t][c], 16)

            experts(0)
            extra_rounds(pool, experts)


_INS = ['x', 'c', 'ctx', 'c_ctx', 'mod_w', 'mod_b', 'norm1_g', 'norm2_g', 'w_in', 'qnorm_a', 'knorm_a', 'qnorm_c',
        'knorm_c', 'sink_c', 'hgrn_lb_logits', 'hgrn_onorm_g', 'w_branch', 'w_out', 'router_w', 'router_b',
        'moe_w1', 'moe_w3', 'moe_w2']


def shape_tables():
    s, t = np.meshgrid(np.arange(P), np.arange(P), indexing="ij")
    same = s // CH == t // CH
    parts = {
        "ident": s == t,
        "tri_fw": same & (s <= t), "tri_bw": same & (s >= t),
        "rem_fw": same & (s > t), "rem_bw": same & (s < t),
        "before": s < t, "ones": np.ones((P, P)), "iota": t + 1,
        "win_prev": np.where(t >= s, 0.0, NEG), "win_next": np.where(t <= s, 0.0, NEG),
    }
    table = np.zeros((P, TABW), np.float64)
    for i, name in enumerate(TABLE):
        table[:, i * P:(i + 1) * P] = parts[name]
    table[:, IND:IND + NCH] = np.arange(P)[:, None] // CH == np.arange(NCH)[None]
    e, j = np.meshgrid(np.arange(4), np.arange(4), indexing="ij")
    table[:, LOW:LOW + 16] = (j < e).reshape(1, 16)
    table[:, TOK:TOK + 2 * XT:2] = np.arange(P)[:, None]
    table[:, TOK + 1:TOK + 2 * XT:2] = P * np.arange(XT)
    table[:, EOFF:EOFF + NE] = P * np.arange(NE)
    a = 2 * np.pi * (np.outer(np.arange(HD), np.arange(HD)) % HD) / HD
    for g in range(2):
        r = slice(g * HD, (g + 1) * HD)
        table[r, DFT + g * HD:DFT + (g + 1) * HD] = np.cos(a)
        table[r, DFT + P + g * HD:DFT + P + (g + 1) * HD] = -np.sin(a)
    b = 2 * np.pi * (np.outer(np.arange(SEQ), np.arange(SEQ)) % SEQ) / SEQ
    norm = (SEQ * HD) ** -0.5
    dft_long = np.stack([np.cos(b), np.sin(b)]) * norm
    pos = np.arange(SEQ)
    freq = (np.float32(10000.0) ** (-np.arange(16, dtype=np.float32) / np.float32(16))).astype(np.float32)
    ang = np.concatenate([(pos // GRID_W).astype(np.float32)[:, None] * freq,
                          (pos % GRID_W).astype(np.float32)[:, None] * freq], axis=1)
    rope = np.concatenate([np.cos(ang), np.sin(ang)], axis=1)
    return {"table": table.astype(np.float32), "dft_long": dft_long.astype(np.float32), "rope": rope.astype(np.float32)}


def kernel(**inputs):
    import concourse.bacc as _bacc
    from concourse.bass_utils import run_bass_kernel_spmd as _run

    nc = _bacc.Bacc("TRN2", target_bir_lowering=False, num_devices=1)
    arrays, args = {}, {}
    for name in _INS:
        arrays[f"in_{name}"] = np.ascontiguousarray(inputs[name])
    for name, a in shape_tables().items():
        arrays[f"in_{name}"] = a
    for key, a in arrays.items():
        args[key[3:]] = nc.dram_tensor(key, a.shape, mybir.dt.from_np(a.dtype), kind="ExternalInput").ap()
    out = nc.dram_tensor("out_0", (1, SEQ, D), F32, kind="ExternalOutput").ap()
    build(nc, args, out)
    r = _run(nc, [arrays], core_ids=[0])
    return r.results[0]["out_0"]
```
